# Optimizing a Trainium2 kernel written in Bass

```python
import math
import jax
import jax.numpy as jnp
from jax import lax
import numpy as np
import jax, jax.numpy as jnp

D_MODEL = 1024
BATCH = 1
SEQ = 512
DEPTH = 2

GRID_W = 64
CTX_LEN = 256
EPS = 1e-6
POOL_GROUPS = 4
POOL_WINDOWS = (2, 4, 8, 16)
POOL_WIDTH = D_MODEL // 4
POOL_GROUP_DIM = POOL_WIDTH // POOL_GROUPS
HEAD_DIM = 128
N_Q_HEADS = (D_MODEL - POOL_WIDTH) // HEAD_DIM
N_KV_HEADS = 2
ATT_WIDTH = N_Q_HEADS * HEAD_DIM
KV_WIDTH = N_KV_HEADS * HEAD_DIM
Q_BLOCK = 128
ROPE_THETA = 10000.0
ROPE_FREQS = HEAD_DIM // 4
EVEN_SPLITS = (POOL_WIDTH, 2 * POOL_WIDTH, 2 * POOL_WIDTH + ATT_WIDTH,
               2 * POOL_WIDTH + ATT_WIDTH + KV_WIDTH, 2 * POOL_WIDTH + ATT_WIDTH + 2 * KV_WIDTH)
EVEN_IN = 2 * POOL_WIDTH + 2 * ATT_WIDTH + 2 * KV_WIDTH
EVEN_MIX = POOL_WIDTH + ATT_WIDTH
HY_ORDER = 2
HY_WIDTH = 3 * D_MODEL // 4
HY_EMB = 33
HY_BANDS = (HY_EMB - 1) // 2
HY_HIDDEN = 64
HY_DECAY_TARGET = 1e-2
HY_FAST_DECAY = 0.3
HY_SLOW_DECAY = 1.5
FN_WIDTH = D_MODEL - HY_WIDTH
ODD_SPLITS = ((HY_ORDER + 1) * HY_WIDTH, (HY_ORDER + 2) * HY_WIDTH,
              (HY_ORDER + 2) * HY_WIDTH + FN_WIDTH)
ODD_IN = (HY_ORDER + 2) * HY_WIDTH + 2 * FN_WIDTH
ODD_MIX = HY_WIDTH + FN_WIDTH
N_EVEN = (DEPTH + 1) // 2
N_ODD = DEPTH // 2


def rmsnorm(x, g):
    xf = x.astype(jnp.float32)
    y = xf * lax.rsqrt(jnp.mean(xf * xf, axis=-1, keepdims=True) + EPS)
    return y.astype(x.dtype) * g

def modulation(cond, w_mod, b_mod):
    m = jax.nn.silu(cond) @ w_mod + b_mod
    return jnp.split(m, 3, axis=-1)

def to_heads(t, n_heads):
    return t.reshape(t.shape[:2] + (n_heads, HEAD_DIM))

def axial_rope_tables(row_idx, col_idx):
    inv_freq = ROPE_THETA ** (-jnp.arange(ROPE_FREQS, dtype=jnp.float32) / ROPE_FREQS)
    ang = jnp.stack([row_idx[:, None] * inv_freq, col_idx[:, None] * inv_freq], axis=1)
    ang = ang[:, None, :, None, :]
    return jnp.cos(ang), jnp.sin(ang)

def apply_rope(x, cos, sin):
    xr = x.reshape(x.shape[:-1] + (2, 2, ROPE_FREQS)).astype(jnp.float32)
    rot = jnp.concatenate([-xr[..., 1:, :], xr[..., :1, :]], axis=-2)
    return (xr * cos + rot * sin).astype(x.dtype).reshape(x.shape)

def blocked_attention(q, k, v):
    b, lq, hq, dh = q.shape
    hkv = k.shape[2]
    grp = hq // hkv
    nb = lq // Q_BLOCK
    qb = q.reshape(b, nb, Q_BLOCK, hkv, grp, dh).transpose(1, 0, 2, 3, 4, 5)
    scale = dh ** -0.5

    def one_block(qblk):
        s = jnp.einsum('bqhgd,bkhd->bhgqk', qblk, k, preferred_element_type=jnp.float32) * scale
        p = jax.nn.softmax(s, axis=-1).astype(v.dtype)
        return jnp.einsum('bhgqk,bkhd->bqhgd', p, v)

    o = lax.map(one_block, qb)
    return o.transpose(1, 0, 2, 3, 4, 5).reshape(b, lq, hq * dh)

def pool_mixer(u, w_grp, scale):
    b, L, _ = u.shape
    ug = u.reshape(b, L, POOL_GROUPS, POOL_GROUP_DIM).astype(jnp.float32)
    cs = jnp.concatenate([jnp.zeros((b, 1, POOL_GROUPS, POOL_GROUP_DIM), jnp.float32),
                          jnp.cumsum(ug, axis=1)], axis=1)
    t = jnp.arange(L)
    outs = []
    for gi, w in enumerate(POOL_WINDOWS):
        lo = jnp.clip(t - w // 2, 0, L)
        hi = jnp.clip(t + w // 2, 0, L)
        csg = cs[:, :, gi]
        win_sum = jnp.take(csg, hi, axis=1) - jnp.take(csg, lo, axis=1)
        cnt = (hi - lo).astype(jnp.float32)[None, :, None]
        outs.append(win_sum / cnt - ug[:, :, gi])
    d = jnp.stack(outs, axis=2).astype(u.dtype)
    y = jnp.einsum('blgc,gcd->blgd', d, w_grp)
    return y.reshape(b, L, POOL_WIDTH) * scale

def even_mix(a_val, a_gate, q, b_gate, k_all, v_all, pool_w, pool_scale, w_out):
    ya = pool_mixer(a_val, pool_w, pool_scale)
    yb = blocked_attention(q, k_all, v_all)
    y = jnp.concatenate([ya * jax.nn.silu(a_gate), yb * jax.nn.silu(b_gate)], axis=-1)
    return y @ w_out

def short_conv3(u, w, b):
    up = jnp.pad(u, ((0, 0), (1, 1), (0, 0)))
    return up[:, :-2] * w[0] + up[:, 1:-1] * w[1] + up[:, 2:] * w[2] + b

def hyena_filters(L, w1, b1, w2, b2, w3, freq):
    f32 = jnp.float32
    t = jnp.linspace(0.0, 1.0, L, dtype=f32)[:, None]
    w = 2.0 * math.pi * jnp.arange(L, dtype=f32)[:, None] / L
    f = jnp.linspace(1e-4, HY_BANDS - 1, HY_BANDS, dtype=f32)[None, :]
    emb = jnp.concatenate([t, jnp.cos(f * w), -jnp.sin(f * w)], axis=-1)
    fr = freq.astype(f32)
    hdn = jnp.sin(fr * (emb @ w1.astype(f32) + b1.astype(f32)))
    hdn = jnp.sin(fr * (hdn @ w2.astype(f32) + b2.astype(f32)))
    h = (hdn @ w3.astype(f32)).reshape(L, HY_ORDER, 2, HY_WIDTH)
    max_decay = math.log(HY_DECAY_TARGET) / HY_FAST_DECAY
    min_decay = math.log(HY_DECAY_TARGET) / HY_SLOW_DECAY
    deltas = jnp.linspace(min_decay, max_decay, HY_WIDTH, dtype=f32)
    decay = jnp.exp(-t * jnp.abs(deltas))
    h = h * decay[:, None, None, :]
    h = h / (jnp.sum(jnp.abs(h), axis=(0, 2), keepdims=True) + EPS)
    zero = jnp.zeros((1, HY_ORDER, HY_WIDTH), f32)
    return jnp.concatenate([h[:, :, 0], zero, h[:0:-1, :, 1]], axis=0)

def fft_long_conv(z, kfull):
    L = z.shape[1]
    zf = jnp.fft.rfft(z, n=2 * L, axis=1)
    kf = jnp.fft.rfft(kfull, n=2 * L, axis=0)
    return jnp.fft.irfft(zf * kf[None], n=2 * L, axis=1)[:, :L]

def hyena_mixer(u, conv_w, conv_b, w1, b1, w2, b2, w3, freq, skip):
    L = u.shape[1]
    uc = short_conv3(u, conv_w, conv_b)
    v, x1, x2 = jnp.split(uc, HY_ORDER + 1, axis=-1)
    k = hyena_filters(L, w1, b1, w2, b2, w3, freq)
    z = v.astype(jnp.float32)
    for o, gate_o in enumerate((x1, x2)):
        z = gate_o.astype(jnp.float32) * (fft_long_conv(z, k[:, o]) + skip[o].astype(jnp.float32) * z)
    return z.astype(u.dtype)

def fourier_mixer(u, w):
    y = jnp.fft.fft2(u.astype(jnp.float32), axes=(1, 2), norm='ortho').real
    return y.astype(u.dtype) @ w

def odd_mix(h, w_in, w_out, fn_w, conv_w, conv_b, w1, b1, w2, b2, w3, freq, skip):
    hy_in, hy_gate, fn_in, fn_gate = jnp.split(h @ w_in, ODD_SPLITS, axis=-1)
    yc = hyena_mixer(hy_in, conv_w, conv_b, w1, b1, w2, b2, w3, freq, skip)
    yd = fourier_mixer(fn_in, fn_w)
    y = jnp.concatenate([yc * jax.nn.silu(hy_gate), yd * jax.nn.silu(fn_gate)], axis=-1)
    return y @ w_out

def first_inputs(seed: int = 0) -> dict:
    key = jax.random.key(seed)
    ks = jax.random.split(key, 26)

    def nrm(k, shape, s):
        return jax.random.normal(k, shape, jnp.float32) * s

    return {
        'x': nrm(ks[0], (BATCH, SEQ, D_MODEL), 1.0),
        'c': nrm(ks[1], (BATCH, D_MODEL), 1.0),
        'ctx': nrm(ks[2], (BATCH, CTX_LEN, D_MODEL), 1.0),
        'c_ctx': nrm(ks[3], (D_MODEL,), 1.0),
        'w_mod': nrm(ks[4], (DEPTH, D_MODEL, 3 * D_MODEL), 0.5 * D_MODEL ** -0.5),
        'b_mod': nrm(ks[5], (DEPTH, 3 * D_MODEL), 0.01),
        'norm_g': 1.0 + nrm(ks[6], (DEPTH, D_MODEL), 0.05),
        'ev_w_in': nrm(ks[7], (N_EVEN, D_MODEL, EVEN_IN), D_MODEL ** -0.5),
        'ev_w_out': nrm(ks[8], (N_EVEN, EVEN_MIX, D_MODEL), EVEN_MIX ** -0.5),
        'pool_w': nrm(ks[9], (N_EVEN, POOL_GROUPS, POOL_GROUP_DIM, POOL_GROUP_DIM), POOL_GROUP_DIM ** -0.5),
        'pool_scale': 1.0 + nrm(ks[10], (N_EVEN, POOL_WIDTH), 0.1),
        'q_norm_g': 1.0 + nrm(ks[11], (N_EVEN, HEAD_DIM), 0.05),
        'k_norm_g': 1.0 + nrm(ks[12], (N_EVEN, HEAD_DIM), 0.05),
        'od_w_in': nrm(ks[13], (N_ODD, D_MODEL, ODD_IN), D_MODEL ** -0.5),
        'od_w_out': nrm(ks[14], (N_ODD, ODD_MIX, D_MODEL), ODD_MIX ** -0.5),
        'hy_conv_w': nrm(ks[15], (N_ODD, 3, (HY_ORDER + 1) * HY_WIDTH), 3 ** -0.5),
        'hy_conv_b': nrm(ks[16], (N_ODD, (HY_ORDER + 1) * HY_WIDTH), 0.01),
        'hy_w1': nrm(ks[17], (N_ODD, HY_EMB, HY_HIDDEN), HY_EMB ** -0.5),
        'hy_b1': nrm(ks[18], (N_ODD, HY_HIDDEN), 0.1),
        'hy_w2': nrm(ks[19], (N_ODD, HY_HIDDEN, HY_HIDDEN), HY_HIDDEN ** -0.5),
        'hy_b2': nrm(ks[20], (N_ODD, HY_HIDDEN), 0.1),
        'hy_w3': nrm(ks[21], (N_ODD, HY_HIDDEN, HY_ORDER * 2 * HY_WIDTH), HY_HIDDEN ** -0.5),
        'hy_freq': 1.0 + nrm(ks[22], (N_ODD, HY_HIDDEN), 0.1),
        'hy_skip': nrm(ks[23], (N_ODD, HY_ORDER, HY_WIDTH), 1.0),
        'fn_w': nrm(ks[24], (N_ODD, FN_WIDTH, FN_WIDTH), FN_WIDTH ** -0.5),
        'final_g': 1.0 + nrm(ks[25], (D_MODEL,), 0.05),
    }

def first_block(x, c, ctx, c_ctx, w_mod, b_mod, norm_g, ev_w_in, ev_w_out, pool_w, pool_scale,
              q_norm_g, k_norm_g, od_w_in, od_w_out, hy_conv_w, hy_conv_b, hy_w1, hy_b1, hy_w2, hy_b2,
              hy_w3, hy_freq, hy_skip, fn_w, final_g):
    n_tok = x.shape[1]
    rows = n_tok // GRID_W
    row_idx = jnp.broadcast_to(jnp.arange(rows, dtype=jnp.float32)[:, None], (rows, GRID_W)).reshape(-1)
    col_idx = jnp.broadcast_to(jnp.arange(GRID_W, dtype=jnp.float32)[None, :], (rows, GRID_W)).reshape(-1)
    cos, sin = axial_rope_tables(row_idx, col_idx)

    for i in range(DEPTH):
        li = i // 2
        is_even = i % 2 == 0
        ctx_needed = any(j % 2 == 0 for j in range(i + 1, DEPTH))
        shift, scale, gate = modulation(c[:, None, :], w_mod[i], b_mod[i])
        h = rmsnorm(x, norm_g[i]) * (1 + scale) + shift
        if is_even or ctx_needed:
            cshift, cscale, cgate = modulation(c_ctx[None, None, :], w_mod[i], b_mod[i])
            hc = rmsnorm(ctx, norm_g[i]) * (1 + cscale) + cshift
        if is_even:
            w_in = ev_w_in[li]
            a_val, a_gate, q, k, v, b_gate = jnp.split(h @ w_in, EVEN_SPLITS, axis=-1)
            q = apply_rope(rmsnorm(to_heads(q, N_Q_HEADS), q_norm_g[li]), cos, sin)
            k = apply_rope(rmsnorm(to_heads(k, N_KV_HEADS), k_norm_g[li]), cos, sin)
            if ctx_needed:
                ca_val, ca_gate, cq, ck, cv, cb_gate = jnp.split(hc @ w_in, EVEN_SPLITS, axis=-1)
            else:
                ck, cv = jnp.split(hc @ w_in[:, EVEN_SPLITS[2]:EVEN_SPLITS[4]], 2, axis=-1)
            ck = rmsnorm(to_heads(ck, N_KV_HEADS), k_norm_g[li])
            cv = to_heads(cv, N_KV_HEADS)
            k_all = jnp.concatenate([ck, k], axis=1)
            v_all = jnp.concatenate([cv, to_heads(v, N_KV_HEADS)], axis=1)
            y = even_mix(a_val, a_gate, q, b_gate, k_all, v_all, pool_w[li], pool_scale[li], ev_w_out[li])
            if ctx_needed:
                cq = rmsnorm(to_heads(cq, N_Q_HEADS), q_norm_g[li])
                yc = even_mix(ca_val, ca_gate, cq, cb_gate, ck, cv, pool_w[li], pool_scale[li], ev_w_out[li])
                ctx = ctx + cgate * yc
            x = x + gate * y
        else:
            y = odd_mix(h, od_w_in[li], od_w_out[li], fn_w[li], hy_conv_w[li], hy_conv_b[li],
                        hy_w1[li], hy_b1[li], hy_w2[li], hy_b2[li], hy_w3[li], hy_freq[li], hy_skip[li])
            if ctx_needed:
                yc = odd_mix(hc, od_w_in[li], od_w_out[li], fn_w[li], hy_conv_w[li], hy_conv_b[li],
                             hy_w1[li], hy_b1[li], hy_w2[li], hy_b2[li], hy_w3[li], hy_freq[li], hy_skip[li])
                ctx = ctx + cgate * yc
            x = x + gate * y
    return rmsnorm(x, final_g)


N_MIXERS = 4
GROUP_WIDTH = D_MODEL // N_MIXERS
HEAD_DIM_2 = 64
N_GROUP_HEADS = GROUP_WIDTH // HEAD_DIM_2
D_FF = 4 * D_MODEL
N_MOD = 6
RMS_EPS = 1e-6
NEG_INF = -1e30

ROPE_THETA_2 = 500000.0
ROPE_DIM = HEAD_DIM_2 // 4

CONV_WIDTH = 3

CMP_BLOCK = 32
CMP_STRIDE = 16
CMP_HIDDEN = 2 * HEAD_DIM_2
SLC_BLOCK = 64
N_SLC = 16
N_INIT_BLOCKS = 1
N_LOCAL_BLOCKS = 2
FORCE_BONUS = 1e4
WINDOW = 512
N_BRANCH = 3

GLA_DK = HEAD_DIM_2 // 2
GLA_DV = HEAD_DIM_2
GLA_RANK = 16
GLA_TAU = 16.0
GLA_CHUNK = 64

GMLP_CHUNK = 128
GMLP_DIM = GROUP_WIDTH // N_GROUP_HEADS

SPLIT_SIZES = (
    GROUP_WIDTH, GROUP_WIDTH, GROUP_WIDTH,
    GROUP_WIDTH, 2 * N_BRANCH * HEAD_DIM_2, N_BRANCH * N_GROUP_HEADS,
    N_GROUP_HEADS * GLA_DK, N_GROUP_HEADS * GLA_DK,
    N_GROUP_HEADS * GLA_DV, N_GROUP_HEADS * GLA_DV, GLA_RANK,
    GROUP_WIDTH, GROUP_WIDTH,
)
D_IN_PROJ = sum(SPLIT_SIZES)


def rms_norm(x, gain=None):
    xf = x.astype(jnp.float32)
    y = xf * lax.rsqrt(jnp.mean(xf * xf, axis=-1, keepdims=True) + RMS_EPS)
    if gain is not None:
        y = y * gain.astype(jnp.float32)
    return y.astype(x.dtype)

def layer_norm(x):
    xf = x.astype(jnp.float32)
    mu = jnp.mean(xf, axis=-1, keepdims=True)
    var = jnp.mean(jnp.square(xf - mu), axis=-1, keepdims=True)
    return ((xf - mu) * lax.rsqrt(var + RMS_EPS)).astype(x.dtype)

def split_cols(z, sizes):
    out, start = [], 0
    for s in sizes:
        out.append(z[..., start:start + s])
        start += s
    return out

def partial_rotary(x, positions):
    half = ROPE_DIM // 2
    inv_freq = ROPE_THETA_2 ** (-jnp.arange(0, ROPE_DIM, 2, dtype=jnp.float32) / ROPE_DIM)
    ang = positions.astype(jnp.float32)[..., None] * inv_freq
    cos = jnp.cos(ang)[:, :, None, :]
    sin = jnp.sin(ang)[:, :, None, :]
    xr = x[..., :ROPE_DIM].astype(jnp.float32)
    x1, x2 = xr[..., :half], xr[..., half:]
    rot = jnp.concatenate([x1 * cos - x2 * sin, x2 * cos + x1 * sin], axis=-1).astype(x.dtype)
    return jnp.concatenate([rot, x[..., ROPE_DIM:]], axis=-1)

def masked_softmax(s, mask):
    p = jax.nn.softmax(jnp.where(mask, s, NEG_INF), axis=-1)
    return jnp.where(mask, p, 0.0)

def short_conv_mixer(h_in, b_gate, c_gate, conv_w):
    z = c_gate * h_in
    y = lax.conv_general_dilated(z, conv_w.astype(z.dtype)[:, None, :], (1,), ((CONV_WIDTH - 1, 0),),
                                 dimension_numbers=('NWC', 'WIO', 'NWC'),
                                 feature_group_count=GROUP_WIDTH)
    return b_gate * y

def cmp_to_slc_matrix(n_cmp, n_blk):
    cs = np.arange(n_cmp) * CMP_STRIDE
    ss = np.arange(n_blk) * SLC_BLOCK
    ov = np.minimum(cs[:, None] + CMP_BLOCK, ss[None, :] + SLC_BLOCK) - np.maximum(cs[:, None], ss[None, :])
    return jnp.asarray(np.clip(ov, 0, None) / CMP_STRIDE, dtype=jnp.float32)

def nsa_mixer(q_in, kv_in, gate_in, positions, cmp_pos, cmp_w1, cmp_w2):
    B, S, _ = q_in.shape
    H, HD = N_GROUP_HEADS, HEAD_DIM_2
    scale = HD ** -0.5
    q = q_in.reshape(B, S, H, HD)
    k_cmp, v_cmp, k_slc, v_slc, k_win, v_win = jnp.split(kv_in, 2 * N_BRANCH, axis=-1)

    n_cmp = (S - CMP_BLOCK) // CMP_STRIDE + 1
    blk = np.arange(n_cmp)[:, None] * CMP_STRIDE + np.arange(CMP_BLOCK)[None, :]

    def compress(t, j):
        z = (t[:, blk] + cmp_pos[j]).reshape(B, n_cmp, CMP_BLOCK * HD)
        return jax.nn.silu(z @ cmp_w1[j]) @ cmp_w2[j]

    kc, vc = compress(k_cmp, 0), compress(v_cmp, 1)
    t_idx = jnp.arange(S)
    cmp_end = jnp.arange(n_cmp) * CMP_STRIDE + CMP_BLOCK - 1
    mask_c = cmp_end[None, :] <= t_idx[:, None]
    s_c = jnp.einsum('bshd,bnd->bhsn', q, kc).astype(jnp.float32) * scale
    p_c = masked_softmax(s_c, mask_c)
    o_cmp = jnp.einsum('bhsn,bnd->bshd', p_c.astype(vc.dtype), vc)

    n_blk = S // SLC_BLOCK
    p_slc = jnp.einsum('bhsn,nj->bsj', p_c, cmp_to_slc_matrix(n_cmp, n_blk))
    cur = (t_idx // SLC_BLOCK)[:, None]
    j = jnp.arange(n_blk)[None, :]
    forced = (j < N_INIT_BLOCKS) | ((cur - j >= 0) & (cur - j < N_LOCAL_BLOCKS))
    score = jnp.where(j <= cur, p_slc + jnp.where(forced, FORCE_BONUS, 0.0), NEG_INF)
    n_top = min(N_SLC, n_blk)
    _, sel_idx = lax.top_k(score, n_top)

    q_r = partial_rotary(q, positions)
    rope_k = lambda t: partial_rotary(t[:, :, None, :], positions)[:, :, 0, :]
    k_s_blk = rope_k(k_slc).reshape(B, n_blk, SLC_BLOCK, HD)
    v_s_blk = v_slc.reshape(B, n_blk, SLC_BLOCK, HD)
    pad = ((0, 0), (WINDOW, 0), (0, 0))
    k_w_pad = jnp.pad(rope_k(k_win), pad)
    v_w_pad = jnp.pad(v_win, pad)

    n_qb = S // Q_BLOCK
    q_blocks = q_r.reshape(B, n_qb, Q_BLOCK, H, HD).transpose(1, 0, 3, 2, 4)
    idx_blocks = sel_idx.reshape(B, n_qb, Q_BLOCK, n_top).transpose(1, 0, 2, 3)
    take = jax.vmap(lambda blocks, idx: blocks[idx])

    def block_fn(args):
        qb, q_b, idx_b = args
        tq = qb * Q_BLOCK + jnp.arange(Q_BLOCK)
        k_sel = take(k_s_blk, idx_b).reshape(B, Q_BLOCK, n_top * SLC_BLOCK, HD)
        v_sel = take(v_s_blk, idx_b).reshape(B, Q_BLOCK, n_top * SLC_BLOCK, HD)
        kpos = (idx_b[..., None] * SLC_BLOCK + jnp.arange(SLC_BLOCK)).reshape(B, Q_BLOCK, n_top * SLC_BLOCK)
        s_s = jnp.einsum('bhqd,bqkd->bhqk', q_b, k_sel).astype(jnp.float32) * scale
        p_s = masked_softmax(s_s, (kpos <= tq[None, :, None])[:, None])
        o_s = jnp.einsum('bhqk,bqkd->bhqd', p_s.astype(v_sel.dtype), v_sel)
        start = qb * Q_BLOCK
        k_wb = lax.dynamic_slice_in_dim(k_w_pad, start, Q_BLOCK + WINDOW, axis=1)
        v_wb = lax.dynamic_slice_in_dim(v_w_pad, start, Q_BLOCK + WINDOW, axis=1)
        kpos_w = start - WINDOW + jnp.arange(Q_BLOCK + WINDOW)
        diff = tq[:, None] - kpos_w[None, :]
        m_w = (diff >= 0) & (diff < WINDOW) & (kpos_w[None, :] >= 0)
        s_w = jnp.einsum('bhqd,bkd->bhqk', q_b, k_wb).astype(jnp.float32) * scale
        p_w = masked_softmax(s_w, m_w)
        o_w = jnp.einsum('bhqk,bkd->bhqd', p_w.astype(v_wb.dtype), v_wb)
        return o_s, o_w

    o_sel, o_win = lax.map(block_fn, (jnp.arange(n_qb), q_blocks, idx_blocks))
    to_bshd = lambda o: o.transpose(1, 0, 3, 2, 4).reshape(B, S, H, HD)
    g = jax.nn.sigmoid(gate_in.astype(jnp.float32)).astype(q.dtype).reshape(B, S, H, N_BRANCH)
    o = g[..., 0:1] * o_cmp + g[..., 1:2] * to_bshd(o_sel) + g[..., 2:3] * to_bshd(o_win)
    return o.reshape(B, S, GROUP_WIDTH)

def gla_mixer(q_in, k_in, v_in, g_in, lr_in, gate_w2, gate_b):
    B, S, _ = q_in.shape
    H, C = N_GROUP_HEADS, GLA_CHUNK
    n_c = S // C
    log_a = jax.nn.log_sigmoid((lr_in @ gate_w2 + gate_b).astype(jnp.float32)) / GLA_TAU

    def chunk(t, d):
        return t.reshape(B, n_c, C, H, d).transpose(0, 3, 1, 2, 4).astype(jnp.float32)

    q = chunk(q_in, GLA_DK) * GLA_DK ** -0.5
    k = chunk(k_in, GLA_DK)
    v = chunk(v_in, GLA_DV)
    b = jnp.cumsum(chunk(log_a, GLA_DK), axis=3)
    b_last = b[:, :, :, -1:, :]
    b_mid = b[:, :, :, C // 2:C // 2 + 1, :]
    causal = jnp.tril(jnp.ones((C, C), dtype=bool))
    att = jnp.einsum('bhntd,bhnsd->bhnts', q * jnp.exp(b - b_mid), k * jnp.exp(b_mid - b))
    o_intra = jnp.einsum('bhnts,bhnsv->bhntv', jnp.where(causal, att, 0.0), v)
    kv = jnp.einsum('bhnsd,bhnsv->bhndv', k * jnp.exp(b_last - b), v)
    decay = jnp.exp(b_last[:, :, :, 0, :])

    def step(state, inp):
        dec, kv_n = inp
        return dec[..., None] * state + kv_n, state

    init = jnp.zeros((B, H, GLA_DK, GLA_DV), jnp.float32)
    _, s_prev = lax.scan(step, init, (jnp.moveaxis(decay, 2, 0), jnp.moveaxis(kv, 2, 0)))
    o_inter = jnp.einsum('bhntd,nbhdv->bhntv', q * jnp.exp(b), s_prev)
    o = (o_intra + o_inter).transpose(0, 2, 3, 1, 4).reshape(B, S, H, GLA_DV)
    g = jax.nn.silu(g_in.astype(jnp.float32)).reshape(B, S, H, GLA_DV)
    return (g * rms_norm(o)).reshape(B, S, GROUP_WIDTH).astype(q_in.dtype)

def gmlp_mixer(u_in, v_in, w_s, b_s):
    B, S, _ = u_in.shape
    G, T = N_GROUP_HEADS, GMLP_CHUNK
    n_ch = S // T
    v = layer_norm(v_in.reshape(B, S, G, GMLP_DIM)).reshape(B, n_ch, T, G, GMLP_DIM)
    w = jnp.where(jnp.tril(jnp.ones((T, T), dtype=bool)), w_s, 0.0)
    mixed = jnp.einsum('gts,bnsgc->bntgc', w, v) + b_s.T[:, :, None]
    return (u_in.reshape(B, n_ch, T, G, GMLP_DIM) * mixed).reshape(B, S, GROUP_WIDTH)

def mixer_block(h, positions, w_in, conv_w, cmp_pos, cmp_w1, cmp_w2, gla_gate_w2, gla_gate_b,
                gmlp_ws, gmlp_b, grp_gain, w_o):
    B, S, _ = h.shape
    (a_h, a_b, a_c, n_q, n_kv, n_g, l_q, l_k, l_v, l_g, l_lr, m_u, m_v) = split_cols(h @ w_in, SPLIT_SIZES)
    outs = jnp.stack([
        short_conv_mixer(a_h, a_b, a_c, conv_w),
        nsa_mixer(n_q, n_kv, n_g, positions, cmp_pos, cmp_w1, cmp_w2),
        gla_mixer(l_q, l_k, l_v, l_g, l_lr, gla_gate_w2, gla_gate_b),
        gmlp_mixer(m_u, m_v, gmlp_ws, gmlp_b),
    ], axis=2)
    outs = rms_norm(outs, grp_gain.reshape(N_MIXERS, GROUP_WIDTH))
    return outs.reshape(B, S, D_MODEL) @ w_o

def second_inputs(seed: int = 0) -> dict:
    key = jax.random.key(seed)
    ks = jax.random.split(key, 20)
    nrm = lambda k, shape, s: jax.random.normal(k, shape, jnp.float32) * s
    positions = (jax.random.randint(ks[2], (BATCH, 1), 0, SEQ, dtype=jnp.int32)
                 + jnp.arange(SEQ, dtype=jnp.int32)[None, :])
    return {
        'x': nrm(ks[0], (BATCH, SEQ, D_MODEL), 1.0),
        'c': nrm(ks[1], (BATCH, D_MODEL), 1.0),
        'positions': positions,
        'w_in': nrm(ks[3], (DEPTH, D_MODEL, D_IN_PROJ), D_MODEL ** -0.5),
        'conv_w': nrm(ks[4], (DEPTH, CONV_WIDTH, GROUP_WIDTH), CONV_WIDTH ** -0.5),
        'cmp_pos': nrm(ks[5], (DEPTH, 2, CMP_BLOCK, HEAD_DIM_2), 0.1),
        'cmp_w1': nrm(ks[6], (DEPTH, 2, CMP_BLOCK * HEAD_DIM_2, CMP_HIDDEN), (CMP_BLOCK * HEAD_DIM_2) ** -0.5),
        'cmp_w2': nrm(ks[7], (DEPTH, 2, CMP_HIDDEN, HEAD_DIM_2), CMP_HIDDEN ** -0.5),
        'gla_gate_w2': nrm(ks[8], (DEPTH, GLA_RANK, N_GROUP_HEADS * GLA_DK), GLA_RANK ** -0.5),
        'gla_gate_b': nrm(ks[9], (DEPTH, N_GROUP_HEADS * GLA_DK), 0.1),
        'gmlp_ws': nrm(ks[10], (DEPTH, N_GROUP_HEADS, GMLP_CHUNK, GMLP_CHUNK), 0.5 * GMLP_CHUNK ** -0.5),
        'gmlp_b': 1.0 + nrm(ks[11], (DEPTH, N_GROUP_HEADS, GMLP_CHUNK), 0.1),
        'grp_gain': 1.0 + nrm(ks[12], (DEPTH, D_MODEL), 0.1),
        'w_o': nrm(ks[13], (DEPTH, D_MODEL, D_MODEL), D_MODEL ** -0.5),
        'norm_g': 1.0 + nrm(ks[14], (DEPTH, 4, D_MODEL), 0.1),
        'w_mod': nrm(ks[15], (DEPTH, D_MODEL, N_MOD * D_MODEL), D_MODEL ** -0.5),
        'b_mod': nrm(ks[16], (DEPTH, N_MOD * D_MODEL), 0.02),
        'w_up': nrm(ks[17], (DEPTH, D_MODEL, D_FF), D_MODEL ** -0.5),
        'w_down': nrm(ks[18], (DEPTH, D_FF, D_MODEL), D_FF ** -0.5),
    }

def second_block(x, c, positions, w_in, conv_w, cmp_pos, cmp_w1, cmp_w2, gla_gate_w2, gla_gate_b,
              gmlp_ws, gmlp_b, grp_gain, w_o, norm_g, w_mod, b_mod, w_up, w_down):
    cond = jax.nn.silu(c)
    for l in range(DEPTH):
        mod = cond @ w_mod[l] + b_mod[l]
        sh1, sc1, gt1, sh2, sc2, gt2 = [m[:, None, :] for m in jnp.split(mod, N_MOD, axis=-1)]
        h = rms_norm(x, norm_g[l, 0]) * (1.0 + sc1) + sh1
        y = mixer_block(h, positions, w_in[l], conv_w[l], cmp_pos[l], cmp_w1[l], cmp_w2[l],
                        gla_gate_w2[l], gla_gate_b[l], gmlp_ws[l], gmlp_b[l], grp_gain[l], w_o[l])
        x = x + gt1 * rms_norm(y, norm_g[l, 1])
        h = rms_norm(x, norm_g[l, 2]) * (1.0 + sc2) + sh2
        y = jnp.square(jax.nn.relu(h @ w_up[l])) @ w_down[l]
        x = x + gt2 * rms_norm(y, norm_g[l, 3])
    return x


def setup_inputs(seed=0):
    out = dict(first_inputs(seed))
    for name, value in second_inputs(seed + 1).items():
        if name != "x":
            out[name + "_2"] = value
    return out


def reference(
    x, c, ctx, c_ctx, w_mod, b_mod, norm_g, ev_w_in, ev_w_out, pool_w, pool_scale, q_norm_g,
    k_norm_g, od_w_in, od_w_out, hy_conv_w, hy_conv_b, hy_w1, hy_b1, hy_w2, hy_b2, hy_w3,
    hy_freq, hy_skip, fn_w, final_g, c_2, positions_2, w_in_2, conv_w_2, cmp_pos_2, cmp_w1_2,
    cmp_w2_2, gla_gate_w2_2, gla_gate_b_2, gmlp_ws_2, gmlp_b_2, grp_gain_2, w_o_2, norm_g_2,
    w_mod_2, b_mod_2, w_up_2, w_down_2,
):
    x = first_block(
        x, c, ctx, c_ctx, w_mod, b_mod, norm_g, ev_w_in, ev_w_out, pool_w, pool_scale, q_norm_g,
        k_norm_g, od_w_in, od_w_out, hy_conv_w, hy_conv_b, hy_w1, hy_b1, hy_w2, hy_b2, hy_w3,
        hy_freq, hy_skip, fn_w, final_g,
    )
    return second_block(
        x, c_2, positions_2, w_in_2, conv_w_2, cmp_pos_2, cmp_w1_2, cmp_w2_2, gla_gate_w2_2,
        gla_gate_b_2, gmlp_ws_2, gmlp_b_2, grp_gain_2, w_o_2, norm_g_2, w_mod_2, b_mod_2,
        w_up_2, w_down_2,
    )


_drawn_inputs = setup_inputs


def setup_inputs(seed=0):
    import zlib

    import numpy as np

    out = dict(_drawn_inputs(seed))
    spreads = {}
    factors = {'ctx': 6.954,
     'c_ctx': 2.865,
     'b_mod': 5.042,
     'pool_scale': 4.931,
     'q_norm_g': 8.0,
     'k_norm_g': 8.0,
     'hy_conv_b': 8.0,
     'hy_b1': 5.569,
     'hy_b2': 4.385,
     'hy_freq': 8.0,
     'cmp_pos_2': 3.012}
    for name, (base, spread) in spreads.items():
        noise = np.random.default_rng([zlib.crc32(name.encode()), seed]).standard_normal(out[name].shape)
        drawn = base * np.exp(spread * noise) if base else spread * noise
        out[name] = jnp.asarray(drawn.astype(out[name].dtype))
    for name, factor in factors.items():
        out[name] = (out[name] * factor).astype(out[name].dtype)
    return out
```

```python
import contextlib
from contextlib import ExitStack

import numpy as np
import concourse.bass as bass
from concourse import mybir

P = 128
D = 1024
KT = D // P
S = 512
NT = S // P
CTX = 256
LAYERS = 2
EPS = 1e-6

ROUND = 12582912.0
TURN = (6.28125, 0.0019350051879882812, 3.019914e-07)
PI_IN = 3.1415925

EV_IN, EV_OUT, OD_IN, OD_OUT = 20, 8, 28, 8
T_EV_IN = 0
T_EV_OUT = T_EV_IN + EV_IN
T_OD_IN = T_EV_OUT + EV_OUT
T_OD_OUT = T_OD_IN + OD_IN
T_LAYERS = T_OD_OUT + OD_OUT
MX_IN, MX_BLOB, MX_OUT, HALF_UP, HALF_DOWN = 22, 2, 8, 16, 16
L_IN = 0
L_BLOB = L_IN + MX_IN
L_OUT = L_BLOB + MX_BLOB
L_FF = L_OUT + MX_OUT
PER_LAYER = L_FF + 2 * (HALF_UP + HALF_DOWN)
PRIME = 4
SEGS = 16
UNITS = 8

COLS = {}
N_COLS = 0
for _name, _n in (("c", 8), ("c_ctx", 8), ("cond", 8 * SEGS), ("b_mod", 8 * SEGS), ("b_mod0", 16), ("g0", 8), ("g1", 8),
                  ("q_g", 1), ("k_g", 1), ("pool_scale", 2), ("conv_w", 54), ("conv_b", 18), ("hy_b1", 1), ("hy_b2", 1),
                  ("freq", 1), ("skip", 12), ("final_g", 8), ("g2", 32 * LAYERS), ("time", 4), ("inv_freq", 1),
                  ("row_valid", 4)):
    COLS[_name] = (N_COLS, _n)
    N_COLS += _n

BLOB = {}
N_BLOB = 0
for _name, _n in (("ws", 512), ("w2k", 128), ("w2v", 128), ("gate_w", 128), ("gm_b", 256), ("conv", 6), ("pos", 32),
                  ("gate_b", 1), ("gain", 8)):
    BLOB[_name] = (N_BLOB, _n)
    N_BLOB += _n


class Ledger:

    def __init__(self, nc, ctx, known):
        self.nc, self.ctx, self.known = nc, ctx, known
        self.engine = None
        self.sems, self.counts, self.marks, self.per, self.stack = {}, {}, {}, {}, []

    def sem(self, name):
        if name not in self.sems:
            self.sems[name] = self.ctx.enter_context(self.nc.semaphore(name))
        return self.sems[name]

    def did(self, label, by=1):
        name = label.split(".")[0]
        if self.engine and name not in self.counts:
            name = f"{name.split('_')[0]}_on_{self.engine}"
        self.counts[name] = self.counts.get(name, 0) + by
        assert label not in self.marks, label
        self.marks[label] = (name, self.counts[name], tuple(k for k, _, _ in self.stack))
        return self.sem(name), by

    def prime(self, name, n):
        self.counts[name] = n
        return self.sem(name), n

    def when(self, label, back=None):
        if self.known is None:
            return self.sem("unknown_yet"), 1
        name, value, loops = self.known[0][label]
        for loop in loops:
            per = self.known[1][loop, name]
            here = [var for k, var, _ in self.stack if k == loop]
            if here:
                value = here[0] * per + (value - (per if back == loop else 0))
            else:
                value = value + (self.known[2][loop] - 1) * per
        return self.sem(name), value

    @contextlib.contextmanager
    def loop(self, engine, name, trips):
        before = dict(self.counts)
        with engine.Fori(0, trips) as i:
            self.stack.append((name, i, trips))
            yield i
            self.stack.pop()
        self.per[name, "trips"] = trips
        for k, n in self.counts.items():
            more = n - before.get(k, 0)
            if more:
                self.per[name, k] = more
                self.counts[k] = n + (trips - 1) * more

    def learnt(self):
        return self.marks, self.per, {k[0]: v for k, v in self.per.items() if k[1] == "trips"}


def program(nc, A, known=None):
    f32, f32r, i32 = mybir.dt.float32, mybir.dt.float32r, mybir.dt.int32
    ACT, ALU, AX = mybir.ActivationFunctionType, mybir.AluOpType, mybir.AxisListType
    add, sub, mul = ALU.add, ALU.subtract, ALU.mult
    ds = bass.ds
    ctx = ExitStack()
    led = Ledger(nc, ctx, known)
    did, when, sem = led.did, led.when, led.sem

    base = (nc.sbuf_base + 63) // 64 * 64
    made = [0]

    def at(offset, shape, dt=f32, name="t"):
        made[0] += 1
        return nc.alloc_sbuf_tensor_at(f"{name}_{made[0]}", shape, dt, offset=base + offset)

    KB = 1024
    X_AT, BIG_AT = 0, 16 * KB
    WIDE_AT = BIG_AT + 64 * KB
    RAW_AT = WIDE_AT + 48 * KB
    SPLIT_AT = RAW_AT + 16 * KB
    MOD_AT = SPLIT_AT + 16 * KB
    TAB_AT = MOD_AT + 20 * KB
    SMALL_AT = TAB_AT + 16 * KB

    X = at(X_AT, [P, KT * S], name="x")
    Z = at(BIG_AT, [P, 32 * S], name="z")
    Hh = at(WIDE_AT, [P, KT, S], f32r, name="h_high")
    Hl = at(WIDE_AT + 16 * KB, [P, KT, S], f32r, name="h_low")
    Y = at(WIDE_AT + 32 * KB, [P, KT * S], name="y")
    Ch = at(WIDE_AT + 32 * KB, [P, KT, CTX], f32r, name="ctx_high")
    Cl = at(WIDE_AT + 40 * KB, [P, KT, CTX], f32r, name="ctx_low")
    RAW = [at(RAW_AT + 8 * KB * i, [P, 2, D], name="w_raw") for i in range(2)]
    WH = [at(SPLIT_AT + 4 * KB * i, [P, KT, P], f32r, name="w_high") for i in range(2)]
    WL = [at(SPLIT_AT + 8 * KB + 4 * KB * i, [P, KT, P], f32r, name="w_low") for i in range(2)]
    MOD = [at(MOD_AT + 4 * KB * i, [P, D], name="mod_raw") for i in range(4)]
    ACC = at(MOD_AT + 16 * KB, [P, D], name="mod_acc")
    small = [0]

    def keep(n, name, dt=f32):
        size = (4 * n + 31) // 32 * 32
        small[0] += size
        return at(SMALL_AT + small[0] - size, [P, n], dt, name=name)

    EYE = keep(3 * P, "eye")
    IDENT, ONES, HALVES = EYE[:, 0:P], EYE[:, P:2 * P], EYE[:, 2 * P:3 * P]
    COL = keep(N_COLS, "cols")
    CVEC = keep(16 + 8 * SEGS, "silu_cond")
    MODV0, MODV = keep(32, "mod0"), keep(8 * SEGS, "modv")
    AFF = keep(16, "norm_gain")
    RS = keep(S, "rs")
    SQ = [keep(S, "sq") for _ in range(2)]
    assert base + SMALL_AT + small[0] <= nc.sbuf_usable_end, small

    def col(name, k=0, n=1, rows=P):
        return COL[0:rows, COLS[name][0] + k:COLS[name][0] + k + n]

    PS = ctx.enter_context(nc.psum_tensor("banks", [P, 8 * S], f32))

    def bank(b, n=S, rows=slice(0, P)):
        return PS[rows, b * S:b * S + n]

    def z(n, rows=slice(0, P)):
        return Z[rows, n * S:(n + 1) * S]

    w_loaded = [sem(f"weights_loaded{i}") for i in range(2)]
    w_high, w_low, w_used = sem("weights_high"), sem("weights_low"), sem("weights_used")
    taken = sem("tile_taken")
    passed = sem("waits_passed")
    mod_loaded = [sem(f"mod_loaded{i}") for i in range(4)]
    mod_used, mod_summed, mod_taken = sem("mod_used"), sem("mod_summed"), sem("mod_taken")

    W4 = 4
    PR = [at(WIDE_AT + W4 * 768 * i, [P, 768], name="probs") for i in range(2)]
    PT = [at(WIDE_AT + W4 * (1536 + 3072 * i), [P, 6, S], name="probs_t") for i in range(2)]
    RSS = [at(WIDE_AT + W4 * (1536 + S * i), [P, S], name="rs_s") for i in range(6)]
    ZN = [at(WIDE_AT + W4 * (1536 + S * (6 + i)), [P, S], name="zn") for i in range(2)]
    RA = [at(WIDE_AT + W4 * (1536 + S * (8 + i)), [P, S], name="rope_a") for i in range(2)]
    RB = [at(WIDE_AT + W4 * (1536 + S * (10 + i)), [P, S], name="rope_b") for i in range(2)]
    PU, PV_, PW_ = [at(WIDE_AT + W4 * (7680 + 1056 * i), [P, 2, 528], name="pool") for i in range(3)]
    TABC = at(TAB_AT, [P, 4 * S + 3 * P], name="tab_attn")
    COS0, SIN0 = TABC[:, 0:S], TABC[:, S:2 * S]
    INVC = TABC[:, 2 * S:4 * S]
    ROPE0 = TABC[:, 4 * S:4 * S + P]
    POOLW = TABC[:, 4 * S + P:4 * S + 3 * P]
    CKV = at(BIG_AT + 20 * 2 * KB, [P, 4, CTX], name="ctx_kv")
    KALL = at(BIG_AT + 22 * 2 * KB, [P, 2, 768], name="k_all")
    VT = at(BIG_AT + 25 * 2 * KB, [P, 6, 2 * P], name="v_tokens")
    CX = at(BIG_AT + 16 * 2 * KB, [P, KT, CTX], name="ctx_in")
    CT_ = at(BIG_AT + 20 * 2 * KB, [P, KT, CTX], name="ctx_t")
    ACC1 = at(BIG_AT + 28 * 2 * KB, [P, D], name="mod_acc_ctx")
    NORM_T = Z[:, 0:KT * S]

    G = 384
    KSP = at(WIDE_AT, [P, 2, 4, G], name="k_spec")
    GSP = at(WIDE_AT + 12 * KB, [P, 2, 4, G], name="g_spec")
    PM = at(WIDE_AT + 24 * KB, [P, 2, 4, G], name="h_sum_diff")
    ZT = at(WIDE_AT + 36 * KB, [P, 4, G], name="z_tokens")
    HT = at(WIDE_AT + 42 * KB, [P, 2, G], name="hy_tmp")
    DFT = at(TAB_AT, [P, 16 * 256], name="dft")
    FWD = DFT[:, 0:2048].rearrange("p (e c t f) -> p e c t f", e=2, c=2, t=2)
    INV = DFT[:, 2048:4096].rearrange("p (e c f t) -> p e c f t", e=2, c=2, f=2)
    HDN = at(BIG_AT + 29 * 2 * KB, [64, S], name="hdn")
    DELTA = at(BIG_AT + 30 * 2 * KB, [P, 768], name="delta")
    EMB = at(WIDE_AT, [33, S], name="emb")
    HW12 = at(WIDE_AT + 2 * KB, [64, 2, 64], name="hy_w12")
    W3 = at(WIDE_AT + 45 * KB, [64, 768], name="hy_w3")
    ARG = [at(WIDE_AT + 4 * KB + 2 * KB * i, [64, S], name="arg") for i in range(4)]
    HH = [at(WIDE_AT + 36 * KB + 1536 * d, [P, G], name="filter") for d in range(2)]
    PMY = [at(WIDE_AT + 24 * KB + 2 * KB * c, [P, S], name="hy_y")[:, :] for c in range(2)]
    ABSA, DEC = SQ[0], SQ[1]
    HINV = AFF[:, 0:3]
    CSC = at(WIDE_AT, [P, 2, S], name="dft_ch")
    CTT = at(WIDE_AT + 4 * KB, [P, 4, S], name="dft_cos")
    NST = at(WIDE_AT + 12 * KB, [P, 4, S], name="dft_sin")
    AB = at(WIDE_AT + 20 * KB, [P, 4, S], name="fn_half")
    U2 = at(WIDE_AT + 28 * KB, [P, 2, S], name="fn_full")
    FNW = at(WIDE_AT + 32 * KB, [P, 2, CTX], name="fn_w")

    PAR = at(MOD_AT, [P, 2 * D], name="layer_params")
    TB2 = at(MOD_AT + 8 * KB, [P, 3 * S + 7 * P], name="tab_layers")
    BIAS, CMPB = TB2[:, 0:P], TB2[:, P:2 * P]
    DUPK, DUPR, ROT2, DUPV = [TB2[:, (2 + i) * P:(3 + i) * P] for i in range(4)]
    TRIL = TB2[:, 6 * P:7 * P]
    SCANM = TB2[:, 7 * P:7 * P + S]
    COS2, SIN2 = TB2[:, 7 * P + S:7 * P + 2 * S], TB2[:, 7 * P + 2 * S:7 * P + 3 * S]
    GMASK = at(MOD_AT + 8 * KB + 4 * (7 * P + 3 * S), [64, S], i32, name="gla_mask")
    CW1 = at(TAB_AT, [P, 32 * P], name="cmp_w1")
    LM = at(MOD_AT + 8 * KB + 4 * (7 * P + 4 * S), [P, 48], name="layer_mod")
    LG = COL[:, COLS["cond"][0]:COLS["cond"][0] + 32]

    def par(name, k=0, n=1, rows=slice(0, P)):
        return PAR[rows, BLOB[name][0] + k:BLOB[name][0] + k + n]

    HIDh = at(BIG_AT, [P, 16, S], f32r, name="hidden_high")
    HIDl = at(BIG_AT + 32 * KB, [P, 16, S], f32r, name="hidden_low")
    POSI = at(BIG_AT + 31 * 2 * KB, [P, S], i32, name="positions")
    TP = at(WIDE_AT, [P, 32, 31], name="cmp_blocks")
    QR = at(WIDE_AT + 4 * 1024, [P, 2, S], name="q_rope")
    KS_, KW_ = [at(WIDE_AT + 4 * (2048 + 512 * i), [P, S], name="k_rope") for i in range(2)]
    VS_, VW_ = [at(WIDE_AT + 4 * (3072 + 512 * i), [P, 4, P], name="v_tok") for i in range(2)]
    GT = at(WIDE_AT + 4 * 4096, [P, 4, 12], name="gates")
    KC = at(WIDE_AT + 4 * 4160, [P, 32], name="k_cmp")
    HC = at(WIDE_AT + 4 * 4192, [P, 2, 32], name="cmp_hidden")
    VC = at(WIDE_AT + 4 * 4256, [32, P], name="v_cmp")
    P2 = [at(WIDE_AT + 4 * (4608 + S * i), [P, S], name="probs2") for i in range(3)]
    PT2 = [at(WIDE_AT + 4 * (6144 + S * i), [P, 4, P], name="probs2_t") for i in range(2)]
    RT = [at(WIDE_AT + 4 * (7168 + S * i), [P, S], name="rope_t") for i in range(2)]
    P2.append(RT[0])
    NO = at(WIDE_AT + 4 * 8192, [P, 2, S], name="nsa_out")
    AO = at(WIDE_AT + 4 * 9216, [P, 2, S], name="conv_out")
    MO = at(WIDE_AT + 4 * 10240, [P, 2, S], name="gmlp_out")
    GO = at(WIDE_AT + 4 * 11264, [P, 2, S], name="gla_out")
    STAT = at(SMALL_AT + small[0], [P, 64], name="stats")
    ST2 = [STAT[:, 8 * i:8 * i + 8] for i in range(4)]
    DECY = STAT[:, 48:56]
    EPSC = at(SMALL_AT + small[0] + 256, [P, 1], name="eps")
    EMB2 = at(WIDE_AT + 12 * KB, [64, S], name="hdn_first")
    AF2 = at(MOD_AT + 4 * 5040, [P, 32], name="layer_gain")
    RL = [at(MOD_AT + 2 * KB * i, [P, S], name="relu") for i in range(2)]
    GE = [at(BIG_AT + 2 * KB * i, [P, S], name="gla_e") for i in range(4)]
    GB, GM = [at(BIG_AT + 2 * KB * (4 + i), [P, S], name="gla_b") for i in range(2)]
    GR = [at(WIDE_AT + 2 * KB * i, [P, S], name="group_rs") for i in range(4)]
    GV = at(WIDE_AT + 12 * KB, [64, 8, 384], name="gla_tok")
    GS = at(BIG_AT + 28 * 2 * KB, [P, 8, 256], name="gla_state")
    GA = at(BIG_AT + 22 * 2 * KB, [64, 4, S], name="gla_att")
    GMV = at(BIG_AT + 26 * 2 * KB, [P, 4, 2 * P], name="gmlp_tok")
    assert base + SMALL_AT + small[0] + 260 <= nc.sbuf_usable_end, small
    block = ctx.enter_context(nc.Block())

    R1 = [("ck", 0), ("ck", 1), ("k", 0), ("k", 1)] + [("q", h) for h in range(6)]
    NC1 = len(R1)
    BATCHES = (range(0, 4), range(4, NC1))
    RS_SLOT = [j if j < 4 else j - 4 for j in range(NC1)]
    V_T, X1_T, X2_T, HG_T, FN_T, FG_T = 0, 6, 12, 18, 24, 26
    STEPS = [(g, o) for g in range(2) for o in range(2)]
    ITEMS = [(h, i, br) for h in range(4) for i in range(NT) for br in range(3)]
    WIDTH = [31 if br == 2 else P * (i + 1) for _, i, br in ITEMS]
    ROT_BANKS = (6, 1, 6, 1)
    SCORE_BANKS = (0, 1, 2, 7)
    MIXED = ("conv_y.all", "nsa_o.3", "gla_y.1", "gm_y.1")
    UNITS_AT = ((0, 1, 2), (3, 4, 5), (6, 7), ())

    @block.sync
    def _(sp):
        sp.dma_start(COL[:, :], A["cols"]).then_inc(*did("in_small.cols", 16))
        sp.dma_start(EYE[:, :], A["eye"]).then_inc(*did("in_small.all", 16))
        sp.dma_start(X[:, :].rearrange("p (k t) -> p k t", k=KT), A["xT"].rearrange("(k p) t -> p k t", p=P)).then_inc(*did("in_x.all", 16))
        sp.dma_start(CX[:, :, :], A["ctxT"].rearrange("(k p) t -> p k t", p=P)).then_inc(*did("in_ctx.all", 16))

        for u in range(2 * UNITS):
            if u >= 4:
                sp.wait_ge(mod_used, u - 3 + PRIME)
            sp.dma_start(MOD[u % 4][:, :], A["wmod0"][u * P:(u + 1) * P, :]).then_inc(mod_loaded[u % 4], 16)
        sp.dma_start(TABC[:, :], A["tab_attn"]).then_inc(*did("in_tabc.all", 16))

        def load_pair(q, half):
            sp.wait_ge(w_low, 4 * q + 2 * half - 2 + PRIME)
            sp.dma_start(RAW[half][:, :, :], A["wt"][ds((2 * q + half) * P, P), :].rearrange("p (n c) -> p n c", n=2)).then_inc(w_loaded[half], 16)

        def load_units(q, ks):
            for k in ks:
                sp.wait_ge(mod_used, 8 * q + 16 + k - 3 + PRIME)
                sp.dma_start(MOD[k % 4][:, :], A["wmod"][ds((8 * q + k) * P, P), :]).then_inc(mod_loaded[k % 4], 16)

        def bodies(name, q0, trips):
            with led.loop(sp, name, trips) as i:
                load_body(i + q0)

        def load_body(q):
            load_units(q, (0, 1, 2, 3))
            load_pair(q, 1)
            load_units(q, (4, 5, 6, 7))
            load_pair(q + 1, 0)

        load_pair(0, 0)
        load_body(0)
        bodies("ev_in", 1, EV_IN // 4 - 1)
        bodies("ev_out", 5, EV_OUT // 4)
        sp.wait_ge(*when("pool_y.1"))
        sp.wait_ge(*when("pool_d.all"))
        sp.dma_start(DFT[:, :], A["dft"]).then_inc(*did("in_hy.dft", 16))
        bodies("od_in", 7, OD_IN // 4)
        sp.wait_ge(w_used, T_OD_OUT + PRIME)
        sp.dma_start(EMB[:, :], A["emb"]).then_inc(*did("in_hy2.emb", 16))
        sp.dma_start(HW12[0:33, 0, :], A["hy_w1"]).then_inc(*did("in_hy2.w1", 16))
        sp.dma_start(HW12[:, 1, :], A["hy_w2"]).then_inc(*did("in_hy2.w2", 16))
        sp.dma_start(DELTA[:, :], A["delta"]).then_inc(*did("in_hy2.all", 16))
        for n, (g, o) in enumerate(STEPS):
            if n:
                sp.wait_ge(*when(f"hy_filt.{n - 1}.7"))
            sp.dma_start(W3[:, :], A["hy_w3"][:, (2 * o + g) * 768:(2 * o + g + 1) * 768]).then_inc(*did(f"in_w3.{n}", 16))
        sp.wait_ge(*when("hy_out.3.2"))
        sp.wait_ge(*when("hy_inv.3.2"))
        sp.dma_start(CSC[:, :, :], A["dft_ch"].rearrange("p (k c) -> p k c", k=2)).then_inc(*did("in_fn.csc", 16))
        sp.dma_start(FNW[:, :, :], A["fn_w"].rearrange("(k p) c -> p k c", p=P)).then_inc(*did("in_fn.w", 16))
        sp.dma_start(CTT[:, :, :], A["dft_cos"].rearrange("(k p) c -> p k c", p=P)).then_inc(*did("in_fn.cos", 16))
        sp.dma_start(NST[:, :, :], A["dft_sin"].rearrange("(k p) c -> p k c", p=P)).then_inc(*did("in_fn.all", 16))
        bodies("od_out", 14, OD_OUT // 4)

        sp.wait_ge(mod_taken, SEGS + 2)
        sp.dma_start(TB2[:, 0:7 * P + S], A["tab_layers"]).then_inc(*did("in_tab2.all", 16))
        sp.dma_start(GMASK[:, :], A["gla_mask"]).then_inc(*did("in_tab2.mask", 16))
        sp.dma_start(POSI[:, :], A["pos"].to_broadcast([P, S])).then_inc(*did("in_tab2.pos", 16))
        with led.loop(sp, "layers", LAYERS) as lay:
            sp.wait_ge(w_used, lay * PER_LAYER + T_LAYERS - 1 + PRIME)
            sp.dma_start(CW1[:, :], A["cmp_w1"][ds(lay * P, P), :]).then_inc(*did("in_cw1.all", 16))

            def plain(name, q0, trips):
                with led.loop(sp, name, trips) as i:
                    for half in (1, 0):
                        load_pair(lay * (PER_LAYER // 4) + i + (T_LAYERS // 4 + q0 + 1 - half), half)
            plain("all_l", 0, PER_LAYER // 4)
        sp.wait_ge(*when("y2_x.7"))
        sp.dma_start(A["out"].rearrange("(k p) t -> p k t", p=P), X[:, :].rearrange("p (k t) -> p k t", k=KT)).then_inc(*did("stored.all", 16))
        sp.wait_ge(*when("stored.all"))

    @block.scalar
    def _(act):
        led.engine = "scalar"
        def split_high(q, b):
            act.wait_ge(w_loaded[b // 2], 16 * q + 16)
            act.wait_ge(w_used, 4 * q + b - 1 + PRIME)
            nc.scalar.activation(WH[b % 2][:, :, :].rearrange("p k c -> p (k c)"), RAW[b // 2][:, b % 2, :], ACT.Copy).then_inc(w_high, 1)

        def copy_out(q, b, dst, func=ACT.Copy):
            act.wait_ge(w_used, 4 * q + b + 1 + PRIME)
            nc.scalar.activation(dst, bank(b), func).then_inc(taken, 1)

        def next_tile(q, b):
            split_high(q + 1 if b == 3 else q, (b + 1) % 4)

        def squares(tag, src, n, k, ready=None):
            if ready:
                act.wait_ge(*ready)
            if k >= 2:
                act.wait_ge(*when(f"{tag}_ss.{k - 2}"))
            nc.scalar.activation(SQ[k % 2][:, 0:n], src, ACT.Square).then_inc(*did(f"{tag}_sq.{k}"))

        def root(tag, b, n, count):
            act.wait_ge(*when(f"{tag}_ss.7"))
            nc.scalar.activation(RS[:, 0:n], bank(b, n), ACT.Ln, bias=EPSC[:, :], scale=1.0 / count).then_inc(*did(f"{tag}_ln.all"))
            act.wait_ge(*when(f"{tag}_ln.all"))
            nc.scalar.activation(RS[:, 0:n], RS[:, 0:n], ACT.Exp, scale=-0.5).then_inc(*did(f"{tag}_rs.all"))

        def square_tile(tag, src, b, slot, *ready):
            act.wait_ge(*ready)
            nc.scalar.activation(SQ[slot][:, :], src, ACT.Square).then_inc(*did(f"{tag}_tile.{b}"))

        def highs(tag, T, B, H, n):
            for k in range(KT):
                act.wait_ge(*when(f"{tag}_t.{k}"))
                nc.scalar.activation(H[:, k, :], T[:, k * n:(k + 1) * n], ACT.Identity, bias=B[:, k:k + 1]).then_inc(*did(f"{tag}_hi.{k}"))

        act.sem_inc(w_high, PRIME)
        act.sem_inc(taken, PRIME)
        act.sem_inc(*led.prime("y1_tile", 4))
        act.sem_inc(*led.prime("y2_tile", 2))
        act.wait_ge(*when("in_small.all"))
        act.wait_ge(*when("eps.all"))
        nc.scalar.activation(CVEC[:, :], COL[:, 0:16 + 8 * SEGS], ACT.Silu).then_inc(*did("silu.conds"))

        act.wait_ge(*when("in_x.all"))
        for k in range(KT):
            squares("n0", X[:, k * S:(k + 1) * S], S, k)
        root("n0", 5, S, D)
        highs("n0", NORM_T, MODV0[:, 0:8], Hh, S)
        act.wait_ge(*when("in_ctx.all"))
        for k in range(KT):
            squares("nc", CX[:, k, :], CTX, k, when(f"n0_ss.{6 + k}") if k < 2 else None)
        act.wait_ge(*when("n0_t.7"))
        root("nc", 6, CTX, D)
        highs("nc", CT_[:, :, :].rearrange("p k t -> p (k t)"), MODV0[:, 16:24], Ch, CTX)

        split_high(0, 0)
        for b in range(4):
            next_tile(0, b)
            copy_out(0, b, z(b))
            act.wait_ge(*when(f"ckv_mm.{b}"))
            nc.scalar.activation(CKV[:, b, :], bank(5 + b % 2, CTX), ACT.Copy).then_inc(*did(f"ckv.{b}"))
        with led.loop(act, "ev_in", EV_IN // 4 - 1) as i:
            for b in range(4):
                next_tile(i + 1, b)
                copy_out(i + 1, b, Z[:, ds((i * 4 + 4 + b) * S, S)])

        act.wait_ge(taken, EV_IN + PRIME)
        for n in range(12, 20):
            nc.scalar.activation(z(n), z(n), ACT.Silu).then_inc(*did(f"ev_gate.{n}"))

        def head_src(j):
            kind, h = R1[j]
            return (CKV[:, h, :], CTX) if kind == "ck" else (z(h) if kind == "k" else z(4 + h), S)

        def head_square(j):
            if j >= 2:
                act.wait_ge(*when(f"hn_ss.{j - 2}"))
            else:
                act.wait_ge(*when("ckv.3"))
            src, n = head_src(j)
            nc.scalar.activation(SQ[j % 2][:, 0:n], src, ACT.Square).then_inc(*did(f"hn_sq.{j}"))

        head_square(0)
        for batch in BATCHES:
            for j in batch:
                if j + 1 < NC1:
                    head_square(j + 1)
                n = head_src(j)[1]
                act.wait_ge(*when(f"hn_ss.{j}"))
                if 4 <= j < 8:
                    act.wait_ge(*when(f"hn_zn.{j - 4}"))
                nc.scalar.activation(RSS[RS_SLOT[j]][:, 0:n], bank(j % 2, n), ACT.Ln, bias=EPSC[:, :], scale=1.0 / P).then_inc(*did(f"hn_ln.{j}"))
            for j in batch:
                n = head_src(j)[1]
                rs = RSS[RS_SLOT[j]][:, 0:n]
                act.wait_ge(*when(f"hn_ln.{j}"))
                nc.scalar.activation(rs, rs, ACT.Exp, scale=-0.5).then_inc(*did(f"hn_rs.{j}"))
        for j in range(6):
            act.wait_ge(*when(f"vt_mm.{j}"))
            nc.scalar.activation(VT[:, j, :], bank(4 + j % 3, 2 * P), ACT.Copy).then_inc(*did(f"vt.{j}"))

        def copy_pt(n):
            h, i = divmod(n, 4)
            act.wait_ge(*when(f"pt_mm.{n}"))
            if h >= 2 and i == 0:
                act.wait_ge(*when(f"attn_o.{h - 2}"))
            nc.scalar.activation(PT[h % 2][:, :, i * P:(i + 1) * P], PS[:, 4 * S:4 * S + 768].rearrange("p (j q) -> p j q", j=6), ACT.Copy).then_inc(*did(f"pt.{n}"))

        for n in range(24):
            act.wait_ge(*when(f"nmax.{n}"))
            if n >= 2:
                act.wait_ge(*when(f"pt_mm.{n - 2}"))
            at0 = (n % 2) * 2 * S
            nc.scalar.activation(PR[n % 2][:, :], PS[:, at0:at0 + 768], ACT.Exp, bias=STAT[:, n:n + 1], scale=float(P) ** -0.5,
                                 accum_out=STAT[:, 32 + n:33 + n]).then_inc(*did(f"prob.{n}"))
            if n:
                copy_pt(n - 1)
        copy_pt(23)

        MIX1 = [10, 11, 4, 5, 6, 7, 8, 9]
        act.wait_ge(*when("attn_o.5"))
        for k, n in enumerate(MIX1):
            act.wait_ge(*when(f"pool_out.{k}" if k < 2 else f"attn_y.{k - 2}"))
            nc.scalar.activation(Hh[:, k, :], z(n), ACT.Copy).then_inc(*did(f"mx1_hi.{k}"))
        with led.loop(act, "ev_out", EV_OUT // 4) as i:
            for b in range(4):
                next_tile(i + 5, b)

        act.wait_ge(taken, T_OD_IN + PRIME)
        for k in range(KT):
            squares("n1", X[:, k * S:(k + 1) * S], S, k)
        root("n1", 5, S, D)
        highs("n1", NORM_T, MODV[:, 8:16], Hh, S)
        with led.loop(act, "od_in", OD_IN // 4) as i:
            for b in range(4):
                next_tile(i + 7, b)
                copy_out(i + 7, b, Z[:, ds((i * 4 + 1 + b) * S, S)])

        act.wait_ge(taken, T_OD_OUT + PRIME)
        for l in range(2):
            act.wait_ge(*when(f"hy_arg.{l}"))
            nc.scalar.activation([EMB2, HDN][l][:, :], ARG[2][:, :], ACT.Sin).then_inc(*did(f"hy_sin.{l}"))
        for n in range(HG_T, HG_T + 6):
            nc.scalar.activation(z(n + 1), z(n + 1), ACT.Silu).then_inc(*did(f"od_gate.{n}"))
        for n in range(FG_T, FG_T + 2):
            nc.scalar.activation(z(n + 1), z(n + 1), ACT.Silu).then_inc(*did(f"od_gate.{n}"))
        for j in range(18):
            if j:
                act.wait_ge(*when(f"conv3.{j - 1}"))
            nc.scalar.activation(z(j), z(j + 1), ACT.Identity, scale=col("conv_w", 18 + j), bias=col("conv_b", j)).then_inc(*did(f"conv_mid.{j}"))
        act.wait_ge(*when("in_hy2.all"))
        for n, (g, o) in enumerate(STEPS):
            for j in range(4):
                if n or j:
                    act.wait_ge(*when(f"hy_d1.{n if j else n - 1}.{j - 1 if j else 3}"))
                nc.scalar.activation(DEC[:, 0:G], DELTA[:, g * G:(g + 1) * G], ACT.Exp, scale=col("time", j)).then_inc(*did(f"hy_dec.{n}.{j}"))
                for d in range(2):
                    act.wait_ge(*when(f"hy_d{d}.{n}.{j}"))
                    if j or n:
                        act.wait_ge(*when(f"hy_abs.{n}.{j - 1}.1" if j else f"hz_fly.{n - 1}.7"))
                    nc.scalar.activation(HT[:, d, :], HH[d][:, :], ACT.Abs).then_inc(*did(f"hy_mag.{n}.{j}.{d}"))
            for kind in ("hk", "hz"):
                if kind == "hz":
                    for j in range(4):
                        act.wait_ge(*when(f"hy_zt_mm.{n}.{j}"))
                        act.wait_ge(*when(f"hy_abs.{n}.3.1"))
                        if n and j == 0:
                            act.wait_ge(*when(f"hz_mm.{n - 1}.1"))
                        nc.scalar.activation(ZT[:, j, :], bank(4 + j, G), ACT.Copy).then_inc(*did(f"hy_zt.{n}.{j}"))
                for ft in range(2):
                    act.wait_ge(*when(f"{kind}_mm.{n}.{ft}"))
                    if ft or kind == "hz":
                        act.wait_ge(*when(f"hk_fly.{n}.7" if kind == "hz" and not ft else f"{kind}_fly.{n}.{4 * ft - 1}"))
                    elif n:
                        act.wait_ge(*when(f"hz_fly.{n - 1}.7"))
                    for c in range(2):
                        nc.scalar.activation(HT[:, c, :], bank(4 * ft + 2 * c + 1, G), ACT.Copy).then_inc(*did(f"{kind}_odd.{n}.{2 * ft + c}"))
        for j in range(4):
            act.wait_ge(*when(f"fn_a.{j}"))
            nc.scalar.activation(AB[:, j, :], bank(j), ACT.Copy).then_inc(*did(f"fn_ab.{j}"))
        for m in range(2):
            act.wait_ge(*when(f"fn_b.{m}"))
            nc.scalar.activation(U2[:, m, :], bank(4 + m), ACT.Copy).then_inc(*did(f"fn_u2.{m}"))
        act.wait_ge(*when("fn_y.1"))
        for k in range(KT):
            act.wait_ge(*when(f"hy_out.{1 if k < 3 else 3}.{k % 3}" if k < 6 else f"fn_out.{k - 6}"))
            nc.scalar.activation(Hh[:, k, :], z(k) if k < 6 else z(FN_T + 1 + k - 6), ACT.Copy).then_inc(*did(f"mx2_hi.{k}"))
        with led.loop(act, "od_out", OD_OUT // 4) as i:
            for b in range(4):
                next_tile(i + 14, b)
        act.wait_ge(taken, T_LAYERS + PRIME)
        for k in range(KT):
            squares("nf", X[:, k * S:(k + 1) * S], S, k)
        root("nf", 5, S, D)
        for c in range(2):
            act.wait_ge(*when(f"rot_arg.{c}"))
            nc.scalar.activation([SIN2, COS2][c], RT[c][:, :], ACT.Sin).then_inc(*did(f"rot.{c}"))

        with led.loop(act, "layers", LAYERS) as lay:
            Q = lay * (PER_LAYER // 4) + T_LAYERS // 4
            act.wait_ge(*when("nf_x.7"))
            act.wait_ge(*when("layer_cols.gain"))
            act.wait_ge(*when("y2_x.7", back="layers"))
            for k in range(KT):
                squares("h1", X[:, k * S:(k + 1) * S], S, k)
            root("h1", 5, S, D)
            highs("h1", NORM_T, LM[:, 0:8], Hh, S)
            with led.loop(act, "mx_in", 5) as i:
                for b in range(4):
                    next_tile(i + Q, b)
                    copy_out(i + Q, b, Z[:, ds((i * 4 + b) * S, S)])
            next_tile(Q + 5, 0)
            copy_out(Q + 5, 0, z(20))
            copy_out(Q + 5, 1, z(21))
            act.wait_ge(taken, 4 * Q + 22 + PRIME)
            act.sem_inc(w_high, 2)
            act.sem_inc(taken, 2)
            split_high(Q + 6, 0)

            for m in range(2):
                act.wait_ge(*when(f"gm_c.{m}"))
                if m == 0:
                    act.wait_ge(*when("h1_ss.7"))
                nc.scalar.activation(SQ[m][:, :], MO[:, m, :], ACT.Square).then_inc(*did(f"gm_sq.{m}"))
            for m in range(2):
                act.wait_ge(*when(f"gm_var.{m}"))
                nc.scalar.activation(P2[m][:, :], bank(2 + m), ACT.Ln, bias=EPSC[:, :], scale=1.0 / 64).then_inc(*did(f"gm_ln.{m}"))
            for m in range(2):
                act.wait_ge(*when(f"gm_ln.{m}"))
                nc.scalar.activation(P2[m][:, :], P2[m][:, :], ACT.Exp, scale=-0.5).then_inc(*did(f"gm_rs.{m}"))
            for c in range(2):
                act.wait_ge(*when(f"cmp_h.{c}"))
                nc.scalar.activation(HC[:, c, 0:31], bank((7, 4)[c], 31), ACT.Silu).then_inc(*did(f"cmp_act.{c}"))
            act.wait_ge(*when("cmp_kv.1"))
            nc.scalar.activation(KC[:, 0:31], bank(2, 31), ACT.Copy).then_inc(*did("cmp_k.all"))
            nc.scalar.activation(VC[0:31, :], bank(3, P, slice(0, 31)), ACT.Copy).then_inc(*did("cmp_v.all"))
            act.wait_ge(*when("gate_t.all"))
            nc.scalar.activation(GT[:, :, :], PS[:, 4 * S:5 * S].rearrange("p (j c) -> p j c", j=4)[:, :, 32:44], ACT.Sigmoid).then_inc(*did("gates.all"))
            for c in range(2):
                act.wait_ge(*when(f"v_tok_mm.{c}"))
                nc.scalar.activation([VS_, VW_][c][:, :, :], PS[:, (5 + c) * S:(6 + c) * S].rearrange("p (j c) -> p j c", j=4), ACT.Copy).then_inc(*did(f"v_tok.{c}"))

            for j in range(2):
                act.wait_ge(*when(f"gm_vt_mm.{2 * j + 1}"))
                nc.scalar.activation(GMV[:, 2 * j:2 * j + 2, :], bank(j).rearrange("p (j c) -> p j c", j=2), ACT.Copy).then_inc(*did(f"gm_vt.{j}"))

            def decay_logs():
                act.wait_ge(*when("gla_x.all"))
                act.wait_ge(*when("gla_min.all"))
                nc.scalar.activation(GE[0][:, :], GE[0][:, :], ACT.Abs).then_inc(*did("gla_abs.all"))
                act.wait_ge(*when("gla_abs.all"))
                nc.scalar.activation(GE[0][:, :], GE[0][:, :], ACT.Exp, scale=-1.0).then_inc(*did("gla_exp.all"))
                act.wait_ge(*when("gla_exp.all"))
                nc.scalar.activation(GE[0][:, :], GE[0][:, :], ACT.Ln, bias=1.0).then_inc(*did("gla_ln.all"))

            def decays():
                for c in range(4):
                    act.wait_ge(*when(f"gla_d.{min(c, 2)}"))
                    nc.scalar.activation(GE[c][:, :], (GE[c] if c < 3 else GB)[:, :], ACT.Exp, scale=1.0 / 16).then_inc(*did(f"gla_e.{c}"))
                nc.scalar.activation(DECY[:, :], GB[:, :].rearrange("p (c t) -> p c t", t=64)[:, :, 63], ACT.Exp, scale=1.0 / 16).then_inc(*did("gla_decay.all"))

            def copy_pt2(n):
                h, i, br = ITEMS[n]
                act.wait_ge(*when(f"p2t_mm.{n}"))
                if n >= 2:
                    act.wait_ge(*when(f"p2v.{n - 2}"))
                if br == 2:
                    nc.scalar.activation(PT2[n % 2][0:31, 0, :], bank(3 + n % 2, P, slice(0, 31)), ACT.Copy).then_inc(*did(f"p2t.{n}"))
                else:
                    nc.scalar.activation(PT2[n % 2][:, 0:i + 1, :], bank(3 + n % 2, (i + 1) * P).rearrange("p (j q) -> p j q", q=P), ACT.Copy).then_inc(*did(f"p2t.{n}"))

            def head_out(h):
                rows = slice(64 * (h % 2), 64 * (h % 2) + 64)
                act.wait_ge(*when(f"p2v.{12 * h + 11}"))
                nc.scalar.activation(NO[rows, h // 2, :], bank(5 + h % 2, S, rows), ACT.Copy).then_inc(*did(f"nsa_o.{h}"))

            for n, (h, i, br) in enumerate(ITEMS):
                w = WIDTH[n]
                act.wait_ge(*when(f"nmax2.{n}"))
                if n >= 4:
                    act.wait_ge(*when(f"p2t_mm.{n - 4}"))
                nc.scalar.activation(P2[n % 4][:, 0:w], bank(SCORE_BANKS[n % 4], w), ACT.Exp, bias=ST2[n % 4][:, 0:1], scale=0.125,
                                     accum_out=ST2[n % 4][:, 1:2]).then_inc(*did(f"prob2.{n}"))
                if n >= 2:
                    copy_pt2(n - 2)
                if n == 4:
                    decay_logs()
                if n == 12:
                    decays()
                if n >= 4 and (n - 4) % 12 == 11:
                    head_out((n - 4) // 12)
            copy_pt2(len(ITEMS) - 2)
            copy_pt2(len(ITEMS) - 1)
            head_out(3)

            for c in range(8):
                act.wait_ge(*when(f"gla_tok_mm.{c}"))
                nc.scalar.activation(GV[:, c, :], bank(4 + c % 2, 384, slice(0, 64)), ACT.Copy).then_inc(*did(f"gla_tok.{c}"))
            for m in range(2):
                nc.scalar.activation(z(15 + m), z(15 + m), ACT.Silu).then_inc(*did(f"gla_gate.{m}"))
            for m in range(2):
                act.wait_ge(*when(f"gla_o.{m}"))
                nc.scalar.activation(GO[:, m, :], bank(6 + m), ACT.Copy).then_inc(*did(f"gla_out.{m}"))
                nc.scalar.activation(SQ[m][:, :], bank(6 + m), ACT.Square).then_inc(*did(f"gla_sq.{m}"))
            for m in range(2):
                act.wait_ge(*when(f"gla_ss.{m}"))
                nc.scalar.activation(GR[m][:, :], bank(m), ACT.Ln, bias=EPSC[:, :], scale=1.0 / 64).then_inc(*did(f"gla_rln.{m}"))
            for m in range(2):
                act.wait_ge(*when(f"gla_rln.{m}"))
                nc.scalar.activation(GR[m][:, :], GR[m][:, :], ACT.Exp, scale=-0.5).then_inc(*did(f"gla_rs.{m}"))

            def group(g):
                return (AO, NO, GO, MO)[g]
            for g in range(4):
                for m in range(2):
                    act.wait_ge(*when(MIXED[g]))
                    if g:
                        act.wait_ge(*when(f"gr_ss.{2 * g - 2 + m}"))
                    else:
                        act.wait_ge(*when(f"gla_ss.{m}"))
                    nc.scalar.activation(SQ[m][:, :], group(g)[:, m, :], ACT.Square).then_inc(*did(f"gr_sq.{2 * g + m}"))
            for g in range(4):
                act.wait_ge(*when(f"gr_ss.{2 * g + 1}"))
                if g < 2:
                    act.wait_ge(*when(f"gla_n.{g}"))
                nc.scalar.activation(GR[g][:, :], bank(4 + g), ACT.Ln, bias=EPSC[:, :], scale=1.0 / 256).then_inc(*did(f"gr_ln.{g}"))
            for g in range(4):
                act.wait_ge(*when(f"gr_ln.{g}"))
                nc.scalar.activation(GR[g][:, :], GR[g][:, :], ACT.Exp, scale=-0.5).then_inc(*did(f"gr_rs.{g}"))
            act.wait_ge(*when("gr_n.7"))
            for k in range(KT):
                nc.scalar.activation(Hh[:, k, :], z(k), ACT.Copy).then_inc(*did(f"mx3_hi.{k}"))
            with led.loop(act, "mx_out", 2) as i:
                for b in range(4):
                    next_tile(i + Q + 6, b)
                    square_tile("y1", bank(b), b, b % 2, w_used, 4 * Q + 4 * i + 24 + b + 1 + PRIME)
                    copy_out(i + Q + 6, b, Y[:, ds((i * 4 + b) * S, S)])
            root("y1", 5, S, D)
            for k in range(KT):
                squares("h2", X[:, k * S:(k + 1) * S], S, k, when(f"y1_x.{k}"))
            act.wait_ge(*when("y1_t.7"))
            root("h2", 6, S, D)
            highs("h2", NORM_T, LM[:, 24:32], Hh, S)
            for a in range(2):
                q0 = Q + 8 + 8 * a
                with led.loop(act, f"up{a}", 4) as i:
                    for b in range(4):
                        next_tile(i + q0, b)
                        act.wait_ge(w_used, 4 * q0 + 4 * i + b + 1 + PRIME)
                        act.wait_ge(*(when(f"hid{a}_b.{b - 2}") if b >= 2 else when(f"hid{a}_b.{b + 2}", back=f"up{a}")))
                        nc.scalar.activation(RL[b % 2][:, :], bank(b), ACT.Relu).then_inc(taken, 1)
                        act.wait_ge(taken, 4 * q0 + 4 * i + b + 1 + PRIME)
                        nc.scalar.activation(SQ[b % 2][:, :], RL[b % 2][:, :], ACT.Square).then_inc(*did(f"relu{a}.{b}"))
                with led.loop(act, f"down{a}", 4) as i:
                    for b in range(4):
                        next_tile(i + q0 + 4, b)
                        if b % 2 and a == 0:
                            act.wait_ge(w_used, 4 * q0 + 4 * i + 16 + b + 1 + PRIME)
                            nc.scalar.activation(Y[:, ds((i * 2 + b // 2) * S, S)], bank(b - 1), ACT.Copy).then_inc(taken, 2)
                        if b % 2 and a == 1:
                            square_tile("y2", Y[:, ds((i * 2 + b // 2) * S, S)], b // 2, b // 2, taken, 4 * q0 + 4 * i + 16 + b + 1 + PRIME)
            root("y2", 5, S, D)

    @block.gpsimd
    def _(pool):
        led.engine = "gpsimd"
        gp = nc.gpsimd
        pool.wait_ge(taken, EV_IN + PRIME)
        pool.wait_ge(*when("in_tabc.all"))
        for c, t in enumerate((PU, PV_, PW_)):
            gp.memset(t[:, :, :], 0.0).then_inc(*did(f"pool_z.{c}"))
        pool.wait_ge(*when("pool_z.2"))
        for m in range(2):
            gp.tensor_copy(PU[:, m, 8:8 + S], z(10 + m)).then_inc(*did(f"pool_u.{m}"))
        pool.wait_ge(*when("pool_u.1"))
        gp.tensor_tensor(PV_[:, :, 0:527], PU[:, :, 0:527], PU[:, :, 1:528], add).then_inc(*did("pool_s.2"))
        pool.wait_ge(*when("pool_s.2"))
        gp.tensor_tensor(PW_[:, :, 0:525], PV_[:, :, 0:525], PV_[:, :, 2:527], add).then_inc(*did("pool_s.4"))
        pool.wait_ge(*when("pool_s.4"))
        gp.tensor_tensor(PV_[:, 1, 0:521], PW_[:, 1, 0:521], PW_[:, 1, 4:525], add).then_inc(*did("pool_s.8"))
        pool.wait_ge(*when("pool_s.8"))
        gp.tensor_tensor(PW_[64:P, 1, 0:513], PV_[64:P, 1, 0:513], PV_[64:P, 1, 8:521], add).then_inc(*did("pool_s.16"))
        pool.wait_ge(*when("pool_s.16"))
        for g, (w, src) in enumerate(((2, PV_), (4, PW_), (8, PV_), (16, PW_))):
            m, rows = g // 2, slice(64 * (g % 2), 64 * (g % 2) + 64)
            gp.tensor_tensor(Z[rows, (10 + m) * S:(11 + m) * S], src[rows, m, 8 - w // 2:8 - w // 2 + S], INVC[rows, m * S:(m + 1) * S], mul).then_inc(*did(f"pool_m.{g}"))
        for g in range(4):
            m, rows = g // 2, slice(64 * (g % 2), 64 * (g % 2) + 64)
            pool.wait_ge(*when(f"pool_m.{g}"))
            gp.tensor_tensor(Z[rows, (10 + m) * S:(11 + m) * S], Z[rows, (10 + m) * S:(11 + m) * S], PU[rows, m, 8:8 + S], sub).then_inc(*did("pool_d.all" if g == 3 else f"pool_d.{g}"))
        with led.loop(pool, "layers", LAYERS) as lay:
            pool.wait_ge(taken, lay * PER_LAYER + (T_LAYERS + L_OUT + PRIME))
            pool.sem_inc(passed, 1)
            gp.memset(GS[:, :, :], 0.0).then_inc(*did("gla_zero.0"))
            gp.memset(GA[:, :, :], 0.0).then_inc(*did("gla_zero.1"))

    @block.vector
    def _(dve):
        led.engine = "vector"
        v = nc.vector

        def split_low(q, b):
            dve.wait_ge(w_high, 4 * q + b + 1 + PRIME)
            v.tensor_tensor(WL[b % 2][:, :, :].rearrange("p k c -> p (k c)"), RAW[b // 2][:, b % 2, :],
                            WH[b % 2][:, :, :].rearrange("p k c -> p (k c)").bitcast(f32), sub).then_inc(w_low, 1)

        def next_tile(q, b):
            split_low(q + 1 if b == 3 else q, (b + 1) % 4)

        def unit(q, k):
            dve.wait_ge(mod_loaded[k % 4], 16 * (2 * q + k // 4 + 5))
            if k:
                dve.wait_ge(mod_used, 8 * q + 16 + k + PRIME)
            else:
                dve.wait_ge(mod_summed, q + 2)
            c = CVEC[:, ds(q * 8 + 16 + k, 1)]
            if k:
                v.scalar_tensor_tensor(ACC[:, :], MOD[k % 4][:, :], c, ACC[:, :], mul, add).then_inc(mod_used, 1)
            else:
                v.tensor_scalar(ACC[:, :], MOD[k % 4][:, :], c, None, mul).then_inc(mod_used, 1)

        def side(q, b):
            next_tile(q, b)
            for k in UNITS_AT[b]:
                unit(q, k)
            if b == 3:
                dve.wait_ge(mod_summed, q + 3)
                v.tensor_tensor(MODV[:, ds(q * 8, 8)], bank(4, 8), COL[:, ds(q * 8 + COLS["b_mod"][0], 8)], add).then_inc(mod_taken, 1)

        def to_halves(tag, src, A_, B, T, L, H, n):
            for k in range(KT + 1):
                if k < KT:
                    v.scalar_tensor_tensor(T[:, k * n:(k + 1) * n], src(k), A_[:, k:k + 1], RS[:, 0:n], mul, mul).then_inc(*did(f"{tag}_t.{k}"))
                if k:
                    dve.wait_ge(*when(f"{tag}_hi.{k - 1}"))
                    v.scalar_tensor_tensor(L[:, k - 1, :], T[:, (k - 1) * n:k * n], B[:, k - 1:k], H[:, k - 1, :].bitcast(f32), add, sub).then_inc(*did(f"{tag}_lo.{k - 1}"))

        def zero_squares(tag):
            v.memset(SQ[1][:, :], 0.0).then_inc(*did(f"{tag}_zero.1"))

        def lows(tag, srcs):
            for k, src in enumerate(srcs):
                dve.wait_ge(*when(f"{tag}_hi.{k}"))
                v.tensor_tensor(Hl[:, k, :], src, Hh[:, k, :].bitcast(f32), sub).then_inc(*did(f"{tag}_lo.{k}"))

        dve.sem_inc(w_low, PRIME)
        dve.sem_inc(mod_used, PRIME)
        dve.sem_inc(*led.prime("hid0_b", 4))
        dve.sem_inc(*led.prime("hid1_b", 4))
        dve.sem_inc(*led.prime("y2_x", 8))
        v.memset(EPSC[:, :], EPS).then_inc(*did("eps.all"))

        dve.wait_ge(*when("silu.conds"))
        for u in range(16):
            s, k = divmod(u, 8)
            dve.wait_ge(mod_loaded[u % 4], 16 * (u // 4 + 1))
            if u and k:
                dve.wait_ge(mod_used, u + PRIME)
            if s and k == 0:
                dve.wait_ge(mod_summed, 1)
            for j, acc in enumerate((ACC, ACC1)):
                c = CVEC[:, 8 * j + k:8 * j + k + 1]
                if k:
                    ins = v.scalar_tensor_tensor(acc[:, :], MOD[u % 4][:, :], c, acc[:, :], mul, add)
                else:
                    ins = v.tensor_scalar(acc[:, :], MOD[u % 4][:, :], c, None, mul)
                ins.then_inc(*((mod_used, 1) if j else did(f"mod0.{u}")))
            if k == 7:
                dve.wait_ge(mod_summed, s + 1)
                for j in range(2):
                    ins = v.tensor_tensor(MODV0[:, 16 * j + 8 * s:16 * j + 8 * s + 8], bank(4, 16)[:, 8 * j:8 * j + 8], col("b_mod0", 8 * s, 8), add)
                    ins.then_inc(*((mod_taken, 1) if j else did(f"mod0_b.{s}")))
        dve.wait_ge(mod_taken, 2)
        for j in range(2):
            v.scalar_tensor_tensor(AFF[:, 8 * j:8 * j + 8], MODV0[:, 16 * j + 8:16 * j + 16], 1.0, col("g0", 0, 8), add, mul).then_inc(*did(f"gain0.{j}"))
        dve.wait_ge(*when("gain0.1"))
        dve.wait_ge(*when("n0_rs.all"))
        to_halves("n0", lambda k: X[:, k * S:(k + 1) * S], AFF[:, 0:8], MODV0[:, 0:8], NORM_T, Hl, Hh, S)
        dve.wait_ge(*when("nc_rs.all"))
        to_halves("nc", lambda k: CX[:, k, :], AFF[:, 8:16], MODV0[:, 16:24], CT_[:, :, :].rearrange("p k t -> p (k t)"), Cl, Ch, CTX)
        split_low(0, 0)
        for b in range(4):
            side(0, b)
        with led.loop(dve, "ev_in", EV_IN // 4 - 1) as i:
            for b in range(4):
                side(i + 1, b)

        def head_norm(j):
            kind, h = R1[j]
            dve.wait_ge(*when(f"hn_rs.{j}"))
            gain = col("q_g") if kind == "q" else col("k_g")
            if kind == "ck":
                v.scalar_tensor_tensor(KALL[:, h, 0:CTX], CKV[:, h, :], gain, RSS[RS_SLOT[j]][:, 0:CTX], mul, mul).then_inc(*did(f"hn_zn.{j}"))
            else:
                if j >= 4:
                    dve.wait_ge(*when(f"hn_rot.{j - 2}"))
                src = z(h) if kind == "k" else z(4 + h)
                v.scalar_tensor_tensor(ZN[j % 2][:, :], src, gain, RSS[RS_SLOT[j]][:, :], mul, mul).then_inc(*did(f"hn_zn.{j}"))

        def head_rope(j):
            kind, h = R1[j]
            if kind == "ck":
                return
            v.tensor_tensor(RA[j % 2][:, :], ZN[j % 2][:, :], COS0, mul).then_inc(*did(f"hn_ra.{j}"))
            dve.wait_ge(*when(f"hn_rot.{j}"))
            v.tensor_tensor(RB[j % 2][:, :], bank(2 + j % 2), SIN0, mul).then_inc(*did(f"hn_rb.{j}"))
            dve.wait_ge(*when(f"hn_rb.{j}"))
            dst = KALL[:, h, CTX:CTX + S] if kind == "k" else z(4 + h)
            v.tensor_tensor(dst, RA[j % 2][:, :], RB[j % 2][:, :], add).then_inc(*did(f"hn_out.{j}"))

        dve.wait_ge(*when("in_tabc.all"))
        dve.wait_ge(*when("ckv.3"))
        head_norm(0)
        for j in range(1, NC1):
            head_norm(j)
            if j > 2:
                dve.wait_ge(*when(f"hn_zn.{j - 1}"))
            head_rope(j - 1)
        head_rope(NC1 - 1)

        def normalise(n):
            dve.wait_ge(*when(f"prob.{n}"))
            v.reciprocal(STAT[:, 32 + n:33 + n], STAT[:, 32 + n:33 + n]).then_inc(*did(f"rsum.{n}"))
            dve.wait_ge(*when(f"rsum.{n}"))
            v.tensor_scalar(PR[n % 2][:, :], PR[n % 2][:, :], STAT[:, 32 + n:33 + n], None, mul).then_inc(*did(f"pnorm.{n}"))

        def head_gate(h):
            dve.wait_ge(*when(f"attn_o.{h}"))
            v.tensor_tensor(z(4 + h), bank(6 + h % 2), z(14 + h), mul).then_inc(*did(f"attn_y.{h}"))

        for n in range(24):
            if n:
                normalise(n - 1)
            dve.wait_ge(*when(f"score.{n}"))
            at0 = (n % 2) * 2 * S
            v.reduce_max(STAT[:, n:n + 1], PS[:, at0:at0 + 768], AX.X).then_inc(*did(f"rmax.{n}"))
            dve.wait_ge(*when(f"rmax.{n}"))
            v.tensor_scalar(STAT[:, n:n + 1], STAT[:, n:n + 1], -float(P) ** -0.5, None, mul).then_inc(*did(f"nmax.{n}"))
            if n >= 6 and n % 4 == 2:
                head_gate((n - 6) // 4)
        normalise(23)
        head_gate(5)
        for m in range(2):
            dve.wait_ge(*when(f"pool_y.{m}"))
            v.scalar_tensor_tensor(z(10 + m), bank(4 + m), col("pool_scale", m), z(12 + m), mul, mul).then_inc(*did(f"pool_out.{m}"))
        lows("mx1", [z(n) for n in (10, 11, 4, 5, 6, 7, 8, 9)])

        def residual(q0, q, i, b, gate0):
            dve.wait_ge(w_used, 4 * q + b + 1 + PRIME)
            n = i * 4 + b
            v.scalar_tensor_tensor(X[:, ds(n * S, S)], bank(b), MODV[:, ds(n + gate0, 1)], X[:, ds(n * S, S)], mul, add).then_inc(taken, 1)

        dve.wait_ge(mod_taken, 3)
        with led.loop(dve, "ev_out", EV_OUT // 4) as i:
            for b in range(4):
                side(i + 5, b)
                residual(5, i + 5, i, b, 0)

        dve.wait_ge(mod_taken, 6)
        v.scalar_tensor_tensor(AFF[:, 0:8], MODV[:, 16:24], 1.0, col("g1", 0, 8), add, mul).then_inc(*did("gain1.all"))
        dve.wait_ge(*when("gain1.all"))
        dve.wait_ge(*when("n1_rs.all"))
        to_halves("n1", lambda k: X[:, k * S:(k + 1) * S], AFF[:, 0:8], MODV[:, 8:16], NORM_T, Hl, Hh, S)
        with led.loop(dve, "od_in", OD_IN // 4) as i:
            for b in range(4):
                side(i + 7, b)

        def reduce_angle(tag, part, arg, tmp, out, shift=0.0):
            steps = [lambda: v.tensor_scalar(tmp, arg, 1.0 / (2 * np.pi), 0.25 if shift else 0.0, mul, add),
                     lambda: v.tensor_scalar(tmp, tmp, ROUND, -ROUND, add, add),
                     lambda: v.scalar_tensor_tensor(out, tmp, -TURN[0], arg, mul, add),
                     lambda: v.scalar_tensor_tensor(out, tmp, -TURN[1], out, mul, add),
                     lambda: v.scalar_tensor_tensor(out, tmp, -TURN[2], out, mul, add),
                     lambda: v.tensor_scalar(out, out, shift, PI_IN, add, ALU.min)]
            for k, step in enumerate(steps):
                step().then_inc(*did(f"{part}.{k}"))
                dve.wait_ge(*when(f"{part}.{k}"))
            v.tensor_scalar(out, out, -PI_IN, None, ALU.max).then_inc(*did(tag))

        for l in range(2):
            dve.wait_ge(*when(f"hy_hid.{l}"))
            if l:
                dve.wait_ge(*when("hy_sin.0"))
            v.tensor_scalar(ARG[0][:, :], bank(l, S, slice(0, 64)), col(f"hy_b{l + 1}", rows=64), col("freq", rows=64), add, mul).then_inc(*did(f"hy_pre.{l}"))
            dve.wait_ge(*when(f"hy_pre.{l}"))
            reduce_angle(f"hy_arg.{l}", f"hy_red{l}", ARG[0][:, :], ARG[1][:, :], ARG[2][:, :])

        for j in range(18):
            dve.wait_ge(*when(f"conv_mid.{j}"))
            v.scalar_tensor_tensor(z(j)[:, 1:S], z(j + 1)[:, 0:S - 1], col("conv_w", j), z(j)[:, 1:S], mul, add).then_inc(*did(f"conv1.{j}"))
            dve.wait_ge(*when(f"conv1.{j}"))
            v.scalar_tensor_tensor(z(j)[:, 0:S - 1], z(j + 1)[:, 1:S], col("conv_w", 36 + j), z(j)[:, 0:S - 1], mul, add).then_inc(*did(f"conv3.{j}"))

        for n, (g, o) in enumerate(STEPS):
            for j in range(4):
                for d in range(2):
                    dve.wait_ge(*when(f"hy_filt.{n}.{2 * j + d}"))
                    if d == 0:
                        dve.wait_ge(*when(f"hy_dec.{n}.{j}"))
                    if j or n:
                        prev = f"hy_sd.{n}.{j - 1}.1" if j else f"hz_fly.{n - 1}.7"
                        dve.wait_ge(*when(prev))
                    v.tensor_tensor(HH[d][:, :], bank(2 * j + d, G), DEC[:, 0:G], mul).then_inc(*did(f"hy_d{d}.{n}.{j}"))
                dve.wait_ge(*when(f"hy_d0.{n}.{j}"))
                dve.wait_ge(*when(f"hy_d1.{n}.{j}"))
                if n and j == 0:
                    dve.wait_ge(*when(f"hy_norm_mm.{n - 1}"))
                if n:
                    dve.wait_ge(*when(f"hk_mm.{n - 1}.1"))
                v.tensor_tensor(PM[:, 0, j, :], HH[0][:, :], HH[1][:, :], add).then_inc(*did(f"hy_sd.{n}.{j}.0"))
                v.tensor_tensor(PM[:, 1, j, :], HH[0][:, :], HH[1][:, :], sub).then_inc(*did(f"hy_sd.{n}.{j}.1"))
                if j == 0:
                    dve.wait_ge(*when(f"hy_sd.{n}.{j}.0"))
                    v.tensor_copy(PM[0:1, 0, 0, :], HH[0][0:1, :]).then_inc(*did(f"hy_lag0.{n}"))
                for d in range(2):
                    dve.wait_ge(*when(f"hy_mag.{n}.{j}.{d}"))
                    if j:
                        v.tensor_tensor(ABSA[:, 0:G], ABSA[:, 0:G], HT[:, d, :], add).then_inc(*did(f"hy_abs.{n}.{j}.{d}"))
                        dve.wait_ge(*when(f"hy_abs.{n}.{j}.{d}"))
                if j == 0:
                    v.tensor_tensor(ABSA[:, 0:G], HT[:, 0, :], HT[:, 1, :], add).then_inc(*did(f"hy_abs.{n}.{j}.1"))
                dve.wait_ge(*when(f"hy_abs.{n}.{j}.1"))
            dve.wait_ge(*when(f"hy_norm_mm.{n}"))
            if n:
                dve.wait_ge(*when(f"hy_out.{n - 1}.2"))
            v.tensor_scalar(HINV, bank(0, 3), 512.0, 512.0 * EPS, mul, add).then_inc(*did(f"hy_inv_a.{n}"))
            dve.wait_ge(*when(f"hy_inv_a.{n}"))
            v.reciprocal(HINV, HINV).then_inc(*did(f"hy_inv_b.{n}"))
            for kind, dst in (("hk", KSP), ("hz", GSP)):
                for ft in range(2):
                    for c in range(2):
                        dve.wait_ge(*when(f"{kind}_odd.{n}.{2 * ft + c}"))
                        if kind == "hz" and n and ft == 0 and c == 0:
                            dve.wait_ge(*when(f"hy_inv.{n - 1}.2"))
                        even, odd = bank(4 * ft + 2 * c, G), HT[:, c, :]
                        v.tensor_tensor(dst[:, ft, 2 * c, :], even, odd, add).then_inc(*did(f"{kind}_fly.{n}.{4 * ft + 2 * c}"))
                        if c == 0:
                            v.tensor_tensor(dst[:, ft, 1, :], even, odd, sub).then_inc(*did(f"{kind}_fly.{n}.{4 * ft + 1}"))
                        else:
                            v.scalar_tensor_tensor(dst[:, ft, 3, :], even, -1.0, odd, mul, add).then_inc(*did(f"{kind}_fly.{n}.{4 * ft + 3}"))
            for ft in range(2):
                K_, G_ = (lambda c: KSP[:, ft, c, :]), (lambda c: GSP[:, ft, c, :])
                tmp = [PM[:, 0, c, :] for c in range(4)] + [PM[:, 1, c, :] for c in range(4)]
                dve.wait_ge(*when(f"hz_fly.{n}.7"))
                dve.wait_ge(*when(f"hk_mm.{n}.1"))
                if ft:
                    dve.wait_ge(*when(f"hg_s.{n}.0.3"))
                for c in range(2):
                    for m, (a, b_) in enumerate(((0, 0), (2, 2), (0, 2), (2, 0))):
                        v.tensor_tensor(tmp[4 * c + m], K_(a + c), G_(b_ + c), mul).then_inc(*did(f"hg_m.{n}.{ft}.{c}.{m}"))
                dve.wait_ge(*when(f"hg_m.{n}.{ft}.1.3"))
                for c in range(2):
                    v.tensor_tensor(tmp[4 * c], tmp[4 * c], tmp[4 * c + 1], sub).then_inc(*did(f"hg_a.{n}.{ft}.{c}.0"))
                    v.tensor_tensor(tmp[4 * c + 2], tmp[4 * c + 2], tmp[4 * c + 3], add).then_inc(*did(f"hg_a.{n}.{ft}.{c}.1"))
                dve.wait_ge(*when(f"hg_a.{n}.{ft}.1.1"))
                v.tensor_tensor(G_(0), tmp[0], tmp[4], add).then_inc(*did(f"hg_s.{n}.{ft}.0"))
                v.tensor_tensor(G_(1), tmp[0], tmp[4], sub).then_inc(*did(f"hg_s.{n}.{ft}.1"))
                v.tensor_tensor(G_(2), tmp[2], tmp[6], sub).then_inc(*did(f"hg_s.{n}.{ft}.2"))
                v.tensor_tensor(G_(3), tmp[2], tmp[6], add).then_inc(*did(f"hg_s.{n}.{ft}.3"))
            for c in range(3):
                zt, gate = z(3 * g + c), z([X1_T, X2_T][o] + 3 * g + c)
                dve.wait_ge(*when(f"hy_inv.{n}.{c}"))
                if c == 0:
                    dve.wait_ge(*when(f"hg_s.{n}.1.3"))
                y = PMY[c % 2]
                v.tensor_scalar(y.rearrange("p (m e) -> p e m", e=2), bank(c).rearrange("p (e m) -> p e m", e=2), AFF[:, c:c + 1], None, mul).then_inc(*did(f"hy_y.{n}.{c}.0"))
                dve.wait_ge(*when(f"hy_y.{n}.{c}.0"))
                v.scalar_tensor_tensor(y, zt, col("skip", 6 * o + 3 * g + c), y, mul, add).then_inc(*did(f"hy_y.{n}.{c}.1"))
                dve.wait_ge(*when(f"hy_y.{n}.{c}.1"))
                if o == 0:
                    v.tensor_tensor(zt, y, gate, mul).then_inc(*did(f"hy_out.{n}.{c}"))
                else:
                    v.tensor_tensor(y, y, gate, mul).then_inc(*did(f"hy_y.{n}.{c}.2"))
                    dve.wait_ge(*when(f"hy_y.{n}.{c}.2"))
                    v.tensor_tensor(zt, y, z(HG_T + 1 + 3 * g + c), mul).then_inc(*did(f"hy_out.{n}.{c}"))
        for m in range(2):
            dve.wait_ge(*when(f"fn_y.{m}"))
            v.tensor_tensor(z(FN_T + 1 + m), bank(6 + m), z(FG_T + 1 + m), mul).then_inc(*did(f"fn_out.{m}"))
        lows("mx2", [z(k) if k < 6 else z(FN_T + 1 + k - 6) for k in range(KT)])
        with led.loop(dve, "od_out", OD_OUT // 4) as i:
            for b in range(4):
                side(i + 14, b)
                residual(14, i + 14, i, b, 24)

        dve.wait_ge(*when("nf_rs.all"))
        for k in range(KT):
            v.scalar_tensor_tensor(X[:, k * S:(k + 1) * S], X[:, k * S:(k + 1) * S], col("final_g", k), RS[:, :], mul, mul).then_inc(*did(f"nf_x.{k}"))
        dve.wait_ge(*when("in_tab2.pos"))
        v.tensor_copy(NORM_T[:, 0:S], POSI[:, :]).then_inc(*did("rot_pos.f"))
        dve.wait_ge(*when("rot_pos.f"))
        v.tensor_scalar(NORM_T[:, S:2 * S], NORM_T[:, 0:S], col("inv_freq"), None, mul).then_inc(*did("rot_pos.angle"))
        dve.wait_ge(*when("rot_pos.angle"))
        reduce_angle("rot_arg.0", "rot_red0", NORM_T[:, S:2 * S], NORM_T[:, 2 * S:3 * S], RT[0][:, :])
        reduce_angle("rot_arg.1", "rot_red1", NORM_T[:, S:2 * S], NORM_T[:, 3 * S:4 * S], RT[1][:, :], float(np.float32(np.pi / 2)))

        with led.loop(dve, "layers", LAYERS) as lay:
            Q = lay * (PER_LAYER // 4) + T_LAYERS // 4
            dve.wait_ge(*when("nf_x.7"))
            dve.wait_ge(*when("y2_x.7", back="layers"))
            v.tensor_copy(LM[:, :], MODV[:, ds(lay * 48 + 32, 48)]).then_inc(*did("layer_cols.mod"))
            v.tensor_copy(LG[:, :], COL[:, ds(lay * 32 + COLS["g2"][0], 32)]).then_inc(*did("layer_cols.gain"))
            dve.wait_ge(*when("layer_cols.gain"))
            for c, (m, how) in enumerate(((8, True), (16, False), (32, True), (40, False))):
                g = LG[:, 8 * c:8 * c + 8]
                if how:
                    v.scalar_tensor_tensor(AF2[:, 8 * c:8 * c + 8], LM[:, m:m + 8], 1.0, g, add, mul).then_inc(*did(f"layer_aff.{c}"))
                else:
                    v.tensor_tensor(AF2[:, 8 * c:8 * c + 8], LM[:, m:m + 8], g, mul).then_inc(*did(f"layer_aff.{c}"))
            dve.wait_ge(*when("layer_aff.3"))
            dve.wait_ge(*when("h1_rs.all"))
            to_halves("h1", lambda k: X[:, k * S:(k + 1) * S], AF2[:, 0:8], LM[:, 0:8], NORM_T, Hl, Hh, S)
            with led.loop(dve, "mx_in", 5) as i:
                for b in range(4):
                    next_tile(i + Q, b)
            next_tile(Q + 5, 0)
            dve.wait_ge(w_loaded[1], 16 * (Q + 5) + 16)
            dve.wait_ge(w_low, 4 * Q + 22 + PRIME)
            for c in range(2):
                v.tensor_copy(PAR[:, c * D:(c + 1) * D], RAW[1][:, c, :]).then_inc(w_low, 1)
            dve.wait_ge(w_low, 4 * Q + 24 + PRIME)
            dve.wait_ge(taken, 4 * Q + 24 + PRIME)
            split_low(Q + 6, 0)

            for m in range(2):
                dve.wait_ge(*when(f"gm_mean.{m}"))
                v.scalar_tensor_tensor(MO[:, m, :], bank(m), -1.0 / 64, z(19 + m), mul, add).then_inc(*did(f"gm_c.{m}"))
            for g in range(4):
                v.tensor_tensor(par("ws", P * g, P), par("ws", P * g, P), TRIL, mul).then_inc(*did(f"gm_w.{g}"))
            for c in range(2):
                v.tensor_tensor(TP[:, 16 * c:16 * c + 16, :], z(8)[:, 16 * c:16 * c + 496].rearrange("p (n j) -> p j n", j=16),
                                par("pos", 16 * c, 16).rearrange("p (j o) -> p j o", o=1).to_broadcast([P, 16, 31]), add).then_inc(*did("cmp_in.all" if c else "cmp_in.0"))
            for m in range(2):
                v.tensor_tensor(z(4 + m), z(4 + m), z(m), mul).then_inc(*did(f"conv_z.{m}"))
            for m in range(2):
                dve.wait_ge(*when(f"conv_z.{m}"))
                v.tensor_scalar(AO[:, m, :], z(4 + m), par("conv", 4 + m), None, mul).then_inc(*did(f"conv_c.{m}"))
            for m in range(2):
                dve.wait_ge(*when(f"conv_c.{m}"))
                v.scalar_tensor_tensor(AO[:, m, 1:S], z(4 + m)[:, 0:S - 1], par("conv", 2 + m), AO[:, m, 1:S], mul, add).then_inc(*did(f"conv_d.{m}"))
            for m in range(2):
                dve.wait_ge(*when(f"conv_d.{m}"))
                v.scalar_tensor_tensor(AO[:, m, 2:S], z(4 + m)[:, 0:S - 2], par("conv", m), AO[:, m, 2:S], mul, add).then_inc(*did(f"conv_e.{m}"))
            for m in range(2):
                dve.wait_ge(*when(f"conv_e.{m}"))
                v.tensor_tensor(AO[:, m, :], AO[:, m, :], z(2 + m), mul).then_inc(*did("conv_y.all" if m else "conv_y.0"))

            for c in range(4):
                if c < 2:
                    v.tensor_tensor(RT[0][:, :], z(6 + c), COS2, mul).then_inc(*did(f"rp_a.{c}"))
                else:
                    dve.wait_ge(*when(f"rp_dup.{c}"))
                    v.tensor_tensor(RT[0][:, :], bank(5), COS2, mul).then_inc(*did(f"rp_a.{c}"))
                dve.wait_ge(*when(f"rp_rot.{c}"))
                v.tensor_tensor(RT[1][:, :], bank(ROT_BANKS[c]), SIN2, mul).then_inc(*did(f"rp_b.{c}"))
                dve.wait_ge(*when(f"rp_b.{c}"))
                dst = QR[:, c, :] if c < 2 else [KS_, KW_][c - 2][:, :]
                v.tensor_tensor(dst, RT[0][:, :], RT[1][:, :], add).then_inc(*did(f"rp.{c}"))
                dve.wait_ge(*when(f"rp.{c}"))

            for m in range(2):
                dve.wait_ge(*when(f"gm_rs.{m}"))
                v.tensor_tensor(MO[:, m, :], MO[:, m, :], P2[m][:, :], mul).then_inc(*did(f"gm_n.{m}"))
            for m in range(2):
                dve.wait_ge(*when(f"gm_mm.{m}"))
                for j in range(4):
                    v.tensor_tensor(MO[:, m, j * P:(j + 1) * P], bank(2 + m)[:, j * P:(j + 1) * P], par("gm_b", m * P, P), add).then_inc(*did(f"gm_t.{4 * m + j}"))
            for m in range(2):
                dve.wait_ge(*when(f"gm_t.{4 * m + 3}"))
                v.tensor_tensor(MO[:, m, :], MO[:, m, :], z(17 + m), mul).then_inc(*did("gm_y.1" if m else "gm_y.0"))

            dve.wait_ge(*when("gla_pre.all"))
            v.tensor_scalar(GE[0][:, :], bank(7), par("gate_b"), None, add).then_inc(*did("gla_x.all"))
            dve.wait_ge(*when("gla_x.all"))
            v.tensor_scalar(GM[:, :], GE[0][:, :], 0.0, None, ALU.min).then_inc(*did("gla_min.all"))

            def decay_sums():
                dve.wait_ge(*when("gla_ln.all"))
                dve.wait_ge(*when("gla_min.all"))
                v.tensor_tensor(GM[:, :], GM[:, :], GE[0][:, :], sub).then_inc(*did("gla_log.all"))
                dve.wait_ge(*when("gla_log.all"))
                v.tensor_tensor_scan(GB[:, :], SCANM, GM[:, :], 0.0, mul, add).then_inc(*did("gla_b.all"))
                dve.wait_ge(*when("gla_b.all"))
                B3 = GB[:, :].rearrange("p (c t) -> p c t", t=64)
                mid, last = (B3[:, :, k:k + 1].to_broadcast([P, 8, 64]) for k in (32, 63))
                e3 = [GE[c][:, :].rearrange("p (c t) -> p c t", t=64) for c in range(3)]
                v.tensor_tensor(e3[0], B3, mid, sub).then_inc(*did("gla_d.0"))
                v.tensor_tensor(e3[1], mid, B3, sub).then_inc(*did("gla_d.1"))
                v.tensor_tensor(e3[2], last, B3, sub).then_inc(*did("gla_d.2"))

            def decay_products():
                for c, (n, scale) in enumerate(((11, 32 ** -0.5), (12, 1.0), (12, 1.0), (11, 32 ** -0.5))):
                    dve.wait_ge(*when(f"gla_e.{c}"))
                    v.scalar_tensor_tensor(GE[c][:, :], z(n), scale, GE[c][:, :], mul, mul).then_inc(*did(f"gla_m.{c}"))

            def normalise2(n):
                h, i, br = ITEMS[n]
                st = ST2[n % 4]
                dve.wait_ge(*when(f"prob2.{n}"))
                v.reciprocal(st[:, 2:3], st[:, 1:2]).then_inc(*did(f"rsum2.{n}"))
                gate = GT[:, i, 3 * h + (br + 1) % 3:3 * h + (br + 1) % 3 + 1]
                dve.wait_ge(*when(f"rsum2.{n}"))
                if br == 2 and i == 0:
                    v.tensor_scalar(st[:, 3:4], st[:, 2:3], gate, col("row_valid", 0), mul, mul).then_inc(*did(f"rfac2.{n}"))
                else:
                    v.tensor_scalar(st[:, 3:4], st[:, 2:3], gate, None, mul).then_inc(*did(f"rfac2.{n}"))
                dve.wait_ge(*when(f"rfac2.{n}"))
                v.tensor_scalar(P2[n % 4][:, 0:WIDTH[n]], P2[n % 4][:, 0:WIDTH[n]], st[:, 3:4], None, mul).then_inc(*did(f"pnorm2.{n}"))

            dve.wait_ge(*when("gates.all"))
            for n, (h, i, br) in enumerate(ITEMS):
                w, st = WIDTH[n], ST2[n % 4]
                dve.wait_ge(*when(f"score2.{n}"))
                part, bias = (bank(SCORE_BANKS[n % 4], 31), CMPB[:, 32 * i:32 * i + 31]) if br == 2 else (bank(SCORE_BANKS[n % 4])[:, w - P:w], BIAS)
                v.tensor_tensor(part, part, bias, add).then_inc(*did(f"mask2.{n}"))
                dve.wait_ge(*when(f"mask2.{n}"))
                v.reduce_max(st[:, 0:1], bank(SCORE_BANKS[n % 4], w), AX.X).then_inc(*did(f"rmax2.{n}"))
                dve.wait_ge(*when(f"rmax2.{n}"))
                v.tensor_scalar(st[:, 0:1], st[:, 0:1], -0.125, None, mul).then_inc(*did(f"nmax2.{n}"))
                if n:
                    normalise2(n - 1)
                if n == 8:
                    decay_sums()
                if n == 16:
                    decay_products()
            normalise2(len(ITEMS) - 1)

            dve.wait_ge(*when("gla_zero.1"))
            dve.sem_inc(passed, 1)
            for h in range(4):
                dve.wait_ge(*when("in_tab2.all"))
                dve.wait_ge(*when(f"gla_att_mm.{h}"))
                dve.sem_inc(passed, 1)
                v.copy_predicated(GA[:, h, :], GMASK[:, :], bank(h, S, slice(0, 64))).then_inc(*did(f"gla_att.{h}"))
            for c in range(7):
                dve.wait_ge(*when(f"gla_kv.{c}"))
                if c:
                    dve.wait_ge(*when(f"gla_st.{c - 1}.3"))
                else:
                    dve.wait_ge(*when("gla_decay.all"))
                for h in range(4):
                    rows, cols_ = slice(32 * h, 32 * h + 32), slice(64 * h, 64 * h + 64)
                    if c:
                        v.scalar_tensor_tensor(GS[rows, c + 1, cols_], GS[rows, c, cols_], DECY[rows, c:c + 1], bank(4 + c % 2)[rows, cols_], mul, add).then_inc(*did(f"gla_st.{c}.{h}"))
                    else:
                        v.tensor_copy(GS[rows, 1, cols_], bank(4)[rows, cols_]).then_inc(*did(f"gla_st.{c}.{h}"))
            for m in range(2):
                dve.wait_ge(*when(f"gla_rs.{m}"))
                v.tensor_tensor(GO[:, m, :], GO[:, m, :], GR[m][:, :], mul).then_inc(*did(f"gla_n.{m}"))
                dve.wait_ge(*when(f"gla_n.{m}"))
                v.tensor_tensor(GO[:, m, :], GO[:, m, :], z(15 + m), mul).then_inc(*did(f"gla_y.{m}"))

            for g in range(4):
                dve.wait_ge(*when(f"gr_rs.{g}"))
                for m in range(2):
                    src = (AO, NO, GO, MO)[g][:, m, :]
                    v.scalar_tensor_tensor(z(2 * g + m), src, par("gain", 2 * g + m), GR[g][:, :], mul, mul).then_inc(*did(f"gr_n.{2 * g + m}"))
            lows("mx3", [z(k) for k in range(KT)])
            zero_squares("y1")
            with led.loop(dve, "mx_out", 2) as i:
                for b in range(4):
                    next_tile(i + Q + 6, b)

            def add_branch(tag, gain):
                dve.wait_ge(*when(f"{tag}_rs.all"))
                for k in range(KT + 1):
                    if k < KT:
                        v.scalar_tensor_tensor(Y[:, k * S:(k + 1) * S], Y[:, k * S:(k + 1) * S], AF2[:, gain + k:gain + k + 1], RS[:, :], mul, mul).then_inc(*did(f"{tag}_t.{k}"))
                    if k:
                        dve.wait_ge(*when(f"{tag}_t.{k - 1}"))
                        v.tensor_tensor(X[:, (k - 1) * S:k * S], X[:, (k - 1) * S:k * S], Y[:, (k - 1) * S:k * S], add).then_inc(*did(f"{tag}_x.{k - 1}"))

            add_branch("y1", 8)
            dve.wait_ge(*when("h2_rs.all"))
            to_halves("h2", lambda k: X[:, k * S:(k + 1) * S], AF2[:, 16:24], LM[:, 24:32], NORM_T, Hl, Hh, S)
            for a in range(2):
                q0 = Q + 8 + 8 * a
                with led.loop(dve, f"up{a}", 4) as i:
                    for b in range(4):
                        next_tile(i + q0, b)
                        hs = (lambda H: H[:, ds(i * 4 + b, 1), :].rearrange("p o t -> p (o t)"))
                        dve.wait_ge(*when(f"relu{a}.{b}"))
                        v.tensor_copy(hs(HIDh), SQ[b % 2][:, :]).then_inc(*did(f"hid{a}_a.{b}"))
                        dve.wait_ge(*when(f"hid{a}_a.{b}"))
                        v.tensor_tensor(hs(HIDl), SQ[b % 2][:, :], hs(HIDh).bitcast(f32), sub).then_inc(*did(f"hid{a}_b.{b}"))
                if a:
                    dve.wait_ge(*when("hid1_b.3"))
                    zero_squares("y2")
                with led.loop(dve, f"down{a}", 4) as i:
                    for b in range(4):
                        next_tile(i + q0 + 4, b)
                        if b % 2 and a == 1:
                            dve.wait_ge(w_used, 4 * q0 + 4 * i + 16 + b + 1 + PRIME)
                            y = Y[:, ds((i * 2 + b // 2) * S, S)]
                            v.tensor_tensor(y, y, bank(b - 1), add).then_inc(taken, 2)
            add_branch("y2", 24)

    @block.tensor
    def _(pe):
        led.engine = "tensor"
        mm = nc.tensor.matmul

        def tile(q, b, H, L, ready=None, n=S, even=None):
            pe.wait_ge(w_low, 4 * q + b + 1 + PRIME)
            start, stop = even in (None, True), even in (None, False)
            if start:
                pe.wait_ge(taken, 4 * q + b - 3 + PRIME)
            out = bank(b if even is None else b & 2, n)
            for k in range(KT):
                if ready:
                    pe.wait_ge(*when(f"{ready}.{k}"))
                kk = k if even in (None, True) else k + KT
                mm(out, WH[b % 2][:, k, :], H[:, kk, :], start=start and k == 0, stop=False)
                mm(out, WH[b % 2][:, k, :], L[:, kk, :], start=False, stop=False)
                last = mm(out, WL[b % 2][:, k, :], H[:, kk, :], start=False, stop=stop and k == KT - 1)
            return last

        def mod_sum(q):
            pe.wait_ge(mod_used, 8 * q + 24 + PRIME)
            pe.wait_ge(mod_taken, q + 2)
            for n in range(8):
                last = mm(bank(4)[:, n:n + 1], ACC[:, n * P:(n + 1) * P], ONES[:, 0:1], start=True, stop=True)
            last.then_inc(mod_summed, 1)

        def body(q, b, ready, **more):
            if b == 3:
                mod_sum(q)
            tile(q, b, Hh, Hl, ready if b == 0 else None, **more).then_inc(w_used, 1)

        def sums(tag, b, n):
            for k in range(KT):
                pe.wait_ge(*when(f"{tag}_sq.{k}"))
                mm(bank(b, n), ONES, SQ[k % 2][:, 0:n], start=k == 0, stop=k == KT - 1).then_inc(*did(f"{tag}_ss.{k}"))

        def open_squares(tag):
            pe.wait_ge(*when(f"{tag}_zero.1"))
            mm(bank(5), ONES, SQ[1][:, :], start=True, stop=False).then_inc(*did(f"{tag}_open.all"))

        def add_squares(tag, b, slot, loop=None):
            pe.wait_ge(*when(f"{tag}_tile.{b}", back=loop))
            mm(bank(5), ONES, SQ[slot][:, :], start=False, stop=False).then_inc(*did(f"{tag}_part.{b}"))

        def last_squares(tag, b):
            pe.wait_ge(*when(f"{tag}_tile.{b}"))
            mm(bank(5), ONES, SQ[1][:, :], start=False, stop=True).then_inc(*did(f"{tag}_ss.7"))

        pe.sem_inc(w_used, PRIME)
        sums("n0", 5, S)
        for s in range(2):
            pe.wait_ge(mod_used, 8 * s + 8 + PRIME)
            if s:
                pe.wait_ge(mod_taken, 1)
            for j, acc in enumerate((ACC, ACC1)):
                for n in range(8):
                    last = mm(bank(4)[:, 8 * j + n:8 * j + n + 1], acc[:, n * P:(n + 1) * P], ONES[:, 0:1], start=True, stop=True)
            last.then_inc(mod_summed, 1)
        sums("nc", 6, CTX)

        for b in range(4):
            body(0, b, "n0_lo")
            if b >= 2:
                pe.wait_ge(*when(f"ckv.{b - 2}"))
            for k in range(KT):
                if b == 0:
                    pe.wait_ge(*when(f"nc_lo.{k}"))
                mm(bank(5 + b % 2, CTX), WH[b % 2][:, k, :], Ch[:, k, :], start=k == 0, stop=False)
                mm(bank(5 + b % 2, CTX), WH[b % 2][:, k, :], Cl[:, k, :], start=False, stop=False)
                last = mm(bank(5 + b % 2, CTX), WL[b % 2][:, k, :], Ch[:, k, :], start=False, stop=k == KT - 1)
            last.then_inc(*did(f"ckv_mm.{b}"))
        with led.loop(pe, "ev_in", EV_IN // 4 - 1) as i:
            for b in range(4):
                body(i + 1, b, "n0_lo")

        pe.wait_ge(taken, EV_IN + PRIME)

        def rot(j):
            if R1[j][0] != "ck":
                pe.wait_ge(*when(f"hn_zn.{j}"))
                if j >= 4:
                    pe.wait_ge(*when(f"hn_rb.{j - 2}"))
                mm(bank(2 + j % 2), ROPE0, ZN[j % 2][:, :], start=True, stop=True).then_inc(*did(f"hn_rot.{j}"))

        for batch in BATCHES:
            for j in batch:
                n = CTX if R1[j][0] == "ck" else S
                pe.wait_ge(*when(f"hn_sq.{j}"))
                if j >= 2:
                    pe.wait_ge(*when(f"hn_ln.{j - 2}"))
                mm(bank(j % 2, n), ONES, SQ[j % 2][:, 0:n], start=True, stop=True).then_inc(*did(f"hn_ss.{j}"))
            for j in batch:
                rot(j)
        for j in range(6):
            if j >= 3:
                pe.wait_ge(*when(f"vt.{j - 3}"))
            for m in range(2):
                src = CKV[:, 2 + m, j * P:(j + 1) * P] if j < 2 else z(2 + m)[:, (j - 2) * P:(j - 1) * P]
                last = nc.tensor.transpose(bank(4 + j % 3)[:, m * P:(m + 1) * P], src, IDENT)
            last.then_inc(*did(f"vt_mm.{j}"))

        def transpose_probs(n):
            pe.wait_ge(*when(f"pnorm.{n}"))
            pe.wait_ge(*when(f"pt.{n - 1}" if n else "vt.5"))
            for j in range(6):
                last = nc.tensor.transpose(PS[:, 4 * S + j * P:4 * S + (j + 1) * P], PR[n % 2][:, j * P:(j + 1) * P], IDENT)
            last.then_inc(*did(f"pt_mm.{n}"))
            if n % 4 == 3:
                h = n // 4
                pe.wait_ge(*when(f"pt.{n}"))
                if h >= 2:
                    pe.wait_ge(*when(f"attn_y.{h - 2}"))
                for j in range(6):
                    last = mm(bank(6 + h % 2), VT[:, j, (h // 3) * P:(h // 3 + 1) * P], PT[h % 2][:, j, :], start=j == 0, stop=j == 5)
                last.then_inc(*did(f"attn_o.{h}"))

        pe.wait_ge(*when("hn_out.9"))
        for n in range(24):
            h, i = divmod(n, 4)
            if n >= 2:
                pe.wait_ge(*when(f"prob.{n - 2}"))
            at0 = (n % 2) * 2 * S
            q_ = z(4 + h)[:, i * P:(i + 1) * P]
            mm(PS[:, at0:at0 + S], q_, KALL[:, h // 3, 0:S], start=True, stop=True)
            mm(PS[:, at0 + S:at0 + 768], q_, KALL[:, h // 3, S:768], start=True, stop=True).then_inc(*did(f"score.{n}"))
            if n:
                transpose_probs(n - 1)
        transpose_probs(23)
        pe.wait_ge(*when("pool_d.all"))
        pe.wait_ge(*when("pt.23"))
        for m in range(2):
            mm(bank(4 + m), POOLW[:, m * P:(m + 1) * P], z(10 + m), start=True, stop=True).then_inc(*did(f"pool_y.{m}"))
        pe.wait_ge(*when("attn_y.5"))
        with led.loop(pe, "ev_out", EV_OUT // 4) as i:
            for b in range(4):
                body(i + 5, b, "mx1_lo")
        sums("n1", 5, S)
        with led.loop(pe, "od_in", OD_IN // 4) as i:
            for b in range(4):
                body(i + 7, b, "n1_lo")

        pe.wait_ge(taken, T_OD_OUT + PRIME)
        pe.wait_ge(*when("in_hy2.all"))
        mm(bank(0, S, slice(0, 64)), HW12[0:33, 0, :], EMB[:, :], start=True, stop=True).then_inc(*did("hy_hid.0"))
        pe.wait_ge(*when("hy_sin.0"))
        mm(bank(1, S, slice(0, 64)), HW12[:, 1, :], EMB2[:, :], start=True, stop=True).then_inc(*did("hy_hid.1"))
        pe.wait_ge(*when("hy_sin.1"))
        for n, (g, o) in enumerate(STEPS):
            pe.wait_ge(*when(f"in_w3.{n}"))
            if n:
                pe.wait_ge(*when(f"hz_fly.{n - 1}.7"))
                pe.wait_ge(*when(f"hy_out.{n - 1}.2"))
            for j in range(4):
                for d in range(2):
                    mm(bank(2 * j + d, G), HDN[:, j * P:(j + 1) * P], W3[:, d * G:(d + 1) * G], start=True, stop=True).then_inc(*did(f"hy_filt.{n}.{2 * j + d}"))
            pe.wait_ge(*when(f"hy_abs.{n}.3.1"))
            for c in range(3):
                last = mm(bank(0)[:, c:c + 1], ABSA[:, c * P:(c + 1) * P], ONES[:, 0:1], start=True, stop=True)
            last.then_inc(*did(f"hy_norm_mm.{n}"))
            pe.wait_ge(*when(f"hy_inv_a.{n}"))
            for kind in ("hk", "hz"):
                if kind == "hz":
                    for j in range(4):
                        pe.wait_ge(*when(f"hk_fly.{n}.7"))
                        for c in range(3):
                            src = z(3 * g + c).rearrange("p (m e) -> p e m", e=2)[:, j // 2, (j % 2) * P:(j % 2 + 1) * P]
                            last = nc.tensor.transpose(bank(4 + j)[:, c * P:(c + 1) * P], src, IDENT)
                        last.then_inc(*did(f"hy_zt_mm.{n}.{j}"))
                    pe.wait_ge(*when(f"hy_zt.{n}.3"))
                for ft in range(2):
                    for c in range(2):
                        for e in range(2):
                            for t in range(2):
                                rhs = PM[:, c, 2 * e + t, :] if kind == "hk" else ZT[:, 2 * e + t, :]
                                last = mm(bank(4 * ft + 2 * c + e, G), FWD[:, e, c, t, ft * P:(ft + 1) * P], rhs, start=t == 0, stop=t == 1)
                    last.then_inc(*did(f"{kind}_mm.{n}.{ft}"))
            pe.wait_ge(*when(f"hg_s.{n}.1.3"))
            for c in range(3):
                for e in range(2):
                    k = 0
                    for s_ in range(2):
                        for ft in range(2):
                            last = mm(bank(c)[:, e * 256:(e + 1) * 256], GSP[:, ft, 2 * s_ + e, c * P:(c + 1) * P], INV[:, e, s_, ft, :], start=k == 0, stop=k == 3)
                            k += 1
                last.then_inc(*did(f"hy_inv.{n}.{c}"))

        pe.wait_ge(*when("in_fn.all"))
        for j in range(4):
            for k in range(2):
                last = mm(bank(j), z(FN_T + 1 + k)[:, j * P:(j + 1) * P], CSC[:, k, :], start=k == 0, stop=k == 1)
            last.then_inc(*did(f"fn_a.{j}"))
        for m in range(2):
            for j in range(4):
                pe.wait_ge(*when(f"fn_ab.{j}"))
                mm(bank(4 + m), AB[:, j, m * P:(m + 1) * P], CTT[:, j, :], start=j == 0, stop=False)
                last = mm(bank(4 + m), AB[:, j, 2 * P + m * P:2 * P + (m + 1) * P], NST[:, j, :], start=False, stop=j == 3)
            last.then_inc(*did(f"fn_b.{m}"))
        for m in range(2):
            for k in range(2):
                pe.wait_ge(*when(f"fn_u2.{k}"))
                last = mm(bank(6 + m), FNW[:, k, m * P:(m + 1) * P], U2[:, k, :], start=k == 0, stop=k == 1)
            last.then_inc(*did(f"fn_y.{m}"))
        with led.loop(pe, "od_out", OD_OUT // 4) as i:
            for b in range(4):
                body(i + 14, b, "mx2_lo")
        sums("nf", 5, S)

        with led.loop(pe, "layers", LAYERS) as lay:
            Q = lay * (PER_LAYER // 4) + T_LAYERS // 4
            sums("h1", 5, S)
            with led.loop(pe, "mx_in", 5) as i:
                for b in range(4):
                    tile(i + Q, b, Hh, Hl, "h1_lo" if b == 0 else None).then_inc(w_used, 1)
            for b in range(2):
                tile(Q + 5, b, Hh, Hl).then_inc(w_used, 1)
            pe.wait_ge(w_used, 4 * Q + 22 + PRIME)
            pe.sem_inc(w_used, 2)
            pe.wait_ge(taken, 4 * Q + 24 + PRIME)

            for m in range(2):
                mm(bank(m), HALVES, z(19 + m), start=True, stop=True).then_inc(*did(f"gm_mean.{m}"))
            pe.wait_ge(*when("in_cw1.all"))
            pe.wait_ge(*when("cmp_in.all"))

            for j in range(32):
                for c in range(2):
                    rows = slice(64 * c, 64 * c + 64)
                    done = mm(bank((7, 4)[c], 31), CW1[rows, j * P:(j + 1) * P], TP[rows, j, :], start=j == 0, stop=j == 31)
                    if j == 31:
                        done.then_inc(*did(f"cmp_h.{c}"))
                if j == 8:
                    for m in range(2):
                        pe.wait_ge(*when(f"gm_sq.{m}"))
                        mm(bank(2 + m), HALVES, SQ[m][:, :], start=True, stop=True).then_inc(*did(f"gm_var.{m}"))
            for c in range(4):
                if c >= 2:
                    pe.wait_ge(*when(f"rp_b.{c - 1}"))
                    mm(bank(5), DUPK, z(7 + c), start=True, stop=True).then_inc(*did(f"rp_dup.{c}"))
                mm(bank(ROT_BANKS[c]), ROT2 if c < 2 else DUPR, z((6 if c < 2 else 7) + c), start=True, stop=True).then_inc(*did(f"rp_rot.{c}"))
            pe.wait_ge(*when("cmp_act.1"))
            mm(bank(2, 31), par("w2k", 0, P), HC[:, 0, 0:31], start=True, stop=True).then_inc(*did("cmp_kv.0"))
            mm(bank(3, P, slice(0, 31)), HC[:, 1, 0:31], par("w2v", 0, P), start=True, stop=True).then_inc(*did("cmp_kv.1"))
            for j in range(4):
                last = nc.tensor.transpose(bank(4)[:, j * P:(j + 1) * P], z(21)[:, j * P:(j + 1) * P], IDENT)
            last.then_inc(*did("gate_t.all"))
            mm(bank(7), par("gate_w", 0, P, slice(0, 16)), z(21)[0:16, :], start=True, stop=True).then_inc(*did("gla_pre.all"))
            pe.wait_ge(*when("rp_b.3"))
            for c in range(2):
                for j in range(4):
                    last = mm(bank(5 + c)[:, j * P:(j + 1) * P], z(9 + c)[64:P, j * P:(j + 1) * P], DUPV[64:P, :], start=True, stop=True)
                last.then_inc(*did(f"v_tok_mm.{c}"))
            pe.wait_ge(*when("gm_n.1"))
            for j in range(4):
                for m in range(2):
                    last = nc.tensor.transpose(bank(j // 2)[:, (j % 2 * 2 + m) * P:(j % 2 * 2 + m + 1) * P], MO[:, m, j * P:(j + 1) * P], IDENT)
                last.then_inc(*did(f"gm_vt_mm.{j}"))
            pe.wait_ge(*when("gm_vt.1"))
            for m in range(2):
                for gpar in range(2):
                    rows = slice(64 * gpar, 64 * gpar + 64)
                    for j in range(4):
                        g = 2 * m + gpar
                        last = mm(bank(2 + m)[rows, j * P:(j + 1) * P], GMV[:, j, 64 * g:64 * g + 64], par("ws", P * g, P), start=True, stop=True)
                last.then_inc(*did(f"gm_mm.{m}"))

            def weigh(n):
                h, i, br = ITEMS[n]
                pe.wait_ge(*when(f"pnorm2.{n}"))
                if n >= 2:
                    pe.wait_ge(*when(f"p2t.{n - 2}"))
                if br == 2:
                    nc.tensor.transpose(bank(3 + n % 2, P, slice(0, 31)), P2[n % 4][:, 0:31], IDENT).then_inc(*did(f"p2t_mm.{n}"))
                else:
                    for j in range(i + 1):
                        last = nc.tensor.transpose(bank(3 + n % 2)[:, j * P:(j + 1) * P], P2[n % 4][:, j * P:(j + 1) * P], IDENT)
                    last.then_inc(*did(f"p2t_mm.{n}"))

            def values(n):
                h, i, br = ITEMS[n]
                pe.wait_ge(*when(f"p2t.{n}"))
                if h >= 2 and i == 0 and br == 0:
                    pe.wait_ge(*when(f"nsa_o.{h - 2}"))
                out = bank(5 + h % 2)[:, i * P:(i + 1) * P]
                if br == 2:
                    last = mm(out, VC[0:31, :], PT2[n % 2][0:31, 0, :], start=False, stop=True)
                else:
                    for j in range(i + 1):
                        last = mm(out, [VS_, VW_][br][:, j, :], PT2[n % 2][:, j, :], start=br == 0 and j == 0, stop=False)
                last.then_inc(*did(f"p2v.{n}"))

            pe.wait_ge(*when("rp.3"))
            pe.wait_ge(*when("v_tok.1"))
            pe.wait_ge(*when("cmp_v.all"))
            for n, (h, i, br) in enumerate(ITEMS):
                rows = slice(64 * (h % 2), 64 * (h % 2) + 64)
                if n >= 4:
                    pe.wait_ge(*when(f"prob2.{n - 4}"))
                elif n == 2:
                    pe.wait_ge(*when("gm_t.3"))
                elif n == 3:
                    pe.wait_ge(*when("gla_x.all"))
                if br == 2:
                    mm(bank(SCORE_BANKS[n % 4], 31), z(6 + h // 2)[rows, i * P:(i + 1) * P], KC[rows, 0:31], start=True, stop=True).then_inc(*did(f"score2.{n}"))
                else:
                    mm(bank(SCORE_BANKS[n % 4], WIDTH[n]), QR[rows, h // 2, i * P:(i + 1) * P], [KS_, KW_][br][rows, 0:WIDTH[n]], start=True, stop=True).then_inc(*did(f"score2.{n}"))
                if n >= 2:
                    weigh(n - 2)
                if n >= 3:
                    values(n - 3)
            for n in range(len(ITEMS), len(ITEMS) + 3):
                if n - 2 < len(ITEMS):
                    weigh(n - 2)
                values(n - 3)

            pe.wait_ge(*when("prob2.47"))
            pe.wait_ge(*when("gla_m.1"))
            for h in range(4):
                rows = slice(32 * h, 32 * h + 32)
                for c in range(8):
                    last = mm(bank(h)[0:64, 64 * c:64 * c + 64], GE[1][rows, 64 * c:64 * c + 64], GE[0][rows, 64 * c:64 * c + 64], start=True, stop=True)
                last.then_inc(*did(f"gla_att_mm.{h}"))
            pe.wait_ge(*when("gla_m.2"))
            for c in range(8):
                pe.wait_ge(*when(f"gla_tok.{c - 2}" if c >= 2 else "nsa_o.3"))
                pe.sem_inc(passed, 1)
                for m, src in enumerate((GE[2][:, :], z(13), z(14))):
                    last = nc.tensor.transpose(bank(4 + c % 2)[0:64, m * P:(m + 1) * P], src[:, 64 * c:64 * c + 64], IDENT)
                last.then_inc(*did(f"gla_tok_mm.{c}"))
            for c in range(7):
                pe.wait_ge(*when("gla_tok.7" if c < 2 else f"gla_st.{c - 2}.3"))
                mm(bank(4 + c % 2, 256), GV[:, c, 0:P], GV[:, c, P:3 * P], start=True, stop=True).then_inc(*did(f"gla_kv.{c}"))
            pe.wait_ge(*when("gla_att.3"))
            pe.wait_ge(*when("gla_m.3"))
            pe.wait_ge(*when("gla_st.6.3"))
            pe.sem_inc(passed, 1)
            for m in range(2):
                for c in range(8):
                    cols_ = slice(64 * c, 64 * c + 64)
                    for hp in range(2):
                        h = 2 * m + hp
                        last = mm(bank(6 + m)[64 * hp:64 * hp + 64, cols_], GV[:, c, P + 64 * h:P + 64 * h + 64], GA[:, h, cols_], start=True, stop=c == 0)
                    if c:
                        last = mm(bank(6 + m)[:, cols_], GS[:, c, P * m:P * m + P], GE[3][:, cols_], start=False, stop=True)
                last.then_inc(*did(f"gla_o.{m}"))
            for m in range(2):
                pe.wait_ge(*when(f"gla_sq.{m}"))
                mm(bank(m), HALVES, SQ[m][:, :], start=True, stop=True).then_inc(*did(f"gla_ss.{m}"))
            for g in range(4):
                for m in range(2):
                    pe.wait_ge(*when(f"gr_sq.{2 * g + m}"))
                    mm(bank(4 + g), ONES, SQ[m][:, :], start=m == 0, stop=m == 1).then_inc(*did(f"gr_ss.{2 * g + m}"))
            open_squares("y1")
            with led.loop(pe, "mx_out", 2) as i:
                for b in range(4):
                    tile(i + Q + 6, b, Hh, Hl, "mx3_lo" if b == 0 else None).then_inc(w_used, 1)
                    add_squares("y1", (b - 1) % 4, (b - 1) % 2, None if b else "mx_out")
            last_squares("y1", 3)
            sums("h2", 6, S)
            for a in range(2):
                q0 = Q + 8 + 8 * a
                with led.loop(pe, f"up{a}", 4) as i:
                    for b in range(4):
                        tile(i + q0, b, Hh, Hl, "h2_lo" if b == 0 else None).then_inc(w_used, 1)
                if a:
                    open_squares("y2")
                with led.loop(pe, f"down{a}", 4) as i:
                    for b in range(4):
                        if b == 0:
                            pe.wait_ge(*when(f"hid{a}_b.3"))
                        tile(i + q0 + 4, b, HIDh, HIDl, even=b % 2 == 0).then_inc(w_used, 1)
                        if a and b == 0:
                            add_squares("y2", 1, 1, "down1")
                        if a and b == 2:
                            add_squares("y2", 0, 0)
            last_squares("y2", 1)

    ctx.close()
    return led.learnt()


def tables():
    f = np.float32
    t = np.arange(S)
    eye = np.eye(P, dtype=f)
    half = np.kron(np.eye(2), np.ones((64, 64))).astype(f)
    out = {"eye": np.concatenate([eye, np.ones((P, P), f), half], 1)}
    inv = np.power(f(10000.0), -np.arange(32, dtype=f) / f(32)).astype(f)
    place = np.stack([(t // 64).astype(f), (t % 64).astype(f)])
    d = np.arange(P)
    ang = (place[d // 64] * inv[d % 32][:, None]).astype(f)
    rope = np.zeros((P, P), f)
    for i in range(P):
        rope[i + 32 if i % 64 < 32 else i - 32, i] = -1.0 if i % 64 < 32 else 1.0
    cnt = np.zeros((P, 2, S), f)
    for g, w in enumerate((2, 4, 8, 16)):
        n = np.clip(t + w // 2, 0, S) - np.clip(t - w // 2, 0, S)
        cnt[64 * (g % 2):64 * (g % 2) + 64, g // 2] = (1.0 / n).astype(f)
    out["tab_attn"] = [np.cos(ang).astype(f), np.sin(ang).astype(f), cnt.reshape(P, -1), rope]
    w = 2 * np.pi * (np.arange(256) + 0.5) / 1024
    fwd = np.zeros((P, 2, 2, 2, 256))
    inv_ = np.zeros((P, 2, 2, 2, 256))
    for e in range(2):
        for c, fn in enumerate((np.cos, np.sin)):
            m = fn(np.outer(2 * np.arange(256) + e, w))
            fwd[:, e, c] = m.reshape(2, P, 256).transpose(1, 0, 2)
            inv_[:, e, c] = m.T.reshape(2, P, 256).transpose(1, 0, 2)
    out["dft"] = np.concatenate([fwd.reshape(P, -1), inv_.reshape(P, -1)], 1).astype(f)
    order = np.concatenate([t[0::2], t[1::2]])
    lin = np.linspace(0.0, 1.0, S, dtype=f)
    ww = (f(2.0 * np.pi) * t.astype(f) / f(S))[:, None]
    ff = np.linspace(1e-4, 15, 16, dtype=f)[None, :]
    emb = np.concatenate([lin[:, None], np.cos(ff * ww), -np.sin(ff * ww)], 1).astype(f)
    out["emb"] = np.ascontiguousarray(emb[order].T)
    deltas = np.abs(np.linspace(np.log(1e-2) / 1.5, np.log(1e-2) / 0.3, 768, dtype=f))
    out["delta"] = np.tile(deltas[None], (P, 1)).astype(f)
    out["time"] = -lin[order].reshape(4, P).T
    c = 2 * np.pi * np.outer(np.arange(256), np.arange(256)) / 256
    s = 1 / np.sqrt(S * 256.0)
    m = np.concatenate([np.cos(c) * s, np.sin(c) * s], 1)
    out["dft_ch"] = np.ascontiguousarray(m.reshape(2, P, 512).transpose(1, 0, 2).reshape(P, -1)).astype(f)
    c = 2 * np.pi * (np.outer(t, t) % S) / S
    out["dft_cos"], out["dft_sin"] = np.cos(c).astype(f), (-np.sin(c)).astype(f)
    q, k = np.arange(P)[:, None], np.arange(P)[None, :]
    bias = np.where(k <= q, 0, -1e30)
    cmpb = np.zeros((P, 4, 32))
    for i in range(4):
        cmpb[:, i] = np.where(16 * np.arange(32)[None] + 31 <= 128 * i + q, 0, -1e30)
    rot = np.zeros((64, 64))
    for i in range(8):
        rot[i + 8, i], rot[i, i + 8] = -1.0, 1.0
    dupk, dupr = np.zeros((P, P)), np.zeros((P, P))
    dupk[:64] = np.concatenate([np.eye(64)] * 2, 1)
    dupr[:64] = np.concatenate([rot] * 2, 1)
    rot2 = np.kron(np.eye(2), rot)
    dupv = np.concatenate([np.concatenate([np.eye(64)] * 2, 1)] * 2, 0)
    tril = np.where(q <= k, 1.0, 0.0)
    scan = np.tile(np.where(t % 64 == 0, 0.0, 1.0)[None], (P, 1))
    out["tab_layers"] = np.concatenate([bias, cmpb.reshape(P, -1), dupk, dupr, rot2, dupv, tril, scan], 1).astype(f)
    out["gla_mask"] = np.tile((np.arange(64)[:, None] <= np.arange(64)[None, :]).astype(np.int32), (1, 8))
    invf = np.power(f(500000.0), -np.arange(0, 16, 2, dtype=f) / f(16)).astype(f)
    r = np.arange(P) % 64
    out["inv_freq"] = np.where(r < 16, invf[r % 8], 0).astype(f)[:, None]
    valid = np.ones((P, 4), f)
    valid[:31, 0] = 0
    out["row_valid"] = valid
    return out


def columns(v):
    return np.ascontiguousarray(v.reshape(-1, P).T)


def tiles(w):
    n = w.shape[1] // P
    return w.reshape(KT, P, n, P).transpose(2, 1, 0, 3).reshape(n, P, D)


def pairs(t):
    return t.reshape(-1, 2, P, D).transpose(0, 2, 1, 3).reshape(-1, P, 2 * D)


def units(w):
    n = w.shape[1] // D
    return w.reshape(KT, P, n, D).transpose(2, 0, 1, 3).reshape(-1, D)


def padded(a, rows=P):
    out = np.zeros((rows,) + a.shape[1:], a.dtype)
    out[:a.shape[0]] = a
    return out


def layout(x, c, ctx, c_ctx, w_mod, b_mod, norm_g, ev_w_in, ev_w_out, pool_w, pool_scale, q_norm_g, k_norm_g, od_w_in,
           od_w_out, hy_conv_w, hy_conv_b, hy_w1, hy_b1, hy_w2, hy_b2, hy_w3, hy_freq, hy_skip, fn_w, final_g, c_2,
           positions_2, w_in_2, conv_w_2, cmp_pos_2, cmp_w1_2, cmp_w2_2, gla_gate_w2_2, gla_gate_b_2, gmlp_ws_2,
           gmlp_b_2, grp_gain_2, w_o_2, norm_g_2, w_mod_2, b_mod_2, w_up_2, w_down_2):
    f = np.float32
    tab = tables()
    A = {"xT": np.ascontiguousarray(x[0].T), "ctxT": np.ascontiguousarray(ctx[0].T), "pos": np.ascontiguousarray(positions_2)}
    cols = {
        "c": columns(c[0]), "c_ctx": columns(c_ctx), "cond": np.concatenate([columns(c[0])] * 4 + [columns(c_2[0])] * 12, 1),
        "b_mod": np.concatenate([columns(b_mod[0, 2 * D:]), columns(b_mod[1]), columns(b_mod_2[0]), columns(b_mod_2[1])], 1),
        "b_mod0": columns(b_mod[0, :2 * D]), "g0": columns(norm_g[0]), "g1": columns(norm_g[1]), "q_g": columns(q_norm_g[0]),
        "k_g": columns(k_norm_g[0]), "pool_scale": columns(pool_scale[0]), "conv_w": np.concatenate([columns(hy_conv_w[0, j]) for j in range(3)], 1),
        "conv_b": columns(hy_conv_b[0]), "hy_b1": padded(hy_b1[0][:, None]), "hy_b2": padded(hy_b2[0][:, None]),
        "freq": padded(hy_freq[0][:, None]), "skip": np.concatenate([columns(hy_skip[0, o]) for o in range(2)], 1),
        "final_g": columns(final_g), "g2": np.concatenate([columns(norm_g_2[l].reshape(-1)) for l in range(LAYERS)], 1),
        "time": tab["time"], "inv_freq": tab["inv_freq"], "row_valid": tab["row_valid"]}
    A["cols"] = np.concatenate([cols[n] for n in COLS], 1).astype(f, copy=False)
    for n in ("eye", "dft", "emb", "delta", "dft_ch", "dft_cos", "dft_sin", "tab_layers", "gla_mask"):
        A[n] = tab[n]
    poolw = np.zeros((P, 2 * P), f)
    for g in range(4):
        poolw[64 * (g % 2):64 * (g % 2) + 64, P * (g // 2) + 64 * (g % 2):P * (g // 2) + 64 * (g % 2) + 64] = pool_w[0, g]
    A["tab_attn"] = np.concatenate(tab["tab_attn"] + [poolw], 1)
    A["hy_w1"], A["hy_w2"], A["fn_w"] = hy_w1[0], hy_w2[0], fn_w[0]
    A["hy_w3"] = np.ascontiguousarray(hy_w3[0].reshape(64, 2, 2, 2, 384).transpose(0, 1, 3, 2, 4).reshape(64, -1))
    A["wmod0"] = units(w_mod[0][:, :2 * D])
    A["wmod"] = np.concatenate([units(w_mod[0][:, 2 * D:]), units(w_mod[1])] + [units(w_mod_2[l]) for l in range(LAYERS)])
    w = ev_w_in[0]
    ev = np.concatenate([w[:, 1280:1536], w[:, 1536:1792], w[:, 512:1280], w[:, 0:256], w[:, 256:512], w[:, 1792:2560]], 1)
    stream = [pairs(tiles(m)) for m in (ev, ev_w_out[0], od_w_in[0], od_w_out[0])]
    blobs = []
    for l in range(LAYERS):
        w = w_in_2[l]
        misc = np.zeros((D, P), f)
        misc[:, 0:16], misc[:, 32:44] = w[:, 2188:2204], w[:, 1408:1420]
        parts = [w[:, 0:768], w[:, 768:1024], w[:, 1024:1408], w[:, 1420:1548], w[:, 1548:1676], w[:, 1676:1932],
                 w[:, 1932:2188], w[:, 2204:2460], w[:, 2460:2716], misc]
        stream.append(pairs(tiles(np.concatenate(parts, 1))))
        cols2 = {
            "ws": gmlp_ws_2[l].transpose(2, 0, 1).reshape(P, 4 * P),
            "w2k": np.concatenate([cmp_w2_2[l, 0]] * 2, 1), "w2v": np.concatenate([cmp_w2_2[l, 1]] * 2, 1),
            "gate_w": padded(gla_gate_w2_2[l]),
            "gm_b": np.concatenate([np.repeat(gmlp_b_2[l, 2 * m:2 * m + 2], 64, 0) for m in range(2)], 1),
            "conv": np.concatenate([columns(conv_w_2[l, j]) for j in range(3)], 1),
            "pos": np.concatenate([cmp_pos_2[l, s].T for s in range(2)], 0), "gate_b": columns(gla_gate_b_2[l]),
            "gain": columns(grp_gain_2[l])}
        blob = np.zeros((1, P, 2 * D), f)
        blob[0, :, :N_BLOB] = np.concatenate([cols2[n] for n in BLOB], 1)
        stream += [blob, pairs(tiles(w_o_2[l]))]
        up = tiles(w_up_2[l])
        down = w_down_2[l].reshape(2, 16, P, KT, P).transpose(0, 3, 2, 1, 4).reshape(2, KT, P, 2 * D)
        for a in range(2):
            stream += [pairs(up[16 * a:16 * a + 16]), down[a]]
    stream.append(np.zeros((1, P, 2 * D), f))
    A["wt"] = np.concatenate(stream).reshape(-1, 2 * D)
    A["cmp_w1"] = np.concatenate([cmp_w1_2[l].reshape(2, 32, 64, P).transpose(0, 2, 1, 3).reshape(P, 32 * P) for l in range(LAYERS)])
    return A


def kernel(**inputs):
    import concourse.bacc as bacc
    from concourse.bass_utils import run_bass_kernel_spmd

    arrays = {k: np.ascontiguousarray(a) for k, a in layout(**{k: np.asarray(a) for k, a in inputs.items()}).items()}

    def build(known=None):
        nc = bacc.Bacc("TRN2", target_bir_lowering=False, num_devices=1)
        A = {k: nc.dram_tensor(f"in_{k}", a.shape, mybir.dt.from_np(a.dtype), kind="ExternalInput").ap() for k, a in arrays.items()}
        A["out"] = nc.dram_tensor("out_x", (D, S), mybir.dt.float32, kind="ExternalOutput").ap()
        return nc, program(nc, A, known)

    nc, _ = build(build()[1])
    r = run_bass_kernel_spmd(nc, [{f"in_{k}": a for k, a in arrays.items()}], core_ids=[0])
    return np.ascontiguousarray(r.results[0]["out_x"].T)[None]
```

```python
import contextlib
from contextlib import ExitStack

import numpy as np
import concourse.bass as bass
from concourse import mybir

P = 128
D = 1024
KT = D // P
S = 512
NT = S // P
CTX = 256
LAYERS = 2
EPS = 1e-6

ROUND = 12582912.0
TURN = (6.28125, 0.0019350051879882812, 3.019914e-07)
PI_IN = 3.1415925

EV_IN, EV_OUT, OD_IN, OD_OUT = 20, 8, 28, 8
T_EV_IN = 0
T_EV_OUT = T_EV_IN + EV_IN
T_OD_IN = T_EV_OUT + EV_OUT
T_OD_OUT = T_OD_IN + OD_IN
T_LAYERS = T_OD_OUT + OD_OUT
MX_IN, MX_BLOB, MX_OUT, HALF_UP, HALF_DOWN = 22, 2, 8, 16, 16
L_IN = 0
L_BLOB = L_IN + MX_IN
L_OUT = L_BLOB + MX_BLOB
L_FF = L_OUT + MX_OUT
PER_LAYER = L_FF + 2 * (HALF_UP + HALF_DOWN)
PRIME = 4
SEGS = 16
UNITS = 8

COLS = {}
N_COLS = 0
for _name, _n in (("c", 8), ("c_ctx", 8), ("cond", 8 * SEGS), ("b_mod", 8 * SEGS), ("b_mod0", 16), ("g0", 8), ("g1", 8),
                  ("q_g", 1), ("k_g", 1), ("pool_scale", 2), ("conv_w", 54), ("conv_b", 18), ("hy_b1", 1), ("hy_b2", 1),
                  ("freq", 1), ("skip", 12), ("final_g", 8), ("g2", 32 * LAYERS), ("time", 4), ("inv_freq", 1),
                  ("row_valid", 4)):
    COLS[_name] = (N_COLS, _n)
    N_COLS += _n

BLOB = {}
N_BLOB = 0
for _name, _n in (("ws", 512), ("w2k", 128), ("w2v", 128), ("gate_w", 128), ("gm_b", 256), ("conv", 6), ("pos", 32),
                  ("gate_b", 1), ("gain", 8)):
    BLOB[_name] = (N_BLOB, _n)
    N_BLOB += _n


class Ledger:

    def __init__(self, nc, ctx, known):
        self.nc, self.ctx, self.known = nc, ctx, known
        self.engine = None
        self.sems, self.counts, self.marks, self.per, self.stack = {}, {}, {}, {}, []

    def sem(self, name):
        if name not in self.sems:
            self.sems[name] = self.ctx.enter_context(self.nc.semaphore(name))
        return self.sems[name]

    def did(self, label, by=1):
        name = label.split(".")[0]
        if self.engine and name not in self.counts:
            name = f"{name.split('_')[0]}_on_{self.engine}"
        self.counts[name] = self.counts.get(name, 0) + by
        assert label not in self.marks, label
        self.marks[label] = (name, self.counts[name], tuple(k for k, _, _ in self.stack))
        return self.sem(name), by

    def prime(self, name, n):
        self.counts[name] = n
        return self.sem(name), n

    def when(self, label, back=None):
        if self.known is None:
            return self.sem("unknown_yet"), 1
        name, value, loops = self.known[0][label]
        for loop in loops:
            per = self.known[1][loop, name]
            here = [var for k, var, _ in self.stack if k == loop]
            if here:
                value = here[0] * per + (value - (per if back == loop else 0))
            else:
                value = value + (self.known[2][loop] - 1) * per
        return self.sem(name), value

    @contextlib.contextmanager
    def loop(self, engine, name, trips):
        before = dict(self.counts)
        with engine.Fori(0, trips) as i:
            self.stack.append((name, i, trips))
            yield i
            self.stack.pop()
        self.per[name, "trips"] = trips
        for k, n in self.counts.items():
            more = n - before.get(k, 0)
            if more:
                self.per[name, k] = more
                self.counts[k] = n + (trips - 1) * more

    def learnt(self):
        return self.marks, self.per, {k[0]: v for k, v in self.per.items() if k[1] == "trips"}


def program(nc, A, known=None):
    f32, f32r, i32 = mybir.dt.float32, mybir.dt.float32r, mybir.dt.int32
    ACT, ALU, AX = mybir.ActivationFunctionType, mybir.AluOpType, mybir.AxisListType
    add, sub, mul = ALU.add, ALU.subtract, ALU.mult
    ds = bass.ds
    ctx = ExitStack()
    led = Ledger(nc, ctx, known)
    did, when, sem = led.did, led.when, led.sem

    base = (nc.sbuf_base + 63) // 64 * 64
    made = [0]

    def at(offset, shape, dt=f32, name="t"):
        made[0] += 1
        return nc.alloc_sbuf_tensor_at(f"{name}_{made[0]}", shape, dt, offset=base + offset)

    KB = 1024
    X_AT, BIG_AT = 0, 16 * KB
    WIDE_AT = BIG_AT + 64 * KB
    RAW_AT = WIDE_AT + 48 * KB
    SPLIT_AT = RAW_AT + 16 * KB
    MOD_AT = SPLIT_AT + 16 * KB
    TAB_AT = MOD_AT + 20 * KB
    SMALL_AT = TAB_AT + 16 * KB

    X = at(X_AT, [P, KT * S], name="x")
    Z = at(BIG_AT, [P, 32 * S], name="z")
    Hh = at(WIDE_AT, [P, KT, S], f32r, name="h_high")
    Hl = at(WIDE_AT + 16 * KB, [P, KT, S], f32r, name="h_low")
    Y = at(WIDE_AT + 32 * KB, [P, KT * S], name="y")
    Ch = at(WIDE_AT + 32 * KB, [P, KT, CTX], f32r, name="ctx_high")
    Cl = at(WIDE_AT + 40 * KB, [P, KT, CTX], f32r, name="ctx_low")
    RAW = [at(RAW_AT + 8 * KB * i, [P, 2, D], name="w_raw") for i in range(2)]
    WH = [at(SPLIT_AT + 4 * KB * i, [P, KT, P], f32r, name="w_high") for i in range(2)]
    WL = [at(SPLIT_AT + 8 * KB + 4 * KB * i, [P, KT, P], f32r, name="w_low") for i in range(2)]
    MOD = [at(MOD_AT + 4 * KB * i, [P, D], name="mod_raw") for i in range(4)]
    ACC = at(MOD_AT + 16 * KB, [P, D], name="mod_acc")
    small = [0]

    def keep(n, name, dt=f32):
        size = (4 * n + 31) // 32 * 32
        small[0] += size
        return at(SMALL_AT + small[0] - size, [P, n], dt, name=name)

    EYE = keep(3 * P, "eye")
    IDENT, ONES, HALVES = EYE[:, 0:P], EYE[:, P:2 * P], EYE[:, 2 * P:3 * P]
    COL = keep(N_COLS, "cols")
    CVEC = keep(16 + 8 * SEGS, "silu_cond")
    MODV0, MODV = keep(32, "mod0"), keep(8 * SEGS, "modv")
    AFF = keep(16, "norm_gain")
    RS = keep(S, "rs")
    SQ = [keep(S, "sq") for _ in range(2)]
    assert base + SMALL_AT + small[0] <= nc.sbuf_usable_end, small

    def col(name, k=0, n=1, rows=P):
        return COL[0:rows, COLS[name][0] + k:COLS[name][0] + k + n]

    PS = ctx.enter_context(nc.psum_tensor("banks", [P, 8 * S], f32))

    def bank(b, n=S, rows=slice(0, P)):
        return PS[rows, b * S:b * S + n]

    def z(n, rows=slice(0, P)):
        return Z[rows, n * S:(n + 1) * S]

    w_loaded = [sem(f"weights_loaded{i}") for i in range(2)]
    w_high, w_low, w_used = sem("weights_high"), sem("weights_low"), sem("weights_used")
    taken = sem("tile_taken")
    passed = sem("waits_passed")
    mod_loaded = [sem(f"mod_loaded{i}") for i in range(4)]
    mod_used, mod_summed, mod_taken = sem("mod_used"), sem("mod_summed"), sem("mod_taken")

    PR = [at(WIDE_AT + 4 * 768 * i, [P, 768], name="probs") for i in range(2)]
    PT = [at(WIDE_AT + 4 * (1536 + 3072 * i), [P, 6, S], name="probs_t") for i in range(2)]
    RSS = [at(WIDE_AT + 4 * (1536 + S * i), [P, S], name="rs_s") for i in range(6)]
    ZN = [at(WIDE_AT + 4 * (1536 + S * (6 + i)), [P, S], name="zn") for i in range(2)]
    RA = [at(WIDE_AT + 4 * (1536 + S * (8 + i)), [P, S], name="rope_a") for i in range(2)]
    RB = [at(WIDE_AT + 4 * (1536 + S * (10 + i)), [P, S], name="rope_b") for i in range(2)]
    PU, PV_, PW_ = [at(WIDE_AT + 4 * (7680 + 1056 * i), [P, 2, 528], name="pool") for i in range(3)]
    TABC = at(TAB_AT, [P, 4 * S + 3 * P], name="tab_attn")
    COS0, SIN0 = TABC[:, 0:S], TABC[:, S:2 * S]
    INVC = TABC[:, 2 * S:4 * S]
    ROPE0 = TABC[:, 4 * S:4 * S + P]
    POOLW = TABC[:, 4 * S + P:4 * S + 3 * P]
    CKV = at(BIG_AT + 20 * 2 * KB, [P, 4, CTX], name="ctx_kv")
    KALL = at(BIG_AT + 22 * 2 * KB, [P, 2, 768], name="k_all")
    VT = at(BIG_AT + 25 * 2 * KB, [P, 6, 2 * P], name="v_tokens")
    CX = at(BIG_AT + 16 * 2 * KB, [P, KT, CTX], name="ctx_in")
    CT_ = at(BIG_AT + 20 * 2 * KB, [P, KT, CTX], name="ctx_t")
    ACC0 = [ACC, at(BIG_AT + 24 * 2 * KB, [P, D], name="mod_acc0")]
    RSC = at(BIG_AT + 30 * 2 * KB, [P, CTX], name="rs_ctx")
    NORM_T = Z[:, 0:KT * S]

    G = 384
    KSP = [at(o, [P, 2, 4, G], name="k_spec") for o in (WIDE_AT, MOD_AT)]
    GSP = at(WIDE_AT + 12 * KB, [P, 2, 4, G], name="g_spec")
    PM = at(WIDE_AT + 24 * KB, [P, 8, G], name="spec_products")
    FSUM = at(MOD_AT + 12 * KB, [P, 4, G], name="filter_sum")
    FDIFF = at(RAW_AT + 8 * KB, [P, 4, G], name="filter_diff")
    ZT = at(WIDE_AT + 36 * KB, [P, 4, G], name="z_tokens")
    ODD = {"hz": at(WIDE_AT + 42 * KB, [P, 2, G], name="z_odd"),
           "hk": at(SPLIT_AT + 12 * KB, [P, 2, G], name="k_odd")}
    MAG = at(SPLIT_AT + 4 * KB, [P, 2, G], name="filter_mag")
    DFT = at(TAB_AT, [P, 16 * 256], name="dft")
    FWD = DFT[:, 0:2048].rearrange("p (e c t f) -> p e c t f", e=2, c=2, t=2)
    INV = DFT[:, 2048:4096].rearrange("p (e c f t) -> p e c f t", e=2, c=2, f=2)
    HDN = at(BIG_AT + 29 * 2 * KB, [P, S], name="hdn")
    DELTA = at(BIG_AT + 30 * 2 * KB, [P, 768], name="delta")
    EMB = at(BIG_AT + 8 * 2 * KB, [33, S], name="emb")
    HW12 = at(BIG_AT + 9 * 2 * KB, [64, 2, 64], name="hy_w12")
    W3 = at(WIDE_AT + 45 * KB, [P, 768], name="hy_w3")
    ARG = [at(BIG_AT + (10 + i) * 2 * KB, [64, S], name="arg") for i in range(3)]
    TAP = [at(WIDE_AT + 12 * KB + 2 * KB * i, [P, S], name="conv_taps") for i in range(3)]
    HH = [at(o, [P, G], name="filter") for o in (MOD_AT + 18 * KB, RAW_AT + 14 * KB)]
    PMY = [at(WIDE_AT + 24 * KB + 2 * KB * c, [P, S], name="hy_y") for c in range(2)]
    ABSA, DEC = SQ[0], SQ[1]
    HINV = [AFF[:, 4 * i:4 * i + 3] for i in range(2)]
    CTT = at(WIDE_AT, [P, 4, S], name="dft_cos")
    U2 = at(WIDE_AT + 8 * KB, [P, 2, S], name="fn_full")
    CSC = at(MOD_AT + 12 * KB, [P, 2, S], name="dft_ch")
    FNW = at(MOD_AT + 16 * KB, [P, 2, CTX], name="fn_w")
    NST = at(RAW_AT + 8 * KB, [P, 4, S], name="dft_sin")
    AB = [at(SPLIT_AT + KB * o, [P, S], name="fn_half") for o in (4, 6, 12, 14)]

    PAR = at(MOD_AT, [P, 2 * D], name="layer_params")
    TB2 = at(MOD_AT + 8 * KB, [P, 3 * S + 7 * P], name="tab_layers")
    BIAS, CMPB = TB2[:, 0:P], TB2[:, P:2 * P]
    DUPK, DUPR, ROT2, DUPV = [TB2[:, (2 + i) * P:(3 + i) * P] for i in range(4)]
    TRIL = TB2[:, 6 * P:7 * P]
    SCANM = TB2[:, 7 * P:7 * P + S]
    COS2, SIN2 = TB2[:, 7 * P + S:7 * P + 2 * S], TB2[:, 7 * P + 2 * S:7 * P + 3 * S]
    GMASK = at(MOD_AT + 8 * KB + 4 * (7 * P + 3 * S), [64, S], i32, name="gla_mask")
    CW1 = at(TAB_AT, [P, 32 * P], name="cmp_w1")
    LM = at(MOD_AT + 8 * KB + 4 * (7 * P + 4 * S), [P, 48], name="layer_mod")
    LG = COL[:, COLS["cond"][0]:COLS["cond"][0] + 32]

    def par(name, k=0, n=1, rows=slice(0, P)):
        return PAR[rows, BLOB[name][0] + k:BLOB[name][0] + k + n]

    HIDh = at(BIG_AT, [P, 16, S], f32r, name="hidden_high")
    HIDl = at(BIG_AT + 32 * KB, [P, 16, S], f32r, name="hidden_low")
    POSI = at(BIG_AT + 31 * 2 * KB, [P, S], i32, name="positions")
    TP = at(WIDE_AT, [P, 2, 16, 31], name="cmp_blocks")
    QR = at(WIDE_AT + 4 * 1024, [P, 2, S], name="q_rope")
    K2 = [at(SPLIT_AT + KB * o, [P, 2, S], name="k_rope") for o in (4, 12)]
    VS_, VW_ = [at(WIDE_AT + 4 * (3072 + 512 * i), [P, 4, P], name="v_tok") for i in range(2)]
    GT = at(WIDE_AT + 4 * 4096, [P, 4, 12], name="gates")
    KC = at(WIDE_AT + 4 * 2048, [P, 2, 32], name="k_cmp")
    HC = at(WIDE_AT + 4 * 4192, [P, 2, 32], name="cmp_hidden")
    VC = at(WIDE_AT + 4 * 4256, [32, P], name="v_cmp")
    P2 = [at(WIDE_AT + 4 * (4608 + S * i), [P, S], name="probs2") for i in range(3)]
    PT2 = [at(WIDE_AT + 4 * (6144 + S * i), [P, 4, P], name="probs2_t") for i in range(2)]
    RT = [at(WIDE_AT + 4 * (7168 + S * i), [P, S], name="rope_t") for i in range(2)]
    P2.append(RT[0])
    NO = at(WIDE_AT + 4 * 8192, [P, 2, S], name="nsa_out")
    AO = at(WIDE_AT + 4 * 9216, [P, 2, S], name="conv_out")
    MO = at(WIDE_AT + 4 * 10240, [P, 2, S], name="gmlp_out")
    GO = at(WIDE_AT + 4 * 11264, [P, 2, S], name="gla_out")
    STAT = at(SMALL_AT + small[0], [P, 64], name="stats")
    ST2 = [STAT[:, 8 * i:8 * i + 8] for i in range(4)]
    DECY = STAT[:, 48:56]
    EPSC = at(SMALL_AT + small[0] + 256, [P, 1], name="eps")
    EMB2 = at(BIG_AT + 13 * 2 * KB, [64, S], name="hdn_first")
    AF2 = at(MOD_AT + 4 * 5040, [P, 32], name="layer_gain")
    RL = [at(MOD_AT + 2 * KB * i, [P, S], name="relu") for i in range(2)]
    GE = [at(BIG_AT + 2 * KB * i, [P, S], name="gla_e") for i in (0, 1, 2, 5)]
    GB, GM = [at(BIG_AT + 2 * KB * i, [P, S], name="gla_b") for i in (4, 3)]
    GR = [at(WIDE_AT + 2 * KB * i, [P, S], name="group_rs") for i in range(6)]
    GV = at(WIDE_AT + 12 * KB, [64, 8, 384], name="gla_tok")
    GS = at(BIG_AT + 28 * 2 * KB, [P, 8, 256], name="gla_state")
    GA = at(BIG_AT + 22 * 2 * KB, [64, 4, S], name="gla_att")
    GMV = at(BIG_AT + 26 * 2 * KB, [P, 4, 2 * P], name="gmlp_tok")
    assert base + SMALL_AT + small[0] + 260 <= nc.sbuf_usable_end, small
    block = ctx.enter_context(nc.Block())

    R1 = [("ck", 0), ("ck", 1), ("k", 0), ("k", 1)] + [("q", h) for h in range(6)]
    NC1 = len(R1)
    BATCHES = (range(0, 4), range(4, NC1))
    RS_SLOT = [j if j < 4 else j - 4 for j in range(NC1)]
    V_T, X1_T, X2_T, FN_T, HG_T, FG_T = 0, 6, 12, 18, 20, 26
    STEPS = [(g, o) for g in range(2) for o in range(2)]
    FILTER_AT = (2, 6, 10, 14)
    SPEC_BANK = {"hk": 0, "hz": 4}
    ITEMS = [(h, i, br) for h in range(4) for i in range(NT) for br in range(3)]
    WIDTH = [31 if br == 2 else P * (i + 1) for _, i, br in ITEMS]
    GROUP_BANK = (0, 2, 5, 1)
    ROT_BANKS = (6, 1, 6, 1)
    SCORE_BANKS = (0, 1, 2, 7)
    MIXED = ("conv_y.all", "nsa_o.3", "gla_y.1", "gm_y.1")
    UNITS_AT = ((0, 1, 2), (3, 4, 5), (6, 7), ())

    @block.sync
    def _(sp):
        sp.dma_start(COL[:, :], A["cols"]).then_inc(*did("in_small.cols", 16))
        sp.dma_start(EYE[:, :], A["eye"]).then_inc(*did("in_small.all", 16))
        sp.dma_start(EMB[:, :], A["emb"]).then_inc(*did("in_net.emb", 16))
        sp.dma_start(HW12[0:33, 0, :], A["hy_w1"]).then_inc(*did("in_net.w1", 16))
        sp.dma_start(HW12[:, 1, :], A["hy_w2"]).then_inc(*did("in_net.all", 16))
        sp.dma_start(X[:, :].rearrange("p (k t) -> p k t", k=KT), A["xT"].rearrange("(k p) t -> p k t", p=P)).then_inc(*did("in_x.all", 16))
        sp.dma_start(CX[:, :, :], A["ctxT"].rearrange("(k p) t -> p k t", p=P)).then_inc(*did("in_ctx.all", 16))

        for u in range(2 * UNITS):
            k, s = divmod(u, 2)
            if k >= 2 and s == 0:
                sp.wait_ge(*when(f"shift.{k - 2}"))
            elif k >= 2:
                sp.wait_ge(mod_used, UNITS + k - 1 + PRIME)
            unit0 = s * UNITS + k
            sp.dma_start(MOD[u % 4][:, :], A["wmod0"][unit0 * P:(unit0 + 1) * P, :]).then_inc(mod_loaded[u % 4], 16)
        sp.dma_start(TABC[:, :], A["tab_attn"]).then_inc(*did("in_tabc.all", 16))

        def load_pair(q, half):
            sp.wait_ge(w_low, 4 * q + 2 * half - 2 + PRIME)
            sp.dma_start(RAW[half][:, :, :], A["wt"][ds((2 * q + half) * P, P), :].rearrange("p (n c) -> p n c", n=2)).then_inc(w_loaded[half], 16)

        def load_units(q, ks):
            for k in ks:
                sp.wait_ge(mod_used, 8 * q + 16 + k - 3 + PRIME)
                sp.dma_start(MOD[k % 4][:, :], A["wmod"][ds((8 * q + k) * P, P), :]).then_inc(mod_loaded[k % 4], 16)

        def bodies(name, q0, trips):
            with led.loop(sp, name, trips) as i:
                load_body(i + q0)

        def load_body(q):
            load_units(q, (0, 1, 2, 3))
            load_pair(q, 1)
            load_units(q, (4, 5, 6, 7))
            load_pair(q + 1, 0)

        load_pair(0, 0)
        sp.wait_ge(*when(f"shift.{UNITS - 1}"))
        sp.wait_ge(mod_used, 2 * UNITS + PRIME)
        load_body(0)
        bodies("ev_in", 1, EV_IN // 4 - 1)
        bodies("ev_out", 5, EV_OUT // 4)
        sp.wait_ge(*when("pool_y.1"))
        sp.wait_ge(*when("pool_d.all"))
        sp.dma_start(DFT[:, :], A["dft"]).then_inc(*did("in_hy.dft", 16))
        bodies("od_in", 7, OD_IN // 4)
        sp.wait_ge(w_used, T_OD_OUT + PRIME)
        sp.dma_start(DELTA[:, :], A["delta"]).then_inc(*did("in_hy2.all", 16))
        for n, (g, o) in enumerate(STEPS):
            if n:
                sp.wait_ge(*when(f"hy_filt.{n - 1}.7"))
            sp.dma_start(W3[0:64, :], A["hy_w3"][:, (2 * o + g) * 768:(2 * o + g + 1) * 768]).then_inc(*did(f"in_w3.{n}", 16))
        sp.wait_ge(*when("hk_mm.3.1"))
        sp.wait_ge(*when("hg_s.2.1.3"))
        sp.dma_start(CSC[:, :, :], A["dft_ch"].rearrange("p (k c) -> p k c", k=2)).then_inc(*did("in_fn.csc", 16))
        sp.dma_start(FNW[:, :, :], A["fn_w"].rearrange("(k p) c -> p k c", p=P)).then_inc(*did("in_fn.w", 16))
        sp.dma_start(CTT[:, :, :], A["dft_cos"].rearrange("(k p) c -> p k c", p=P)).then_inc(*did("in_fn.cos", 16))
        sp.dma_start(NST[:, :, :], A["dft_sin"].rearrange("(k p) c -> p k c", p=P)).then_inc(*did("in_fn.all", 16))
        sp.wait_ge(*when("hy_out.3.2"))
        sp.wait_ge(*when("fn_out.1"))
        sp.dma_start(POSI[:, :], A["pos"].to_broadcast([P, S])).then_inc(*did("in_pos.all", 16))
        bodies("od_out", 14, OD_OUT // 4)

        sp.wait_ge(mod_taken, SEGS + 2)
        sp.dma_start(TB2[:, 0:7 * P + S], A["tab_layers"]).then_inc(*did("in_tab2.all", 16))
        sp.dma_start(GMASK[:, :], A["gla_mask"]).then_inc(*did("in_tab2.mask", 16))
        with led.loop(sp, "layers", LAYERS) as lay:
            sp.wait_ge(w_used, lay * PER_LAYER + T_LAYERS - 1 + PRIME)
            sp.dma_start(CW1[:, :], A["cmp_w1"][ds(lay * P, P), :]).then_inc(*did("in_cw1.all", 16))

            with led.loop(sp, "layer_pairs", PER_LAYER // 4) as i:
                for half in (1, 0):
                    load_pair(lay * (PER_LAYER // 4) + i + (T_LAYERS // 4 + 1 - half), half)
        sp.wait_ge(*when("y2_x.7"))
        sp.dma_start(A["out"].rearrange("(k p) t -> p k t", p=P), X[:, :].rearrange("p (k t) -> p k t", k=KT)).then_inc(*did("stored.all", 16))
        sp.wait_ge(*when("stored.all"))

    @block.scalar
    def _(act):
        led.engine = "scalar"
        def split_high(q, b):
            act.wait_ge(w_loaded[b // 2], 16 * q + 16)
            act.wait_ge(w_used, 4 * q + b - 1 + PRIME)
            nc.scalar.activation(WH[b % 2][:, :, :].rearrange("p k c -> p (k c)"), RAW[b // 2][:, b % 2, :], ACT.Copy).then_inc(w_high, 1)

        def copy_out(q, b, dst, func=ACT.Copy):
            act.wait_ge(w_used, 4 * q + b + 1 + PRIME)
            nc.scalar.activation(dst, bank(b), func).then_inc(taken, 1)

        def next_tile(q, b):
            split_high(q + 1 if b == 3 else q, (b + 1) % 4)

        def squares(tag, src, n, k, ready=None):
            if ready:
                act.wait_ge(*ready)
            if k >= 2:
                act.wait_ge(*when(f"{tag}_ss.{k - 2}"))
            nc.scalar.activation(SQ[k % 2][:, 0:n], src, ACT.Square).then_inc(*did(f"{tag}_sq.{k}"))

        def root(tag, b, n, count, rs=RS):
            act.wait_ge(*when(f"{tag}_ss.7"))
            nc.scalar.activation(rs[:, 0:n], bank(b, n), ACT.Ln, bias=EPSC[:, :], scale=1.0 / count).then_inc(*did(f"{tag}_ln.all"))
            act.wait_ge(*when(f"{tag}_ln.all"))
            nc.scalar.activation(rs[:, 0:n], rs[:, 0:n], ACT.Exp, scale=-0.5).then_inc(*did(f"{tag}_rs.all"))

        def square_tile(tag, src, b, slot, *ready):
            act.wait_ge(*ready)
            nc.scalar.activation(SQ[slot][:, :], src, ACT.Square).then_inc(*did(f"{tag}_tile.{b}"))

        def highs(tag, T, B, H, n):
            for k in range(KT):
                act.wait_ge(*when(f"{tag}_t.{k}"))
                nc.scalar.activation(H[:, k, :], T[:, k * n:(k + 1) * n], ACT.Identity, bias=B[:, k:k + 1]).then_inc(*did(f"{tag}_hi.{k}"))

        act.sem_inc(w_high, PRIME)
        act.sem_inc(taken, PRIME)
        act.sem_inc(*led.prime("y1_tile", 4))
        act.sem_inc(*led.prime("y2_tile", 2))
        act.wait_ge(*when("in_small.all"))
        act.wait_ge(*when("eps.all"))
        nc.scalar.activation(CVEC[:, :], COL[:, 0:16 + 8 * SEGS], ACT.Silu).then_inc(*did("silu.conds"))

        for l in range(2):
            act.wait_ge(*when(f"hy_arg.{l}"))
            nc.scalar.activation([EMB2, HDN][l][0:64, :], ARG[2][:, :], ACT.Sin).then_inc(*did(f"hy_sin.{l}"))

        act.wait_ge(*when("in_x.all"))
        for k in range(KT):
            squares("n0", X[:, k * S:(k + 1) * S], S, k)
        act.wait_ge(*when("in_ctx.all"))
        for k in range(KT):
            squares("nc", CX[:, k, :], CTX, k, when(f"n0_ss.{6 + k}") if k < 2 else None)
        root("n0", 5, S, D)
        root("nc", 6, CTX, D, RSC)
        highs("n0", NORM_T, MODV0[:, 0:8], Hh, S)
        split_high(0, 0)
        highs("nc", CT_[:, :, :].rearrange("p k t -> p (k t)"), MODV0[:, 16:24], Ch, CTX)

        for b in range(4):
            next_tile(0, b)
            copy_out(0, b, z(b))
            act.wait_ge(*when(f"ckv_mm.{b}"))
            nc.scalar.activation(CKV[:, b, :], bank(5 + b % 2, CTX), ACT.Copy).then_inc(*did(f"ckv.{b}"))
        for name, q0, func in (("ev_values", 1, ACT.Copy), ("ev_gates", 3, ACT.Silu)):
            with led.loop(act, name, 2) as i:
                for b in range(4):
                    next_tile(i + q0, b)
                    copy_out(i + q0, b, Z[:, ds((i * 4 + 4 * q0 + b) * S, S)], func)
        act.wait_ge(taken, EV_IN + PRIME)

        def head_src(j):
            kind, h = R1[j]
            return (CKV[:, h, :], CTX) if kind == "ck" else (z(h) if kind == "k" else z(4 + h), S)

        def head_square(j):
            if j >= 2:
                act.wait_ge(*when(f"hn_ss.{j - 2}"))
            else:
                act.wait_ge(*when("ckv.3"))
            src, n = head_src(j)
            nc.scalar.activation(SQ[j % 2][:, 0:n], src, ACT.Square).then_inc(*did(f"hn_sq.{j}"))

        head_square(0)
        for batch in BATCHES:
            for j in batch:
                if j + 1 < NC1:
                    head_square(j + 1)
                n = head_src(j)[1]
                act.wait_ge(*when(f"hn_ss.{j}"))
                if 4 <= j < 8:
                    act.wait_ge(*when(f"hn_zn.{j - 4}"))
                nc.scalar.activation(RSS[RS_SLOT[j]][:, 0:n], bank(j % 2, n), ACT.Ln, bias=EPSC[:, :], scale=1.0 / P).then_inc(*did(f"hn_ln.{j}"))
            for j in batch:
                n = head_src(j)[1]
                rs = RSS[RS_SLOT[j]][:, 0:n]
                act.wait_ge(*when(f"hn_ln.{j}"))
                nc.scalar.activation(rs, rs, ACT.Exp, scale=-0.5).then_inc(*did(f"hn_rs.{j}"))
        for j in range(6):
            act.wait_ge(*when(f"vt_mm.{j}"))
            nc.scalar.activation(VT[:, j, :], bank(4 + j % 3, 2 * P), ACT.Copy).then_inc(*did(f"vt.{j}"))

        def copy_pt(n):
            h, i = divmod(n, 4)
            act.wait_ge(*when(f"pt_mm.{n}"))
            if h >= 2 and i == 0:
                act.wait_ge(*when(f"attn_o.{h - 2}"))
            nc.scalar.activation(PT[h % 2][:, :, i * P:(i + 1) * P], PS[:, 4 * S:4 * S + 768].rearrange("p (j q) -> p j q", j=6), ACT.Copy).then_inc(*did(f"pt.{n}"))

        for n in range(24):
            act.wait_ge(*when(f"nmax.{n}"))
            if n >= 2:
                act.wait_ge(*when(f"pt_mm.{n - 2}"))
            at0 = (n % 2) * 2 * S
            nc.scalar.activation(PR[n % 2][:, :], PS[:, at0:at0 + 768], ACT.Exp, bias=STAT[:, n:n + 1], scale=float(P) ** -0.5,
                                 accum_out=STAT[:, 32 + n:33 + n]).then_inc(*did(f"prob.{n}"))
            if n:
                copy_pt(n - 1)
        copy_pt(23)

        MIX1 = [10, 11, 4, 5, 6, 7, 8, 9]
        act.wait_ge(*when("attn_o.5"))
        for k, n in enumerate(MIX1):
            act.wait_ge(*when(f"pool_out.{k}" if k < 2 else f"attn_y.{k - 2}"))
            nc.scalar.activation(Hh[:, k, :], z(n), ACT.Copy).then_inc(*did(f"mx1_hi.{k}"))
        with led.loop(act, "ev_out", EV_OUT // 4) as i:
            for b in range(4):
                next_tile(i + 5, b)

        act.wait_ge(taken, T_OD_IN + PRIME)
        for k in range(KT):
            squares("n1", X[:, k * S:(k + 1) * S], S, k)
        root("n1", 5, S, D)
        highs("n1", NORM_T, MODV[:, 8:16], Hh, S)
        for name, q0, trips, func in (("od_values", 0, 5, ACT.Copy), ("od_gates", 5, 2, ACT.Silu)):
            with led.loop(act, name, trips) as i:
                for b in range(4):
                    next_tile(i + 7 + q0, b)
                    copy_out(i + 7 + q0, b, Z[:, ds((i * 4 + 4 * q0 + 1 + b) * S, S)], func)

        act.wait_ge(taken, T_OD_OUT + PRIME)
        def decay(n, j):
            if n or j:
                act.wait_ge(*when(f"hy_d1.{n if j else n - 1}.{(j - 1) % 4}"))
            g = STEPS[n][0]
            nc.scalar.activation(DEC[:, 0:G], DELTA[:, g * G:(g + 1) * G], ACT.Exp, scale=col("time", j)).then_inc(*did(f"hy_dec.{n}.{j}"))

        def magnitudes(n, j):
            for d in range(2):
                act.wait_ge(*when(f"hy_d{d}.{n}.{j}"))
                if j or n:
                    act.wait_ge(*when(f"hy_abs.{n if j else n - 1}.{(j - 1) % 4}.1"))
                nc.scalar.activation(MAG[:, d, :], HH[d][:, :], ACT.Abs).then_inc(*did(f"hy_mag.{n}.{j}.{d}"))

        def by_tokens(n):
            for j in range(4):
                act.wait_ge(*when(f"hy_zt_mm.{n}.{j}"))
                if n and j == 0:
                    act.wait_ge(*when(f"hz_mm.{n - 1}.1"))
                nc.scalar.activation(ZT[:, j, :], bank(4 + j, G), ACT.Copy).then_inc(*did(f"hy_zt.{n}.{j}"))

        def odd_part(kind, n, ft):
            act.wait_ge(*when(f"{kind}_mm.{n}.{ft}"))
            if ft or n:
                act.wait_ge(*when(f"{kind}_fly.{n}.3" if ft else f"{kind}_fly.{n - 1}.7"))
            for c in range(2):
                nc.scalar.activation(ODD[kind][:, c, :], bank(SPEC_BANK[kind] + 2 * c + 1, G), ACT.Copy).then_inc(*did(f"{kind}_odd.{n}.{2 * ft + c}"))

        act.wait_ge(*when("in_hy2.all"))
        for j in range(18):
            if j >= 3:
                act.wait_ge(*when(f"conv3.{j - 3}"))
            nc.scalar.activation(TAP[j % 3][:, :], z(j + 1), ACT.Identity, scale=col("conv_w", 18 + j), bias=col("conv_b", j)).then_inc(*did(f"conv_mid.{j}"))
            if j in FILTER_AT:
                decay(0, FILTER_AT.index(j))
                magnitudes(0, FILTER_AT.index(j))
        for ft in range(2):
            odd_part("hk", 0, ft)
        for n in range(len(STEPS)):
            more = n + 1 < len(STEPS)
            by_tokens(n)
            if more:
                for j in range(2):
                    decay(n + 1, j)
                    magnitudes(n + 1, j)
            odd_part("hz", n, 0)
            if more:
                for j in range(2, 4):
                    decay(n + 1, j)
                    magnitudes(n + 1, j)
            else:
                for j in range(4):
                    act.wait_ge(*when(f"fn_a.{j}"))
                    nc.scalar.activation(AB[j][:, :], bank(j), ACT.Copy).then_inc(*did(f"fn_ab.{j}"))
            odd_part("hz", n, 1)
            if more:
                for ft in range(2):
                    odd_part("hk", n + 1, ft)
        for m in range(2):
            act.wait_ge(*when(f"fn_b.{m}"))
            nc.scalar.activation(U2[:, m, :], bank(m), ACT.Copy).then_inc(*did(f"fn_u2.{m}"))
        act.wait_ge(*when("fn_y.1"))
        for k in range(KT):
            act.wait_ge(*when(f"hy_out.{1 if k < 3 else 3}.{k % 3}" if k < 6 else f"fn_out.{k - 6}"))
            nc.scalar.activation(Hh[:, k, :], z(k) if k < 6 else z(FN_T + 1 + k - 6), ACT.Copy).then_inc(*did(f"mx2_hi.{k}"))
        with led.loop(act, "od_out", OD_OUT // 4) as i:
            for b in range(4):
                next_tile(i + 14, b)
        act.wait_ge(taken, T_LAYERS + PRIME)
        for k in range(KT):
            squares("nf", X[:, k * S:(k + 1) * S], S, k)
        root("nf", 5, S, D)
        for c in range(2):
            act.wait_ge(*when(f"rot_arg.{c}"))
            nc.scalar.activation([SIN2, COS2][c], RT[c][:, :], ACT.Sin).then_inc(*did(f"rot.{c}"))

        with led.loop(act, "layers", LAYERS) as lay:
            Q = lay * (PER_LAYER // 4) + T_LAYERS // 4
            for k in range(KT):
                act.wait_ge(*when(f"nf_x.{k}"))
                squares("h1", X[:, k * S:(k + 1) * S], S, k, when(f"y2_x.{k}", back="layers"))
            root("h1", 5, S, D)
            highs("h1", NORM_T, LM[:, 0:8], Hh, S)
            with led.loop(act, "mx_in", 5) as i:
                for b in range(4):
                    next_tile(i + Q, b)
                    copy_out(i + Q, b, Z[:, ds((i * 4 + b) * S, S)])
            next_tile(Q + 5, 0)
            copy_out(Q + 5, 0, z(20))
            copy_out(Q + 5, 1, z(21))
            act.wait_ge(taken, 4 * Q + 22 + PRIME)
            act.sem_inc(w_high, 2)
            act.sem_inc(taken, 2)
            split_high(Q + 6, 0)

            for m in range(2):
                act.wait_ge(*when(f"gm_c.{m}"))
                if m == 0:
                    act.wait_ge(*when("h1_ss.7"))
                nc.scalar.activation(SQ[m][:, :], MO[:, m, :], ACT.Square).then_inc(*did(f"gm_sq.{m}"))
            for m in range(2):
                act.wait_ge(*when(f"gm_var.{m}"))
                nc.scalar.activation(P2[m][:, :], bank(2 + m), ACT.Ln, bias=EPSC[:, :], scale=1.0 / 64).then_inc(*did(f"gm_ln.{m}"))
            for m in range(2):
                act.wait_ge(*when(f"gm_ln.{m}"))
                nc.scalar.activation(P2[m][:, :], P2[m][:, :], ACT.Exp, scale=-0.5).then_inc(*did(f"gm_rs.{m}"))
            for c in range(2):
                act.wait_ge(*when(f"cmp_h.{c}"))
                nc.scalar.activation(HC[:, c, 0:31], bank((7, 4)[c], 31), ACT.Silu).then_inc(*did(f"cmp_act.{c}"))
            act.wait_ge(*when("cmp_kv.1"))
            act.wait_ge(*when("k_zero.all"))
            for r in range(2):
                rows = slice(64 * r, 64 * r + 64)
                nc.scalar.activation(KC[rows, r, 0:31], bank(2, 31, rows), ACT.Copy).then_inc(*did("cmp_k.all" if r else "cmp_k.0"))
            nc.scalar.activation(VC[0:31, :], bank(3, P, slice(0, 31)), ACT.Copy).then_inc(*did("cmp_v.all"))
            act.wait_ge(*when("gate_t.all"))
            nc.scalar.activation(GT[:, :, :], PS[:, 4 * S:5 * S].rearrange("p (j c) -> p j c", j=4)[:, :, 32:44], ACT.Sigmoid).then_inc(*did("gates.all"))
            for c in range(2):
                act.wait_ge(*when(f"v_tok_mm.{c}"))
                nc.scalar.activation([VS_, VW_][c][:, :, :], PS[:, (5 + c) * S:(6 + c) * S].rearrange("p (j c) -> p j c", j=4), ACT.Copy).then_inc(*did(f"v_tok.{c}"))

            for j in range(2):
                act.wait_ge(*when(f"gm_vt_mm.{2 * j + 1}"))
                nc.scalar.activation(GMV[:, 2 * j:2 * j + 2, :], bank(j).rearrange("p (j c) -> p j c", j=2), ACT.Copy).then_inc(*did(f"gm_vt.{j}"))

            def decay_logs():
                act.wait_ge(*when("gla_x.all"))
                act.wait_ge(*when("gla_min.all"))
                nc.scalar.activation(GE[0][:, :], GE[0][:, :], ACT.Abs).then_inc(*did("gla_abs.all"))
                act.wait_ge(*when("gla_abs.all"))
                nc.scalar.activation(GE[0][:, :], GE[0][:, :], ACT.Exp, scale=-1.0).then_inc(*did("gla_exp.all"))
                act.wait_ge(*when("gla_exp.all"))
                nc.scalar.activation(GE[0][:, :], GE[0][:, :], ACT.Ln, bias=1.0).then_inc(*did("gla_ln.all"))

            def decays():
                for c in range(4):
                    act.wait_ge(*when(f"gla_d.{min(c, 2)}"))
                    nc.scalar.activation(GE[c][:, :], (GE[c] if c < 3 else GB)[:, :], ACT.Exp, scale=1.0 / 16).then_inc(*did(f"gla_e.{c}"))
                nc.scalar.activation(DECY[:, :], GB[:, :].rearrange("p (c t) -> p c t", t=64)[:, :, 63], ACT.Exp, scale=1.0 / 16).then_inc(*did("gla_decay.all"))

            def copy_pt2(n):
                h, i, br = ITEMS[n]
                act.wait_ge(*when(f"p2t_mm.{n}"))
                if n >= 2:
                    act.wait_ge(*when(f"p2v.{n - 2}"))
                if br == 2:
                    nc.scalar.activation(PT2[n % 2][0:31, 0, :], bank(3 + n % 2, P, slice(0, 31)), ACT.Copy).then_inc(*did(f"p2t.{n}"))
                else:
                    nc.scalar.activation(PT2[n % 2][:, 0:i + 1, :], bank(3 + n % 2, (i + 1) * P).rearrange("p (j q) -> p j q", q=P), ACT.Copy).then_inc(*did(f"p2t.{n}"))

            def head_out(h):
                rows = slice(64 * (h % 2), 64 * (h % 2) + 64)
                act.wait_ge(*when(f"p2v.{12 * h + 11}"))
                nc.scalar.activation(NO[rows, h // 2, :], bank(5 + h % 2, S, rows), ACT.Copy).then_inc(*did(f"nsa_o.{h}"))

            for n, (h, i, br) in enumerate(ITEMS):
                w = WIDTH[n]
                act.wait_ge(*when(f"nmax2.{n}"))
                if n >= 4:
                    act.wait_ge(*when(f"p2t_mm.{n - 4}"))
                nc.scalar.activation(P2[n % 4][:, 0:w], bank(SCORE_BANKS[n % 4], w), ACT.Exp, bias=ST2[n % 4][:, 0:1], scale=0.125,
                                     accum_out=ST2[n % 4][:, 1:2]).then_inc(*did(f"prob2.{n}"))
                if n >= 2:
                    copy_pt2(n - 2)
                if n == 4:
                    decay_logs()
                if n == 12:
                    decays()
                if n >= 4 and (n - 4) % 12 == 11:
                    head_out((n - 4) // 12)
            copy_pt2(len(ITEMS) - 2)
            copy_pt2(len(ITEMS) - 1)
            head_out(3)

            for c in range(8):
                act.wait_ge(*when(f"gla_tok_mm.{c}"))
                nc.scalar.activation(GV[:, c, :], bank(4 + c % 2, 384, slice(0, 64)), ACT.Copy).then_inc(*did(f"gla_tok.{c}"))
            def group_squares(g, before):
                for m in range(2):
                    act.wait_ge(*when(MIXED[g]))
                    act.wait_ge(*when(before[m]))
                    nc.scalar.activation(SQ[m][:, :], (AO, NO, GO, MO)[g][:, m, :], ACT.Square).then_inc(*did(f"gr_sq.{2 * g + m}"))

            def group_log(g):
                act.wait_ge(*when(f"gr_ss.{2 * g + 1}"))
                nc.scalar.activation(GR[g][:, :], bank(GROUP_BANK[g]), ACT.Ln, bias=EPSC[:, :], scale=1.0 / 256).then_inc(*did(f"gr_ln.{g}"))

            def group_root(g):
                act.wait_ge(*when(f"gr_ln.{g}"))
                nc.scalar.activation(GR[g][:, :], GR[g][:, :], ACT.Exp, scale=-0.5).then_inc(*did(f"gr_rs.{g}"))

            group_squares(0, ("gm_var.0", "gm_var.1"))
            group_squares(3, ("gr_ss.0", "gr_ss.1"))
            group_squares(1, ("gr_ss.6", "gr_ss.7"))
            for m in range(2):
                nc.scalar.activation(z(15 + m), z(15 + m), ACT.Silu).then_inc(*did(f"gla_gate.{m}"))
            for g in (0, 3, 1):
                group_log(g)
            for g in (0, 3, 1):
                group_root(g)
            for m in range(2):
                act.wait_ge(*when(f"gla_o.{m}"))
                nc.scalar.activation(GO[:, m, :], bank(6 + m), ACT.Copy).then_inc(*did(f"gla_out.{m}"))
                act.wait_ge(*when(f"gr_ss.{2 + m}"))
                nc.scalar.activation(SQ[m][:, :], bank(6 + m), ACT.Square).then_inc(*did(f"gla_sq.{m}"))
            for m in range(2):
                act.wait_ge(*when(f"gla_ss.{m}"))
                nc.scalar.activation(GR[4 + m][:, :], bank(3 + m), ACT.Ln, bias=EPSC[:, :], scale=1.0 / 64).then_inc(*did(f"gla_rln.{m}"))
            for m in range(2):
                act.wait_ge(*when(f"gla_rln.{m}"))
                nc.scalar.activation(GR[4 + m][:, :], GR[4 + m][:, :], ACT.Exp, scale=-0.5).then_inc(*did(f"gla_rs.{m}"))
            group_squares(2, ("gla_ss.0", "gla_ss.1"))
            group_log(2)
            group_root(2)
            act.wait_ge(*when("gr_n.5"))
            for k in range(KT):
                nc.scalar.activation(Hh[:, k, :], z(k), ACT.Copy).then_inc(*did(f"mx3_hi.{k}"))
            with led.loop(act, "mx_out", 2) as i:
                for b in range(4):
                    next_tile(i + Q + 6, b)
                    square_tile("y1", bank(b), b, b % 2, w_used, 4 * Q + 4 * i + 24 + b + 1 + PRIME)
                    copy_out(i + Q + 6, b, Y[:, ds((i * 4 + b) * S, S)])
            root("y1", 5, S, D)
            for k in range(KT):
                squares("h2", X[:, k * S:(k + 1) * S], S, k, when(f"y1_x.{k}"))
            act.wait_ge(*when("y1_t.7"))
            root("h2", 6, S, D)
            highs("h2", NORM_T, LM[:, 24:32], Hh, S)
            for a in range(2):
                q0 = Q + 8 + 8 * a
                with led.loop(act, f"up{a}", 4) as i:
                    for b in range(4):
                        next_tile(i + q0, b)
                        act.wait_ge(w_used, 4 * q0 + 4 * i + b + 1 + PRIME)
                        act.wait_ge(*(when(f"hid{a}_b.{b - 2}") if b >= 2 else when(f"hid{a}_b.{b + 2}", back=f"up{a}")))
                        nc.scalar.activation(RL[b % 2][:, :], bank(b), ACT.Relu).then_inc(taken, 1)
                        act.wait_ge(taken, 4 * q0 + 4 * i + b + 1 + PRIME)
                        nc.scalar.activation(SQ[b % 2][:, :], RL[b % 2][:, :], ACT.Square).then_inc(*did(f"relu{a}.{b}"))
                with led.loop(act, f"down{a}", 4) as i:
                    for b in range(4):
                        next_tile(i + q0 + 4, b)
                        if b % 2 and a == 0:
                            act.wait_ge(w_used, 4 * q0 + 4 * i + 16 + b + 1 + PRIME)
                            nc.scalar.activation(Y[:, ds((i * 2 + b // 2) * S, S)], bank(b - 1), ACT.Copy).then_inc(taken, 2)
                        if b % 2 and a == 1:
                            square_tile("y2", Y[:, ds((i * 2 + b // 2) * S, S)], b // 2, b // 2, taken, 4 * q0 + 4 * i + 16 + b + 1 + PRIME)
            root("y2", 5, S, D)

    @block.gpsimd
    def _(pool):
        led.engine = "gpsimd"
        gp = nc.gpsimd
        pool.wait_ge(taken, EV_IN + PRIME)
        pool.wait_ge(*when("in_tabc.all"))
        for c, t in enumerate((PU, PV_, PW_)):
            gp.memset(t[:, :, :], 0.0).then_inc(*did(f"pool_z.{c}"))
        pool.wait_ge(*when("pool_z.2"))
        for m in range(2):
            gp.tensor_copy(PU[:, m, 8:8 + S], z(10 + m)).then_inc(*did(f"pool_u.{m}"))
        pool.wait_ge(*when("pool_u.1"))
        gp.tensor_tensor(PV_[:, :, 0:527], PU[:, :, 0:527], PU[:, :, 1:528], add).then_inc(*did("pool_s.2"))
        pool.wait_ge(*when("pool_s.2"))
        gp.tensor_tensor(PW_[:, :, 0:525], PV_[:, :, 0:525], PV_[:, :, 2:527], add).then_inc(*did("pool_s.4"))
        pool.wait_ge(*when("pool_s.4"))
        gp.tensor_tensor(PV_[:, 1, 0:521], PW_[:, 1, 0:521], PW_[:, 1, 4:525], add).then_inc(*did("pool_s.8"))
        pool.wait_ge(*when("pool_s.8"))
        gp.tensor_tensor(PW_[64:P, 1, 0:513], PV_[64:P, 1, 0:513], PV_[64:P, 1, 8:521], add).then_inc(*did("pool_s.16"))
        pool.wait_ge(*when("pool_s.16"))
        for g, (w, src) in enumerate(((2, PV_), (4, PW_), (8, PV_), (16, PW_))):
            m, rows = g // 2, slice(64 * (g % 2), 64 * (g % 2) + 64)
            gp.tensor_tensor(Z[rows, (10 + m) * S:(11 + m) * S], src[rows, m, 8 - w // 2:8 - w // 2 + S], INVC[rows, m * S:(m + 1) * S], mul).then_inc(*did(f"pool_m.{g}"))
        for g in range(4):
            m, rows = g // 2, slice(64 * (g % 2), 64 * (g % 2) + 64)
            pool.wait_ge(*when(f"pool_m.{g}"))
            gp.tensor_tensor(Z[rows, (10 + m) * S:(11 + m) * S], Z[rows, (10 + m) * S:(11 + m) * S], PU[rows, m, 8:8 + S], sub).then_inc(*did("pool_d.all" if g == 3 else f"pool_d.{g}"))
        with led.loop(pool, "layers", LAYERS) as lay:
            pool.wait_ge(taken, lay * PER_LAYER + (T_LAYERS + L_OUT + PRIME))
            pool.sem_inc(passed, 1)
            for c in range(2):
                gp.memset(K2[c][:, :, :], 0.0).then_inc(*did(f"k_zero.{c}"))
            gp.memset(KC[:, :, :], 0.0).then_inc(*did("k_zero.all"))
            gp.memset(GS[:, :, :], 0.0).then_inc(*did("gla_zero.0"))
            gp.memset(GA[:, :, :], 0.0).then_inc(*did("gla_zero.1"))

    @block.vector
    def _(dve):
        led.engine = "vector"
        v = nc.vector

        def split_low(q, b):
            dve.wait_ge(w_high, 4 * q + b + 1 + PRIME)
            v.tensor_tensor(WL[b % 2][:, :, :].rearrange("p k c -> p (k c)"), RAW[b // 2][:, b % 2, :],
                            WH[b % 2][:, :, :].rearrange("p k c -> p (k c)").bitcast(f32), sub).then_inc(w_low, 1)

        def next_tile(q, b):
            split_low(q + 1 if b == 3 else q, (b + 1) % 4)

        def unit(q, k):
            dve.wait_ge(mod_loaded[k % 4], 16 * (2 * q + k // 4 + 5))
            if k:
                dve.wait_ge(mod_used, 8 * q + 16 + k + PRIME)
            else:
                dve.wait_ge(mod_summed, q + 2)
            c = CVEC[:, ds(q * 8 + 16 + k, 1)]
            if k:
                v.scalar_tensor_tensor(ACC[:, :], MOD[k % 4][:, :], c, ACC[:, :], mul, add).then_inc(mod_used, 1)
            else:
                v.tensor_scalar(ACC[:, :], MOD[k % 4][:, :], c, None, mul).then_inc(mod_used, 1)

        def side(q, b):
            next_tile(q, b)
            for k in UNITS_AT[b]:
                unit(q, k)
            if b == 3:
                dve.wait_ge(mod_summed, q + 3)
                v.tensor_tensor(MODV[:, ds(q * 8, 8)], bank(4, 8), COL[:, ds(q * 8 + COLS["b_mod"][0], 8)], add).then_inc(mod_taken, 1)

        def to_halves(tag, src, A_, B, T, L, H, n, rs=RS):
            for k in range(KT + 1):
                if k < KT:
                    v.scalar_tensor_tensor(T[:, k * n:(k + 1) * n], src(k), A_[:, k:k + 1], rs[:, 0:n], mul, mul).then_inc(*did(f"{tag}_t.{k}"))
                if k:
                    dve.wait_ge(*when(f"{tag}_hi.{k - 1}"))
                    v.scalar_tensor_tensor(L[:, k - 1, :], T[:, (k - 1) * n:k * n], B[:, k - 1:k], H[:, k - 1, :].bitcast(f32), add, sub).then_inc(*did(f"{tag}_lo.{k - 1}"))

        def zero_squares(tag):
            v.memset(SQ[1][:, :], 0.0).then_inc(*did(f"{tag}_zero.1"))

        def lows(tag, srcs):
            for k, src in enumerate(srcs):
                dve.wait_ge(*when(f"{tag}_hi.{k}"))
                v.tensor_tensor(Hl[:, k, :], src, Hh[:, k, :].bitcast(f32), sub).then_inc(*did(f"{tag}_lo.{k}"))

        dve.sem_inc(w_low, PRIME)
        dve.sem_inc(mod_used, PRIME + UNITS)
        dve.sem_inc(*led.prime("hid0_b", 4))
        dve.sem_inc(*led.prime("hid1_b", 4))
        dve.sem_inc(*led.prime("y2_x", 8))
        v.memset(EPSC[:, :], EPS).then_inc(*did("eps.all"))

        def reduce_angle(tag, part, arg, tmp, out, shift=0.0):
            steps = [lambda: v.tensor_scalar(tmp, arg, 1.0 / (2 * np.pi), 0.25 if shift else 0.0, mul, add),
                     lambda: v.tensor_scalar(tmp, tmp, ROUND, -ROUND, add, add),
                     lambda: v.scalar_tensor_tensor(out, tmp, -TURN[0], arg, mul, add),
                     lambda: v.scalar_tensor_tensor(out, tmp, -TURN[1], out, mul, add),
                     lambda: v.scalar_tensor_tensor(out, tmp, -TURN[2], out, mul, add),
                     lambda: v.tensor_scalar(out, out, shift, PI_IN, add, ALU.min)]
            for k, step in enumerate(steps):
                step().then_inc(*did(f"{part}.{k}"))
                dve.wait_ge(*when(f"{part}.{k}"))
            v.tensor_scalar(out, out, -PI_IN, None, ALU.max).then_inc(*did(tag))

        v.memset(HDN[64:P, :], 0.0).then_inc(*did("hy_zero.0"))
        for l in range(2):
            dve.wait_ge(*when(f"hy_hid.{l}"))
            if l:
                dve.wait_ge(*when("hy_sin.0"))
            v.tensor_scalar(ARG[0][:, :], bank(l, S, slice(0, 64)), col(f"hy_b{l + 1}", rows=64), col("freq", rows=64), add, mul).then_inc(*did(f"hy_pre.{l}"))
            dve.wait_ge(*when(f"hy_pre.{l}"))
            reduce_angle(f"hy_arg.{l}", f"hy_red{l}", ARG[0][:, :], ARG[1][:, :], ARG[2][:, :])

        dve.wait_ge(*when("silu.conds"))
        for k in range(UNITS):
            u = 2 * k + 1
            dve.wait_ge(mod_loaded[u % 4], 16 * (u // 4 + 1))
            if k:
                dve.wait_ge(mod_used, UNITS + k + PRIME)
            for j, acc in enumerate(ACC0):
                c = CVEC[:, 8 * j + k:8 * j + k + 1]
                if k:
                    ins = v.scalar_tensor_tensor(acc[:, :], MOD[u % 4][:, :], c, acc[:, :], mul, add)
                else:
                    ins = v.tensor_scalar(acc[:, :], MOD[u % 4][:, :], c, None, mul)
                ins.then_inc(*((mod_used, 1) if j else did(f"mod0.{k}")))
        dve.wait_ge(*when(f"shift.{UNITS - 1}"))
        dve.wait_ge(mod_summed, 2)
        for s, sums in enumerate((bank(7, 16).rearrange("p (n j) -> p j n", j=2), bank(4, 16).rearrange("p (j n) -> p j n", j=2))):
            for j in range(2):
                ins = v.tensor_tensor(MODV0[:, 16 * j + 8 * s:16 * j + 8 * s + 8], sums[:, j, :], col("b_mod0", 8 * s, 8), add)
                ins.then_inc(*((mod_taken, 1) if j else did(f"mod0_b.{s}")))
        dve.wait_ge(mod_taken, 2)
        for j in range(2):
            v.scalar_tensor_tensor(AFF[:, 8 * j:8 * j + 8], MODV0[:, 16 * j + 8:16 * j + 16], 1.0, col("g0", 0, 8), add, mul).then_inc(*did(f"gain0.{j}"))
        dve.wait_ge(*when("gain0.1"))
        dve.wait_ge(*when("n0_rs.all"))
        to_halves("n0", lambda k: X[:, k * S:(k + 1) * S], AFF[:, 0:8], MODV0[:, 0:8], NORM_T, Hl, Hh, S)
        split_low(0, 0)
        dve.wait_ge(*when("nc_rs.all"))
        to_halves("nc", lambda k: CX[:, k, :], AFF[:, 8:16], MODV0[:, 16:24], CT_[:, :, :].rearrange("p k t -> p (k t)"), Cl, Ch, CTX, RSC)
        for b in range(4):
            side(0, b)
        with led.loop(dve, "ev_in", EV_IN // 4 - 1) as i:
            for b in range(4):
                side(i + 1, b)

        def head_norm(j):
            kind, h = R1[j]
            dve.wait_ge(*when(f"hn_rs.{j}"))
            gain = col("q_g") if kind == "q" else col("k_g")
            if kind == "ck":
                v.scalar_tensor_tensor(KALL[:, h, 0:CTX], CKV[:, h, :], gain, RSS[RS_SLOT[j]][:, 0:CTX], mul, mul).then_inc(*did(f"hn_zn.{j}"))
            else:
                if j >= 4:
                    dve.wait_ge(*when(f"hn_rot.{j - 2}"))
                src = z(h) if kind == "k" else z(4 + h)
                v.scalar_tensor_tensor(ZN[j % 2][:, :], src, gain, RSS[RS_SLOT[j]][:, :], mul, mul).then_inc(*did(f"hn_zn.{j}"))

        def head_rope(j):
            kind, h = R1[j]
            if kind == "ck":
                return
            v.tensor_tensor(RA[j % 2][:, :], ZN[j % 2][:, :], COS0, mul).then_inc(*did(f"hn_ra.{j}"))
            dve.wait_ge(*when(f"hn_rot.{j}"))
            v.tensor_tensor(RB[j % 2][:, :], bank(2 + j % 2), SIN0, mul).then_inc(*did(f"hn_rb.{j}"))
            dve.wait_ge(*when(f"hn_rb.{j}"))
            dst = KALL[:, h, CTX:CTX + S] if kind == "k" else z(4 + h)
            v.tensor_tensor(dst, RA[j % 2][:, :], RB[j % 2][:, :], add).then_inc(*did(f"hn_out.{j}"))

        dve.wait_ge(*when("in_tabc.all"))
        dve.wait_ge(*when("ckv.3"))
        head_norm(0)
        for j in range(1, NC1):
            head_norm(j)
            if j > 2:
                dve.wait_ge(*when(f"hn_zn.{j - 1}"))
            head_rope(j - 1)
        head_rope(NC1 - 1)

        def normalise(n):
            dve.wait_ge(*when(f"prob.{n}"))
            v.reciprocal(STAT[:, 32 + n:33 + n], STAT[:, 32 + n:33 + n]).then_inc(*did(f"rsum.{n}"))
            dve.wait_ge(*when(f"rsum.{n}"))
            v.tensor_scalar(PR[n % 2][:, :], PR[n % 2][:, :], STAT[:, 32 + n:33 + n], None, mul).then_inc(*did(f"pnorm.{n}"))

        def head_gate(h):
            dve.wait_ge(*when(f"attn_o.{h}"))
            v.tensor_tensor(z(4 + h), bank(6 + h % 2), z(14 + h), mul).then_inc(*did(f"attn_y.{h}"))

        for n in range(24):
            if n:
                normalise(n - 1)
            dve.wait_ge(*when(f"score.{n}"))
            at0 = (n % 2) * 2 * S
            v.reduce_max(STAT[:, n:n + 1], PS[:, at0:at0 + 768], AX.X).then_inc(*did(f"rmax.{n}"))
            dve.wait_ge(*when(f"rmax.{n}"))
            v.tensor_scalar(STAT[:, n:n + 1], STAT[:, n:n + 1], -float(P) ** -0.5, None, mul).then_inc(*did(f"nmax.{n}"))
            if n >= 6 and n % 4 == 2:
                head_gate((n - 6) // 4)
        normalise(23)
        head_gate(5)
        for m in range(2):
            dve.wait_ge(*when(f"pool_y.{m}"))
            v.scalar_tensor_tensor(z(10 + m), bank(4 + m), col("pool_scale", m), z(12 + m), mul, mul).then_inc(*did(f"pool_out.{m}"))
        lows("mx1", [z(n) for n in (10, 11, 4, 5, 6, 7, 8, 9)])

        def residual(q, i, b, gate0):
            dve.wait_ge(w_used, 4 * q + b + 1 + PRIME)
            n = i * 4 + b
            v.scalar_tensor_tensor(X[:, ds(n * S, S)], bank(b), MODV[:, ds(n + gate0, 1)], X[:, ds(n * S, S)], mul, add).then_inc(taken, 1)

        dve.wait_ge(mod_taken, 3)
        with led.loop(dve, "ev_out", EV_OUT // 4) as i:
            for b in range(4):
                side(i + 5, b)
                residual(i + 5, i, b, 0)

        dve.wait_ge(mod_taken, 6)
        v.scalar_tensor_tensor(AFF[:, 0:8], MODV[:, 16:24], 1.0, col("g1", 0, 8), add, mul).then_inc(*did("gain1.all"))
        dve.wait_ge(*when("gain1.all"))
        dve.wait_ge(*when("n1_rs.all"))
        to_halves("n1", lambda k: X[:, k * S:(k + 1) * S], AFF[:, 0:8], MODV[:, 8:16], NORM_T, Hl, Hh, S)
        with led.loop(dve, "od_in", OD_IN // 4) as i:
            for b in range(4):
                side(i + 7, b)

        dve.wait_ge(w_used, T_OD_OUT + PRIME)
        v.memset(W3[64:P, :], 0.0).then_inc(*did("hy_zero.1"))

        def filter_tile(n, j):
            for d in range(2):
                dve.wait_ge(*when(f"hy_filt.{n}.{2 * j + d}"))
                if d == 0:
                    dve.wait_ge(*when(f"hy_dec.{n}.{j}"))
                if j or n:
                    dve.wait_ge(*when(f"hy_abs.{n if j else n - 1}.{(j - 1) % 4}.1"))
                v.tensor_tensor(HH[d][:, :], bank(2 * (j % 2) + d, G), DEC[:, 0:G], mul).then_inc(*did(f"hy_d{d}.{n}.{j}"))
            dve.wait_ge(*when(f"hy_d1.{n}.{j}"))
            if n:
                dve.wait_ge(*when(f"hk_mm.{n - 1}.1"))
                dve.wait_ge(*when(f"hy_norm_mm.{n - 1}"))
            v.tensor_tensor(FSUM[:, j, :], HH[0][:, :], HH[1][:, :], add).then_inc(*did(f"hy_sd.{n}.{j}.0"))
            v.tensor_tensor(FDIFF[:, j, :], HH[0][:, :], HH[1][:, :], sub).then_inc(*did(f"hy_sd.{n}.{j}.1"))
            if j == 0:
                dve.wait_ge(*when(f"hy_sd.{n}.{j}.0"))
                v.tensor_copy(FSUM[0:1, 0, :], HH[0][0:1, :]).then_inc(*did(f"hy_lag0.{n}"))
            for d in range(2):
                dve.wait_ge(*when(f"hy_mag.{n}.{j}.{d}"))
                if j:
                    v.tensor_tensor(ABSA[:, 0:G], ABSA[:, 0:G], MAG[:, d, :], add).then_inc(*did(f"hy_abs.{n}.{j}.{d}"))
                    dve.wait_ge(*when(f"hy_abs.{n}.{j}.{d}"))
            if j == 0:
                v.tensor_tensor(ABSA[:, 0:G], MAG[:, 0, :], MAG[:, 1, :], add).then_inc(*did(f"hy_abs.{n}.{j}.1"))

        def filter_norm(n):
            inv = HINV[n % 2]
            dve.wait_ge(*when(f"hy_norm_mm.{n}"))
            if n >= 2:
                dve.wait_ge(*when(f"hy_out.{n - 2}.2"))
            v.tensor_scalar(inv, bank(0, 3), 512.0, 512.0 * EPS, mul, add).then_inc(*did(f"hy_inv_a.{n}"))
            dve.wait_ge(*when(f"hy_inv_a.{n}"))
            v.reciprocal(inv, inv).then_inc(*did(f"hy_inv_b.{n}"))

        def spectrum(kind, n, ft):
            dst = KSP[n % 2] if kind == "hk" else GSP
            if kind == "hz" and n and ft == 0:
                dve.wait_ge(*when(f"hy_inv.{n - 1}.2"))
            if kind == "hk" and n >= 2 and ft == 0:
                dve.wait_ge(*when(f"hg_s.{n - 2}.1.3"))
            for c in range(2):
                dve.wait_ge(*when(f"{kind}_odd.{n}.{2 * ft + c}"))
                even, odd = bank(SPEC_BANK[kind] + 2 * c, G), ODD[kind][:, c, :]
                v.tensor_tensor(dst[:, ft, 2 * c, :], even, odd, add).then_inc(*did(f"{kind}_fly.{n}.{4 * ft + 2 * c}"))
                if c == 0:
                    v.tensor_tensor(dst[:, ft, 1, :], even, odd, sub).then_inc(*did(f"{kind}_fly.{n}.{4 * ft + 1}"))
                else:
                    v.scalar_tensor_tensor(dst[:, ft, 3, :], even, -1.0, odd, mul, add).then_inc(*did(f"{kind}_fly.{n}.{4 * ft + 3}"))

        def products(n, ft):
            K_ = lambda c: KSP[n % 2][:, ft, c:c + 2, :]
            G_ = lambda c: GSP[:, ft, c:c + 2, :]
            tmp = lambda m: PM[:, 2 * m:2 * m + 2, :]
            dve.wait_ge(*when(f"hz_fly.{n}.{4 * ft + 3}"))
            dve.wait_ge(*when(f"hk_fly.{n}.7"))
            if ft:
                dve.wait_ge(*when(f"hg_s.{n}.0.3"))
            elif n:
                dve.wait_ge(*when(f"hy_out.{n - 1}.2"))
            for m, (a, b_) in enumerate(((0, 0), (2, 2), (0, 2), (2, 0))):
                v.tensor_tensor(tmp(m), K_(a), G_(b_), mul).then_inc(*did(f"hg_m.{n}.{ft}.{m}"))
            dve.wait_ge(*when(f"hg_m.{n}.{ft}.3"))
            v.tensor_tensor(tmp(0), tmp(0), tmp(1), sub).then_inc(*did(f"hg_a.{n}.{ft}.0"))
            v.tensor_tensor(tmp(2), tmp(2), tmp(3), add).then_inc(*did(f"hg_a.{n}.{ft}.1"))
            re, im = [(lambda c, m=m: PM[:, 2 * m + c, :]) for m in (0, 2)]
            dve.wait_ge(*when(f"hg_a.{n}.{ft}.1"))
            v.tensor_tensor(GSP[:, ft, 0, :], re(0), re(1), add).then_inc(*did(f"hg_s.{n}.{ft}.0"))
            v.tensor_tensor(GSP[:, ft, 1, :], re(0), re(1), sub).then_inc(*did(f"hg_s.{n}.{ft}.1"))
            v.tensor_tensor(GSP[:, ft, 2, :], im(0), im(1), sub).then_inc(*did(f"hg_s.{n}.{ft}.2"))
            v.tensor_tensor(GSP[:, ft, 3, :], im(0), im(1), add).then_inc(*did(f"hg_s.{n}.{ft}.3"))

        def output(n, c):
            g, o = STEPS[n]
            zt, gate = z(3 * g + c), z([X1_T, X2_T][o] + 3 * g + c)
            dve.wait_ge(*when(f"hy_inv.{n}.{c}"))
            dve.wait_ge(*when(f"hy_out.{n}.{c - 1}" if c else f"hg_s.{n}.1.3"))
            y = PMY[c % 2][:, :]
            v.tensor_scalar(y.rearrange("p (m e) -> p e m", e=2), bank(4 + c).rearrange("p (e m) -> p e m", e=2), HINV[n % 2][:, c:c + 1], None, mul).then_inc(*did(f"hy_y.{n}.{c}.0"))
            dve.wait_ge(*when(f"hy_y.{n}.{c}.0"))
            v.scalar_tensor_tensor(y, zt, col("skip", 6 * o + 3 * g + c), y, mul, add).then_inc(*did(f"hy_y.{n}.{c}.1"))
            dve.wait_ge(*when(f"hy_y.{n}.{c}.1"))
            if o == 0:
                v.tensor_tensor(zt, y, gate, mul).then_inc(*did(f"hy_out.{n}.{c}"))
            else:
                v.tensor_tensor(y, y, gate, mul).then_inc(*did(f"hy_y.{n}.{c}.2"))
                dve.wait_ge(*when(f"hy_y.{n}.{c}.2"))
                v.tensor_tensor(zt, y, z(HG_T + 1 + 3 * g + c), mul).then_inc(*did(f"hy_out.{n}.{c}"))

        for j in range(18):
            dve.wait_ge(*when(f"conv_mid.{j}"))
            tap = TAP[j % 3]
            v.scalar_tensor_tensor(tap[:, 1:S], z(j + 1)[:, 0:S - 1], col("conv_w", j), tap[:, 1:S], mul, add).then_inc(*did(f"conv1.{j}"))
            dve.wait_ge(*when(f"conv1.{j}"))
            v.tensor_copy(z(j)[:, S - 1:S], tap[:, S - 1:S]).then_inc(*did(f"conv2.{j}"))
            v.scalar_tensor_tensor(z(j)[:, 0:S - 1], z(j + 1)[:, 1:S], col("conv_w", 36 + j), tap[:, 0:S - 1], mul, add).then_inc(*did(f"conv3.{j}"))
            if j in FILTER_AT:
                filter_tile(0, FILTER_AT.index(j))
        filter_norm(0)
        for ft in range(2):
            spectrum("hk", 0, ft)
        for n in range(len(STEPS)):
            more = n + 1 < len(STEPS)
            if more:
                filter_tile(n + 1, 0)
                filter_tile(n + 1, 1)
            spectrum("hz", n, 0)
            if more:
                filter_tile(n + 1, 2)
                filter_tile(n + 1, 3)
                filter_norm(n + 1)
            products(n, 0)
            spectrum("hz", n, 1)
            if more:
                spectrum("hk", n + 1, 0)
            products(n, 1)
            if more:
                spectrum("hk", n + 1, 1)
            for c in range(3):
                output(n, c)
        for m in range(2):
            dve.wait_ge(*when(f"fn_y.{m}"))
            v.tensor_tensor(z(FN_T + 1 + m), bank(2 + m), z(FG_T + 1 + m), mul).then_inc(*did(f"fn_out.{m}"))
        dve.wait_ge(*when("hy_out.3.2"))
        lows("mx2", [z(k) if k < 6 else z(FN_T + 1 + k - 6) for k in range(KT)])
        with led.loop(dve, "od_out", OD_OUT // 4) as i:
            for b in range(4):
                side(i + 14, b)
                residual(i + 14, i, b, 24)

        dve.wait_ge(w_used, T_LAYERS + PRIME)
        dve.wait_ge(*when("in_pos.all"))
        v.tensor_copy(NORM_T[:, 0:S], POSI[:, :]).then_inc(*did("rot_pos.f"))
        dve.wait_ge(*when("rot_pos.f"))
        v.tensor_scalar(NORM_T[:, S:2 * S], NORM_T[:, 0:S], col("inv_freq"), None, mul).then_inc(*did("rot_pos.angle"))
        dve.wait_ge(*when("rot_pos.angle"))
        reduce_angle("rot_arg.0", "rot_red0", NORM_T[:, S:2 * S], NORM_T[:, 2 * S:3 * S], RT[0][:, :])
        reduce_angle("rot_arg.1", "rot_red1", NORM_T[:, S:2 * S], NORM_T[:, 3 * S:4 * S], RT[1][:, :], float(np.float32(np.pi / 2)))
        dve.wait_ge(*when("nf_rs.all"))
        for k in range(KT):
            v.scalar_tensor_tensor(X[:, k * S:(k + 1) * S], X[:, k * S:(k + 1) * S], col("final_g", k), RS[:, :], mul, mul).then_inc(*did(f"nf_x.{k}"))

        with led.loop(dve, "layers", LAYERS) as lay:
            Q = lay * (PER_LAYER // 4) + T_LAYERS // 4
            dve.wait_ge(*when("nf_x.7"))
            dve.wait_ge(*when("y2_x.7", back="layers"))
            v.tensor_copy(LM[:, :], MODV[:, ds(lay * 48 + 32, 48)]).then_inc(*did("layer_cols.mod"))
            v.tensor_copy(LG[:, :], COL[:, ds(lay * 32 + COLS["g2"][0], 32)]).then_inc(*did("layer_cols.gain"))
            dve.wait_ge(*when("layer_cols.gain"))
            for c, (m, how) in enumerate(((8, True), (16, False), (32, True), (40, False))):
                g = LG[:, 8 * c:8 * c + 8]
                if how:
                    v.scalar_tensor_tensor(AF2[:, 8 * c:8 * c + 8], LM[:, m:m + 8], 1.0, g, add, mul).then_inc(*did(f"layer_aff.{c}"))
                else:
                    v.tensor_tensor(AF2[:, 8 * c:8 * c + 8], LM[:, m:m + 8], g, mul).then_inc(*did(f"layer_aff.{c}"))
            dve.wait_ge(*when("layer_aff.3"))
            dve.wait_ge(*when("h1_rs.all"))
            to_halves("h1", lambda k: X[:, k * S:(k + 1) * S], AF2[:, 0:8], LM[:, 0:8], NORM_T, Hl, Hh, S)
            with led.loop(dve, "mx_in", 5) as i:
                for b in range(4):
                    next_tile(i + Q, b)
            next_tile(Q + 5, 0)
            dve.wait_ge(w_loaded[1], 16 * (Q + 5) + 16)
            dve.wait_ge(w_low, 4 * Q + 22 + PRIME)
            for c in range(2):
                v.tensor_copy(PAR[:, c * D:(c + 1) * D], RAW[1][:, c, :]).then_inc(w_low, 1)
            dve.wait_ge(w_low, 4 * Q + 24 + PRIME)
            dve.wait_ge(taken, 4 * Q + 24 + PRIME)
            split_low(Q + 6, 0)

            for m in range(2):
                dve.wait_ge(*when(f"gm_mean.{m}"))
                v.scalar_tensor_tensor(MO[:, m, :], bank(m), -1.0 / 64, z(19 + m), mul, add).then_inc(*did(f"gm_c.{m}"))
            for g in range(4):
                v.tensor_tensor(par("ws", P * g, P), par("ws", P * g, P), TRIL, mul).then_inc(*did(f"gm_w.{g}"))
            for c in range(2):
                dve.wait_ge(*when(f"cmp_dup.{c}"))
                for r in range(2):
                    rows = slice(64 * r, 64 * r + 64)
                    v.tensor_tensor(TP[rows, c, :, :], bank(5 + c, S, rows)[:, 16 * r:16 * r + 496].rearrange("p (n j) -> p j n", j=16),
                                    par("pos", 16 * c, 16, rows).rearrange("p (j o) -> p j o", o=1).to_broadcast([64, 16, 31]), add).then_inc(*did(f"cmp_in.{2 * c + r}"))
            for m in range(2):
                v.tensor_tensor(z(4 + m), z(4 + m), z(m), mul).then_inc(*did(f"conv_z.{m}"))
            for m in range(2):
                dve.wait_ge(*when(f"conv_z.{m}"))
                v.tensor_scalar(AO[:, m, :], z(4 + m), par("conv", 4 + m), None, mul).then_inc(*did(f"conv_c.{m}"))
            for m in range(2):
                dve.wait_ge(*when(f"conv_c.{m}"))
                v.scalar_tensor_tensor(AO[:, m, 1:S], z(4 + m)[:, 0:S - 1], par("conv", 2 + m), AO[:, m, 1:S], mul, add).then_inc(*did(f"conv_d.{m}"))
            for m in range(2):
                dve.wait_ge(*when(f"conv_d.{m}"))
                v.scalar_tensor_tensor(AO[:, m, 2:S], z(4 + m)[:, 0:S - 2], par("conv", m), AO[:, m, 2:S], mul, add).then_inc(*did(f"conv_e.{m}"))
            for m in range(2):
                dve.wait_ge(*when(f"conv_e.{m}"))
                v.tensor_tensor(AO[:, m, :], AO[:, m, :], z(2 + m), mul).then_inc(*did("conv_y.all" if m else "conv_y.0"))

            for c in range(4):
                if c < 2:
                    v.tensor_tensor(RT[0][:, :], z(6 + c), COS2, mul).then_inc(*did(f"rp_a.{c}"))
                else:
                    dve.wait_ge(*when(f"rp_dup.{c}"))
                    v.tensor_tensor(RT[0][:, :], bank(5), COS2, mul).then_inc(*did(f"rp_a.{c}"))
                dve.wait_ge(*when(f"rp_rot.{c}"))
                v.tensor_tensor(RT[1][:, :], bank(ROT_BANKS[c]), SIN2, mul).then_inc(*did(f"rp_b.{c}"))
                dve.wait_ge(*when(f"rp_b.{c}"))
                if c < 2:
                    v.tensor_tensor(QR[:, c, :], RT[0][:, :], RT[1][:, :], add).then_inc(*did(f"rp.{c}"))
                else:
                    dve.wait_ge(*when("k_zero.all"))
                    v.tensor_tensor(K2[c - 2][0:64, 0, :], RT[0][0:64, :], RT[1][0:64, :], add).then_inc(*did(f"rp_even.{c}"))
                    v.tensor_tensor(K2[c - 2][64:P, 1, :], RT[0][64:P, :], RT[1][64:P, :], add).then_inc(*did(f"rp.{c}"))
                dve.wait_ge(*when(f"rp.{c}"))

            for m in range(2):
                dve.wait_ge(*when(f"gm_rs.{m}"))
                v.tensor_tensor(MO[:, m, :], MO[:, m, :], P2[m][:, :], mul).then_inc(*did(f"gm_n.{m}"))
            for m in range(2):
                dve.wait_ge(*when(f"gm_mm.{m}"))
                for j in range(4):
                    v.tensor_tensor(MO[:, m, j * P:(j + 1) * P], bank(2 + m)[:, j * P:(j + 1) * P], par("gm_b", m * P, P), add).then_inc(*did(f"gm_t.{4 * m + j}"))
            for m in range(2):
                dve.wait_ge(*when(f"gm_t.{4 * m + 3}"))
                v.tensor_tensor(MO[:, m, :], MO[:, m, :], z(17 + m), mul).then_inc(*did("gm_y.1" if m else "gm_y.0"))

            dve.wait_ge(*when("gla_pre.all"))
            v.tensor_scalar(GE[0][:, :], bank(7), par("gate_b"), None, add).then_inc(*did("gla_x.all"))
            dve.wait_ge(*when("gla_x.all"))
            v.tensor_scalar(GM[:, :], GE[0][:, :], 0.0, None, ALU.min).then_inc(*did("gla_min.all"))

            def decay_sums():
                dve.wait_ge(*when("gla_ln.all"))
                dve.wait_ge(*when("gla_min.all"))
                v.tensor_tensor(GM[:, :], GM[:, :], GE[0][:, :], sub).then_inc(*did("gla_log.all"))
                dve.wait_ge(*when("gla_log.all"))
                v.tensor_tensor_scan(GB[:, :], SCANM, GM[:, :], 0.0, mul, add).then_inc(*did("gla_b.all"))
                dve.wait_ge(*when("gla_b.all"))
                B3 = GB[:, :].rearrange("p (c t) -> p c t", t=64)
                mid, last = (B3[:, :, k:k + 1].to_broadcast([P, 8, 64]) for k in (32, 63))
                e3 = [GE[c][:, :].rearrange("p (c t) -> p c t", t=64) for c in range(3)]
                v.tensor_tensor(e3[0], B3, mid, sub).then_inc(*did("gla_d.0"))
                v.tensor_tensor(e3[1], mid, B3, sub).then_inc(*did("gla_d.1"))
                v.tensor_tensor(e3[2], last, B3, sub).then_inc(*did("gla_d.2"))

            def decay_products():
                for c, (n, scale) in enumerate(((11, 32 ** -0.5), (12, 1.0), (12, 1.0), (11, 32 ** -0.5))):
                    dve.wait_ge(*when(f"gla_e.{c}"))
                    v.scalar_tensor_tensor(GE[c][:, :], z(n), scale, GE[c][:, :], mul, mul).then_inc(*did(f"gla_m.{c}"))

            def normalise2(n):
                h, i, br = ITEMS[n]
                st = ST2[n % 4]
                dve.wait_ge(*when(f"prob2.{n}"))
                v.reciprocal(st[:, 2:3], st[:, 1:2]).then_inc(*did(f"rsum2.{n}"))
                gate = GT[:, i, 3 * h + (br + 1) % 3:3 * h + (br + 1) % 3 + 1]
                dve.wait_ge(*when(f"rsum2.{n}"))
                if br == 2 and i == 0:
                    v.tensor_scalar(st[:, 3:4], st[:, 2:3], gate, col("row_valid", 0), mul, mul).then_inc(*did(f"rfac2.{n}"))
                else:
                    v.tensor_scalar(st[:, 3:4], st[:, 2:3], gate, None, mul).then_inc(*did(f"rfac2.{n}"))
                dve.wait_ge(*when(f"rfac2.{n}"))
                v.tensor_scalar(P2[n % 4][:, 0:WIDTH[n]], P2[n % 4][:, 0:WIDTH[n]], st[:, 3:4], None, mul).then_inc(*did(f"pnorm2.{n}"))

            dve.wait_ge(*when("gates.all"))
            for n, (h, i, br) in enumerate(ITEMS):
                w, st = WIDTH[n], ST2[n % 4]
                dve.wait_ge(*when(f"score2.{n}"))
                part, bias = (bank(SCORE_BANKS[n % 4], 31), CMPB[:, 32 * i:32 * i + 31]) if br == 2 else (bank(SCORE_BANKS[n % 4])[:, w - P:w], BIAS)
                v.tensor_tensor(part, part, bias, add).then_inc(*did(f"mask2.{n}"))
                dve.wait_ge(*when(f"mask2.{n}"))
                v.reduce_max(st[:, 0:1], bank(SCORE_BANKS[n % 4], w), AX.X).then_inc(*did(f"rmax2.{n}"))
                dve.wait_ge(*when(f"rmax2.{n}"))
                v.tensor_scalar(st[:, 0:1], st[:, 0:1], -0.125, None, mul).then_inc(*did(f"nmax2.{n}"))
                if n:
                    normalise2(n - 1)
                if n == 8:
                    decay_sums()
                if n == 16:
                    decay_products()
            normalise2(len(ITEMS) - 1)

            dve.wait_ge(*when("gla_zero.1"))
            dve.sem_inc(passed, 1)
            for h in range(4):
                dve.wait_ge(*when("in_tab2.all"))
                dve.wait_ge(*when(f"gla_att_mm.{h}"))
                dve.sem_inc(passed, 1)
                v.copy_predicated(GA[:, h, :], GMASK[:, :], bank(h, S, slice(0, 64))).then_inc(*did(f"gla_att.{h}"))
            for c in range(7):
                dve.wait_ge(*when(f"gla_kv.{c}"))
                if c:
                    dve.wait_ge(*when(f"gla_st.{c - 1}.3"))
                else:
                    dve.wait_ge(*when("gla_decay.all"))
                for h in range(4):
                    rows, cols_ = slice(32 * h, 32 * h + 32), slice(64 * h, 64 * h + 64)
                    if c:
                        v.scalar_tensor_tensor(GS[rows, c + 1, cols_], GS[rows, c, cols_], DECY[rows, c:c + 1], bank(4 + c % 2)[rows, cols_], mul, add).then_inc(*did(f"gla_st.{c}.{h}"))
                    else:
                        v.tensor_copy(GS[rows, 1, cols_], bank(4)[rows, cols_]).then_inc(*did(f"gla_st.{c}.{h}"))
            def group_norm(g):
                dve.wait_ge(*when(f"gr_rs.{g}"))
                for m in range(2):
                    src = (AO, NO, GO, MO)[g][:, m, :]
                    v.scalar_tensor_tensor(z(2 * g + m), src, par("gain", 2 * g + m), GR[g][:, :], mul, mul).then_inc(*did(f"gr_n.{2 * g + m}"))

            for g in (0, 3, 1):
                group_norm(g)
            for m in range(2):
                dve.wait_ge(*when(f"gla_rs.{m}"))
                v.tensor_tensor(GO[:, m, :], GO[:, m, :], GR[4 + m][:, :], mul).then_inc(*did(f"gla_n.{m}"))
                dve.wait_ge(*when(f"gla_n.{m}"))
                v.tensor_tensor(GO[:, m, :], GO[:, m, :], z(15 + m), mul).then_inc(*did(f"gla_y.{m}"))
            group_norm(2)
            lows("mx3", [z(k) for k in range(KT)])
            zero_squares("y1")
            with led.loop(dve, "mx_out", 2) as i:
                for b in range(4):
                    next_tile(i + Q + 6, b)

            def add_branch(tag, gain):
                dve.wait_ge(*when(f"{tag}_rs.all"))
                for k in range(KT + 1):
                    if k < KT:
                        v.scalar_tensor_tensor(Y[:, k * S:(k + 1) * S], Y[:, k * S:(k + 1) * S], AF2[:, gain + k:gain + k + 1], RS[:, :], mul, mul).then_inc(*did(f"{tag}_t.{k}"))
                    if k:
                        dve.wait_ge(*when(f"{tag}_t.{k - 1}"))
                        v.tensor_tensor(X[:, (k - 1) * S:k * S], X[:, (k - 1) * S:k * S], Y[:, (k - 1) * S:k * S], add).then_inc(*did(f"{tag}_x.{k - 1}"))

            add_branch("y1", 8)
            dve.wait_ge(*when("h2_rs.all"))
            to_halves("h2", lambda k: X[:, k * S:(k + 1) * S], AF2[:, 16:24], LM[:, 24:32], NORM_T, Hl, Hh, S)
            for a in range(2):
                q0 = Q + 8 + 8 * a
                with led.loop(dve, f"up{a}", 4) as i:
                    for b in range(4):
                        next_tile(i + q0, b)
                        hs = (lambda H: H[:, ds(i * 4 + b, 1), :].rearrange("p o t -> p (o t)"))
                        dve.wait_ge(*when(f"relu{a}.{b}"))
                        v.tensor_copy(hs(HIDh), SQ[b % 2][:, :]).then_inc(*did(f"hid{a}_a.{b}"))
                        dve.wait_ge(*when(f"hid{a}_a.{b}"))
                        v.tensor_tensor(hs(HIDl), SQ[b % 2][:, :], hs(HIDh).bitcast(f32), sub).then_inc(*did(f"hid{a}_b.{b}"))
                if a:
                    dve.wait_ge(*when("hid1_b.3"))
                    zero_squares("y2")
                with led.loop(dve, f"down{a}", 4) as i:
                    for b in range(4):
                        next_tile(i + q0 + 4, b)
                        if b % 2 and a == 1:
                            dve.wait_ge(w_used, 4 * q0 + 4 * i + 16 + b + 1 + PRIME)
                            y = Y[:, ds((i * 2 + b // 2) * S, S)]
                            v.tensor_tensor(y, y, bank(b - 1), add).then_inc(taken, 2)
            add_branch("y2", 24)

    @block.tensor
    def _(pe):
        led.engine = "tensor"
        mm = nc.tensor.matmul

        def tile(q, b, H, L, ready=None, n=S, even=None):
            pe.wait_ge(w_low, 4 * q + b + 1 + PRIME)
            start, stop = even in (None, True), even in (None, False)
            if start:
                pe.wait_ge(taken, 4 * q + b - 3 + PRIME)
            out = bank(b if even is None else b & 2, n)
            for k in range(KT):
                if ready:
                    pe.wait_ge(*when(f"{ready}.{k}"))
                kk = k if even in (None, True) else k + KT
                mm(out, WH[b % 2][:, k, :], H[:, kk, :], start=start and k == 0, stop=False)
                mm(out, WH[b % 2][:, k, :], L[:, kk, :], start=False, stop=False)
                last = mm(out, WL[b % 2][:, k, :], H[:, kk, :], start=False, stop=stop and k == KT - 1)
            return last

        def mod_sum(q):
            pe.wait_ge(mod_used, 8 * q + 24 + PRIME)
            pe.wait_ge(mod_taken, q + 2)
            for n in range(8):
                last = mm(bank(4)[:, n:n + 1], ACC[:, n * P:(n + 1) * P], ONES[:, 0:1], start=True, stop=True)
            last.then_inc(mod_summed, 1)

        def body(q, b, ready, **more):
            if b == 3:
                mod_sum(q)
            tile(q, b, Hh, Hl, ready if b == 0 else None, **more).then_inc(w_used, 1)

        def sums(tag, b, n):
            for k in range(KT):
                pe.wait_ge(*when(f"{tag}_sq.{k}"))
                mm(bank(b, n), ONES, SQ[k % 2][:, 0:n], start=k == 0, stop=k == KT - 1).then_inc(*did(f"{tag}_ss.{k}"))

        def open_squares(tag):
            pe.wait_ge(*when(f"{tag}_zero.1"))
            mm(bank(5), ONES, SQ[1][:, :], start=True, stop=False).then_inc(*did(f"{tag}_open.all"))

        def add_squares(tag, b, slot, loop=None):
            pe.wait_ge(*when(f"{tag}_tile.{b}", back=loop))
            mm(bank(5), ONES, SQ[slot][:, :], start=False, stop=False).then_inc(*did(f"{tag}_part.{b}"))

        def last_squares(tag, b):
            pe.wait_ge(*when(f"{tag}_tile.{b}"))
            mm(bank(5), ONES, SQ[1][:, :], start=False, stop=True).then_inc(*did(f"{tag}_ss.7"))

        def shift_units(ks):
            for k in ks:
                pe.wait_ge(mod_loaded[2 * k % 4], 16 * (2 * k // 4 + 1))
                for n in range(8):
                    last = mm(bank(7)[:, 2 * n:2 * n + 2], MOD[2 * k % 4][:, n * P:(n + 1) * P], CVEC[:, 0:16].rearrange("p (j k) -> p j k", j=2)[:, :, k],
                              start=k + n == 0, stop=k + n == UNITS + 6)
                last.then_inc(*did(f"shift.{k}"))

        pe.sem_inc(w_used, PRIME)
        pe.wait_ge(*when("in_small.all"))
        pe.wait_ge(*when("in_net.all"))
        mm(bank(0, S, slice(0, 64)), HW12[0:33, 0, :], EMB[:, :], start=True, stop=True).then_inc(*did("hy_hid.0"))
        pe.wait_ge(*when("hy_sin.0"))
        mm(bank(1, S, slice(0, 64)), HW12[:, 1, :], EMB2[:, :], start=True, stop=True).then_inc(*did("hy_hid.1"))
        shift_units(range(0, 4))
        sums("n0", 5, S)
        shift_units(range(4, UNITS))
        sums("nc", 6, CTX)
        pe.wait_ge(mod_used, 2 * UNITS + PRIME)
        for j, acc in enumerate(ACC0):
            for n in range(8):
                last = mm(bank(4)[:, 8 * j + n:8 * j + n + 1], acc[:, n * P:(n + 1) * P], ONES[:, 0:1], start=True, stop=True)
        last.then_inc(mod_summed, 2)

        for b in range(4):
            body(0, b, "n0_lo")
            if b >= 2:
                pe.wait_ge(*when(f"ckv.{b - 2}"))
            for k in range(KT):
                if b == 0:
                    pe.wait_ge(*when(f"nc_lo.{k}"))
                mm(bank(5 + b % 2, CTX), WH[b % 2][:, k, :], Ch[:, k, :], start=k == 0, stop=False)
                mm(bank(5 + b % 2, CTX), WH[b % 2][:, k, :], Cl[:, k, :], start=False, stop=False)
                last = mm(bank(5 + b % 2, CTX), WL[b % 2][:, k, :], Ch[:, k, :], start=False, stop=k == KT - 1)
            last.then_inc(*did(f"ckv_mm.{b}"))
        with led.loop(pe, "ev_in", EV_IN // 4 - 1) as i:
            for b in range(4):
                body(i + 1, b, "n0_lo")

        pe.wait_ge(taken, EV_IN + PRIME)

        def rot(j):
            if R1[j][0] != "ck":
                pe.wait_ge(*when(f"hn_zn.{j}"))
                if j >= 4:
                    pe.wait_ge(*when(f"hn_rb.{j - 2}"))
                mm(bank(2 + j % 2), ROPE0, ZN[j % 2][:, :], start=True, stop=True).then_inc(*did(f"hn_rot.{j}"))

        for batch in BATCHES:
            for j in batch:
                n = CTX if R1[j][0] == "ck" else S
                pe.wait_ge(*when(f"hn_sq.{j}"))
                if j >= 2:
                    pe.wait_ge(*when(f"hn_ln.{j - 2}"))
                mm(bank(j % 2, n), ONES, SQ[j % 2][:, 0:n], start=True, stop=True).then_inc(*did(f"hn_ss.{j}"))
            for j in batch:
                rot(j)
        for j in range(6):
            if j >= 3:
                pe.wait_ge(*when(f"vt.{j - 3}"))
            for m in range(2):
                src = CKV[:, 2 + m, j * P:(j + 1) * P] if j < 2 else z(2 + m)[:, (j - 2) * P:(j - 1) * P]
                last = nc.tensor.transpose(bank(4 + j % 3)[:, m * P:(m + 1) * P], src, IDENT)
            last.then_inc(*did(f"vt_mm.{j}"))

        def transpose_probs(n):
            pe.wait_ge(*when(f"pnorm.{n}"))
            pe.wait_ge(*when(f"pt.{n - 1}" if n else "vt.5"))
            for j in range(6):
                last = nc.tensor.transpose(PS[:, 4 * S + j * P:4 * S + (j + 1) * P], PR[n % 2][:, j * P:(j + 1) * P], IDENT)
            last.then_inc(*did(f"pt_mm.{n}"))

        def head_values(h):
            pe.wait_ge(*when(f"pt.{4 * h + 3}"))
            if h >= 2:
                pe.wait_ge(*when(f"attn_y.{h - 2}"))
            for j in range(6):
                last = mm(bank(6 + h % 2), VT[:, j, (h // 3) * P:(h // 3 + 1) * P], PT[h % 2][:, j, :], start=j == 0, stop=j == 5)
            last.then_inc(*did(f"attn_o.{h}"))

        pe.wait_ge(*when("hn_out.9"))
        for n in range(24):
            h, i = divmod(n, 4)
            if n >= 2:
                pe.wait_ge(*when(f"prob.{n - 2}"))
            at0 = (n % 2) * 2 * S
            q_ = z(4 + h)[:, i * P:(i + 1) * P]
            mm(PS[:, at0:at0 + S], q_, KALL[:, h // 3, 0:S], start=True, stop=True)
            mm(PS[:, at0 + S:at0 + 768], q_, KALL[:, h // 3, S:768], start=True, stop=True).then_inc(*did(f"score.{n}"))
            if n >= 5 and n % 4 == 1:
                head_values((n - 5) // 4)
            if n:
                transpose_probs(n - 1)
        transpose_probs(23)
        head_values(5)
        pe.wait_ge(*when("pool_d.all"))
        pe.wait_ge(*when("pt.23"))
        for m in range(2):
            mm(bank(4 + m), POOLW[:, m * P:(m + 1) * P], z(10 + m), start=True, stop=True).then_inc(*did(f"pool_y.{m}"))
        pe.wait_ge(*when("attn_y.5"))
        with led.loop(pe, "ev_out", EV_OUT // 4) as i:
            for b in range(4):
                body(i + 5, b, "mx1_lo")
        sums("n1", 5, S)
        with led.loop(pe, "od_in", OD_IN // 4) as i:
            for b in range(4):
                body(i + 7, b, "n1_lo")

        pe.wait_ge(taken, T_OD_OUT + PRIME)

        def filters(n, j):
            if j == 0:
                pe.wait_ge(*when(f"in_w3.{n}"))
                pe.wait_ge(*when("hy_zero.1"))
            if j >= 2:
                pe.wait_ge(*when(f"hy_d1.{n}.{j - 2}"))
            elif n:
                pe.wait_ge(*when(f"hk_fly.{n - 1}.7"))
            for d in range(2):
                mm(bank(2 * (j % 2) + d, G), HDN[:, j * P:(j + 1) * P], W3[:, d * G:(d + 1) * G], start=True, stop=True).then_inc(*did(f"hy_filt.{n}.{2 * j + d}"))

        def norm_sums(n):
            pe.wait_ge(*when(f"hy_abs.{n}.3.1"))
            for c in range(3):
                last = mm(bank(0)[:, c:c + 1], ABSA[:, c * P:(c + 1) * P], ONES[:, 0:1], start=True, stop=True)
            last.then_inc(*did(f"hy_norm_mm.{n}"))

        def transform(kind, n, ft):
            if ft:
                pe.wait_ge(*when(f"{kind}_fly.{n}.3"))
            else:
                pe.wait_ge(*when(f"hy_inv_a.{n}" if kind == "hk" else f"hy_zt.{n}.3"))
            for c in range(2):
                for e in range(2):
                    for t in range(2):
                        rhs = (ZT if kind == "hz" else (FSUM, FDIFF)[c])[:, 2 * e + t, :]
                        last = mm(bank(SPEC_BANK[kind] + 2 * c + e, G), FWD[:, e, c, t, ft * P:(ft + 1) * P], rhs, start=t == 0, stop=t == 1)
            last.then_inc(*did(f"{kind}_mm.{n}.{ft}"))

        def to_tokens(n):
            g = STEPS[n][0]
            pe.wait_ge(*when(f"hy_out.{n - 1}.2" if n else "conv3.17"))
            for j in range(4):
                for c in range(3):
                    src = z(3 * g + c).rearrange("p (m e) -> p e m", e=2)[:, j // 2, (j % 2) * P:(j % 2 + 1) * P]
                    last = nc.tensor.transpose(bank(4 + j)[:, c * P:(c + 1) * P], src, IDENT)
                last.then_inc(*did(f"hy_zt_mm.{n}.{j}"))

        def back(n):
            pe.wait_ge(*when(f"hg_s.{n}.1.3"))
            for c in range(3):
                for e in range(2):
                    k = 0
                    for s_ in range(2):
                        for ft in range(2):
                            last = mm(bank(4 + c)[:, e * 256:(e + 1) * 256], GSP[:, ft, 2 * s_ + e, c * P:(c + 1) * P], INV[:, e, s_, ft, :], start=k == 0, stop=k == 3)
                            k += 1
                last.then_inc(*did(f"hy_inv.{n}.{c}"))

        def over_channels():
            pe.wait_ge(*when("in_fn.all"))
            for j in range(4):
                for k in range(2):
                    last = mm(bank(j), z(FN_T + 1 + k)[:, j * P:(j + 1) * P], CSC[:, k, :], start=k == 0, stop=k == 1)
                last.then_inc(*did(f"fn_a.{j}"))

        def over_time():
            pe.wait_ge(*when("fn_ab.3"))
            for m in range(2):
                for j in range(4):
                    mm(bank(m), AB[j][:, m * P:(m + 1) * P], CTT[:, j, :], start=j == 0, stop=False)
                    last = mm(bank(m), AB[j][:, 2 * P + m * P:2 * P + (m + 1) * P], NST[:, j, :], start=False, stop=j == 3)
                last.then_inc(*did(f"fn_b.{m}"))

        def fourier_weights():
            for m in range(2):
                for k in range(2):
                    pe.wait_ge(*when(f"fn_u2.{k}"))
                    last = mm(bank(2 + m), FNW[:, k, m * P:(m + 1) * P], U2[:, k, :], start=k == 0, stop=k == 1)
                last.then_inc(*did(f"fn_y.{m}"))

        for j in range(4):
            filters(0, j)
        norm_sums(0)
        for ft in range(2):
            transform("hk", 0, ft)
        for n in range(len(STEPS)):
            more = n + 1 < len(STEPS)
            to_tokens(n)
            if more:
                filters(n + 1, 0)
                filters(n + 1, 1)
            transform("hz", n, 0)
            if more:
                filters(n + 1, 2)
                filters(n + 1, 3)
                norm_sums(n + 1)
            else:
                over_channels()
            transform("hz", n, 1)
            if more:
                transform("hk", n + 1, 0)
                transform("hk", n + 1, 1)
            else:
                over_time()
            back(n)
        fourier_weights()

        with led.loop(pe, "od_out", OD_OUT // 4) as i:
            for b in range(4):
                body(i + 14, b, "mx2_lo")
        sums("nf", 5, S)

        with led.loop(pe, "layers", LAYERS) as lay:
            Q = lay * (PER_LAYER // 4) + T_LAYERS // 4
            sums("h1", 5, S)
            with led.loop(pe, "mx_in", 5) as i:
                for b in range(4):
                    tile(i + Q, b, Hh, Hl, "h1_lo" if b == 0 else None).then_inc(w_used, 1)
            for b in range(2):
                tile(Q + 5, b, Hh, Hl).then_inc(w_used, 1)
            pe.wait_ge(w_used, 4 * Q + 22 + PRIME)
            pe.sem_inc(w_used, 2)
            pe.wait_ge(taken, 4 * Q + 24 + PRIME)

            for m in range(2):
                mm(bank(m), HALVES, z(19 + m), start=True, stop=True).then_inc(*did(f"gm_mean.{m}"))
            for c in range(2):
                mm(bank(5 + c), (DUPK, DUPV)[c], z(8), start=True, stop=True).then_inc(*did(f"cmp_dup.{c}"))
            pe.wait_ge(*when("in_cw1.all"))
            for c in range(2):
                pe.wait_ge(*when(f"cmp_in.{2 * c + 1}"))
                for j in range(16):
                    done = mm(bank((7, 4)[c], 31), CW1[:, (16 * c + j) * P:(16 * c + j + 1) * P], TP[:, c, j, :], start=j == 0, stop=j == 15)
                done.then_inc(*did(f"cmp_h.{c}"))
                if c == 0:
                    for m in range(2):
                        pe.wait_ge(*when(f"gm_sq.{m}"))
                        mm(bank(2 + m), HALVES, SQ[m][:, :], start=True, stop=True).then_inc(*did(f"gm_var.{m}"))
            for c in range(4):
                if c >= 2:
                    pe.wait_ge(*when(f"rp_b.{c - 1}"))
                    mm(bank(5), DUPK, z(7 + c), start=True, stop=True).then_inc(*did(f"rp_dup.{c}"))
                mm(bank(ROT_BANKS[c]), ROT2 if c < 2 else DUPR, z((6 if c < 2 else 7) + c), start=True, stop=True).then_inc(*did(f"rp_rot.{c}"))
            pe.wait_ge(*when("cmp_act.1"))
            mm(bank(2, 31), par("w2k", 0, P), HC[:, 0, 0:31], start=True, stop=True).then_inc(*did("cmp_kv.0"))
            mm(bank(3, P, slice(0, 31)), HC[:, 1, 0:31], par("w2v", 0, P), start=True, stop=True).then_inc(*did("cmp_kv.1"))
            for j in range(4):
                last = nc.tensor.transpose(bank(4)[:, j * P:(j + 1) * P], z(21)[:, j * P:(j + 1) * P], IDENT)
            last.then_inc(*did("gate_t.all"))
            mm(bank(7), par("gate_w", 0, P, slice(0, 16)), z(21)[0:16, :], start=True, stop=True).then_inc(*did("gla_pre.all"))
            pe.wait_ge(*when("rp_b.3"))
            for c in range(2):
                for j in range(4):
                    last = mm(bank(5 + c)[:, j * P:(j + 1) * P], z(9 + c)[:, j * P:(j + 1) * P], DUPV, start=True, stop=True)
                last.then_inc(*did(f"v_tok_mm.{c}"))
            pe.wait_ge(*when("gm_n.1"))
            for j in range(4):
                for m in range(2):
                    last = nc.tensor.transpose(bank(j // 2)[:, (j % 2 * 2 + m) * P:(j % 2 * 2 + m + 1) * P], MO[:, m, j * P:(j + 1) * P], IDENT)
                last.then_inc(*did(f"gm_vt_mm.{j}"))
            pe.wait_ge(*when("gm_vt.1"))
            for m in range(2):
                for gpar in range(2):
                    rows = slice(64 * gpar, 64 * gpar + 64)
                    for j in range(4):
                        g = 2 * m + gpar
                        last = mm(bank(2 + m)[rows, j * P:(j + 1) * P], GMV[:, j, 64 * g:64 * g + 64], par("ws", P * g, P), start=True, stop=True)
                last.then_inc(*did(f"gm_mm.{m}"))

            def weigh(n):
                h, i, br = ITEMS[n]
                pe.wait_ge(*when(f"pnorm2.{n}"))
                if n >= 2:
                    pe.wait_ge(*when(f"p2t.{n - 2}"))
                if br == 2:
                    nc.tensor.transpose(bank(3 + n % 2, P, slice(0, 31)), P2[n % 4][:, 0:31], IDENT).then_inc(*did(f"p2t_mm.{n}"))
                else:
                    for j in range(i + 1):
                        last = nc.tensor.transpose(bank(3 + n % 2)[:, j * P:(j + 1) * P], P2[n % 4][:, j * P:(j + 1) * P], IDENT)
                    last.then_inc(*did(f"p2t_mm.{n}"))

            def values(n):
                h, i, br = ITEMS[n]
                pe.wait_ge(*when(f"p2t.{n}"))
                if h >= 2 and i == 0 and br == 0:
                    pe.wait_ge(*when(f"nsa_o.{h - 2}"))
                out = bank(5 + h % 2)[:, i * P:(i + 1) * P]
                if br == 2:
                    last = mm(out, VC[0:31, :], PT2[n % 2][0:31, 0, :], start=False, stop=True)
                else:
                    for j in range(i + 1):
                        last = mm(out, [VS_, VW_][br][:, j, :], PT2[n % 2][:, j, :], start=br == 0 and j == 0, stop=False)
                last.then_inc(*did(f"p2v.{n}"))

            pe.wait_ge(*when("rp.3"))
            pe.wait_ge(*when("v_tok.1"))
            pe.wait_ge(*when("cmp_v.all"))
            for n, (h, i, br) in enumerate(ITEMS):
                if n >= 4:
                    pe.wait_ge(*when(f"prob2.{n - 4}"))
                elif n == 2:
                    pe.wait_ge(*when("gm_t.3"))
                elif n == 3:
                    pe.wait_ge(*when("gla_x.all"))
                if br == 2:
                    mm(bank(SCORE_BANKS[n % 4], 31), z(6 + h // 2)[:, i * P:(i + 1) * P], KC[:, h % 2, 0:31], start=True, stop=True).then_inc(*did(f"score2.{n}"))
                else:
                    mm(bank(SCORE_BANKS[n % 4], WIDTH[n]), QR[:, h // 2, i * P:(i + 1) * P], K2[br][:, h % 2, 0:WIDTH[n]], start=True, stop=True).then_inc(*did(f"score2.{n}"))
                if n >= 2:
                    weigh(n - 2)
                if n >= 3:
                    values(n - 3)
            for n in range(len(ITEMS), len(ITEMS) + 3):
                if n - 2 < len(ITEMS):
                    weigh(n - 2)
                values(n - 3)

            pe.wait_ge(*when("prob2.47"))
            pe.wait_ge(*when("gla_m.1"))
            for h in range(4):
                rows = slice(32 * h, 32 * h + 32)
                for c in range(8):
                    last = mm(bank(h)[0:64, 64 * c:64 * c + 64], GE[1][rows, 64 * c:64 * c + 64], GE[0][rows, 64 * c:64 * c + 64], start=True, stop=True)
                last.then_inc(*did(f"gla_att_mm.{h}"))
            pe.wait_ge(*when("gla_m.2"))
            for c in range(8):
                pe.wait_ge(*when(f"gla_tok.{c - 2}" if c >= 2 else "nsa_o.3"))
                pe.sem_inc(passed, 1)
                for m, src in enumerate((GE[2][:, :], z(13), z(14))):
                    last = nc.tensor.transpose(bank(4 + c % 2)[0:64, m * P:(m + 1) * P], src[:, 64 * c:64 * c + 64], IDENT)
                last.then_inc(*did(f"gla_tok_mm.{c}"))

            def group_sum(g, m):
                pe.wait_ge(*when(f"gr_sq.{2 * g + m}"))
                mm(bank(GROUP_BANK[g]), ONES, SQ[m][:, :], start=m == 0, stop=m == 1).then_inc(*did(f"gr_ss.{2 * g + m}"))

            pe.wait_ge(*when("gla_att.3"))
            for c in range(7):
                pe.wait_ge(*when("gla_tok.7" if c < 2 else f"gla_st.{c - 2}.3"))
                mm(bank(4 + c % 2, 256), GV[:, c, 0:P], GV[:, c, P:3 * P], start=True, stop=True).then_inc(*did(f"gla_kv.{c}"))
                if c:
                    group_sum((0, 3, 1)[(c - 1) // 2], (c - 1) % 2)
            pe.wait_ge(*when("gla_m.3"))
            pe.wait_ge(*when("gla_st.6.3"))
            pe.sem_inc(passed, 1)
            for m in range(2):
                for c in range(8):
                    cols_ = slice(64 * c, 64 * c + 64)
                    for hp in range(2):
                        h = 2 * m + hp
                        last = mm(bank(6 + m)[64 * hp:64 * hp + 64, cols_], GV[:, c, P + 64 * h:P + 64 * h + 64], GA[:, h, cols_], start=True, stop=c == 0)
                    if c:
                        last = mm(bank(6 + m)[:, cols_], GS[:, c, P * m:P * m + P], GE[3][:, cols_], start=False, stop=True)
                last.then_inc(*did(f"gla_o.{m}"))
            for m in range(2):
                pe.wait_ge(*when(f"gla_sq.{m}"))
                mm(bank(3 + m), HALVES, SQ[m][:, :], start=True, stop=True).then_inc(*did(f"gla_ss.{m}"))
            group_sum(2, 0)
            group_sum(2, 1)
            open_squares("y1")
            with led.loop(pe, "mx_out", 2) as i:
                for b in range(4):
                    tile(i + Q + 6, b, Hh, Hl, "mx3_lo" if b == 0 else None).then_inc(w_used, 1)
                    add_squares("y1", (b - 1) % 4, (b - 1) % 2, None if b else "mx_out")
            last_squares("y1", 3)
            sums("h2", 6, S)
            for a in range(2):
                q0 = Q + 8 + 8 * a
                with led.loop(pe, f"up{a}", 4) as i:
                    for b in range(4):
                        tile(i + q0, b, Hh, Hl, "h2_lo" if b == 0 else None).then_inc(w_used, 1)
                if a:
                    open_squares("y2")
                with led.loop(pe, f"down{a}", 4) as i:
                    for b in range(4):
                        if b == 0:
                            pe.wait_ge(*when(f"hid{a}_b.3"))
                        tile(i + q0 + 4, b, HIDh, HIDl, even=b % 2 == 0).then_inc(w_used, 1)
                        if a and b == 0:
                            add_squares("y2", 1, 1, "down1")
                        if a and b == 2:
                            add_squares("y2", 0, 0)
            last_squares("y2", 1)

    ctx.close()
    return led.learnt()


def tables():
    f = np.float32
    t = np.arange(S)
    eye = np.eye(P, dtype=f)
    half = np.kron(np.eye(2), np.ones((64, 64))).astype(f)
    out = {"eye": np.concatenate([eye, np.ones((P, P), f), half], 1)}
    inv = np.power(f(10000.0), -np.arange(32, dtype=f) / f(32)).astype(f)
    place = np.stack([(t // 64).astype(f), (t % 64).astype(f)])
    d = np.arange(P)
    ang = (place[d // 64] * inv[d % 32][:, None]).astype(f)
    rope = np.zeros((P, P), f)
    for i in range(P):
        rope[i + 32 if i % 64 < 32 else i - 32, i] = -1.0 if i % 64 < 32 else 1.0
    cnt = np.zeros((P, 2, S), f)
    for g, w in enumerate((2, 4, 8, 16)):
        n = np.clip(t + w // 2, 0, S) - np.clip(t - w // 2, 0, S)
        cnt[64 * (g % 2):64 * (g % 2) + 64, g // 2] = (1.0 / n).astype(f)
    out["tab_attn"] = [np.cos(ang).astype(f), np.sin(ang).astype(f), cnt.reshape(P, -1), rope]
    w = 2 * np.pi * (np.arange(256) + 0.5) / 1024
    fwd = np.zeros((P, 2, 2, 2, 256))
    inv_ = np.zeros((P, 2, 2, 2, 256))
    for e in range(2):
        for c, fn in enumerate((np.cos, np.sin)):
            m = fn(np.outer(2 * np.arange(256) + e, w))
            fwd[:, e, c] = m.reshape(2, P, 256).transpose(1, 0, 2)
            inv_[:, e, c] = m.T.reshape(2, P, 256).transpose(1, 0, 2)
    out["dft"] = np.concatenate([fwd.reshape(P, -1), inv_.reshape(P, -1)], 1).astype(f)
    order = np.concatenate([t[0::2], t[1::2]])
    lin = np.linspace(0.0, 1.0, S, dtype=f)
    ww = (f(2.0 * np.pi) * t.astype(f) / f(S))[:, None]
    ff = np.linspace(1e-4, 15, 16, dtype=f)[None, :]
    emb = np.concatenate([lin[:, None], np.cos(ff * ww), -np.sin(ff * ww)], 1).astype(f)
    out["emb"] = np.ascontiguousarray(emb[order].T)
    deltas = np.abs(np.linspace(np.log(1e-2) / 1.5, np.log(1e-2) / 0.3, 768, dtype=f))
    out["delta"] = np.tile(deltas[None], (P, 1)).astype(f)
    out["time"] = -lin[order].reshape(4, P).T
    c = 2 * np.pi * np.outer(np.arange(256), np.arange(256)) / 256
    s = 1 / np.sqrt(S * 256.0)
    m = np.concatenate([np.cos(c) * s, np.sin(c) * s], 1)
    out["dft_ch"] = np.ascontiguousarray(m.reshape(2, P, 512).transpose(1, 0, 2).reshape(P, -1)).astype(f)
    c = 2 * np.pi * (np.outer(t, t) % S) / S
    out["dft_cos"], out["dft_sin"] = np.cos(c).astype(f), (-np.sin(c)).astype(f)
    q, k = np.arange(P)[:, None], np.arange(P)[None, :]
    bias = np.where(k <= q, 0, -1e30)
    cmpb = np.zeros((P, 4, 32))
    for i in range(4):
        cmpb[:, i] = np.where(16 * np.arange(32)[None] + 31 <= 128 * i + q, 0, -1e30)
    rot = np.zeros((64, 64))
    for i in range(8):
        rot[i + 8, i], rot[i, i + 8] = -1.0, 1.0
    dupk, dupr = np.zeros((P, P)), np.zeros((P, P))
    dupk[:64] = np.concatenate([np.eye(64)] * 2, 1)
    dupr[:64] = np.concatenate([rot] * 2, 1)
    rot2 = np.kron(np.eye(2), rot)
    dupv = np.roll(dupk, 64, 0)
    tril = np.where(q <= k, 1.0, 0.0)
    scan = np.tile(np.where(t % 64 == 0, 0.0, 1.0)[None], (P, 1))
    out["tab_layers"] = np.concatenate([bias, cmpb.reshape(P, -1), dupk, dupr, rot2, dupv, tril, scan], 1).astype(f)
    out["gla_mask"] = np.tile((np.arange(64)[:, None] <= np.arange(64)[None, :]).astype(np.int32), (1, 8))
    invf = np.power(f(500000.0), -np.arange(0, 16, 2, dtype=f) / f(16)).astype(f)
    r = np.arange(P) % 64
    out["inv_freq"] = np.where(r < 16, invf[r % 8], 0).astype(f)[:, None]
    valid = np.ones((P, 4), f)
    valid[:31, 0] = 0
    out["row_valid"] = valid
    return out


def columns(v):
    return np.ascontiguousarray(v.reshape(-1, P).T)


def tiles(w):
    n = w.shape[1] // P
    return w.reshape(KT, P, n, P).transpose(2, 1, 0, 3).reshape(n, P, D)


def pairs(t):
    return t.reshape(-1, 2, P, D).transpose(0, 2, 1, 3).reshape(-1, P, 2 * D)


def units(w):
    n = w.shape[1] // D
    return w.reshape(KT, P, n, D).transpose(2, 0, 1, 3).reshape(-1, D)


def padded(a, rows=P):
    out = np.zeros((rows,) + a.shape[1:], a.dtype)
    out[:a.shape[0]] = a
    return out


def layout(x, c, ctx, c_ctx, w_mod, b_mod, norm_g, ev_w_in, ev_w_out, pool_w, pool_scale, q_norm_g, k_norm_g, od_w_in,
           od_w_out, hy_conv_w, hy_conv_b, hy_w1, hy_b1, hy_w2, hy_b2, hy_w3, hy_freq, hy_skip, fn_w, final_g, c_2,
           positions_2, w_in_2, conv_w_2, cmp_pos_2, cmp_w1_2, cmp_w2_2, gla_gate_w2_2, gla_gate_b_2, gmlp_ws_2,
           gmlp_b_2, grp_gain_2, w_o_2, norm_g_2, w_mod_2, b_mod_2, w_up_2, w_down_2):
    f = np.float32
    tab = tables()
    A = {"xT": np.ascontiguousarray(x[0].T), "ctxT": np.ascontiguousarray(ctx[0].T), "pos": np.ascontiguousarray(positions_2)}
    cols = {
        "c": columns(c[0]), "c_ctx": columns(c_ctx), "cond": np.concatenate([columns(c[0])] * 4 + [columns(c_2[0])] * 12, 1),
        "b_mod": np.concatenate([columns(b_mod[0, 2 * D:]), columns(b_mod[1]), columns(b_mod_2[0]), columns(b_mod_2[1])], 1),
        "b_mod0": columns(b_mod[0, :2 * D]), "g0": columns(norm_g[0]), "g1": columns(norm_g[1]), "q_g": columns(q_norm_g[0]),
        "k_g": columns(k_norm_g[0]), "pool_scale": columns(pool_scale[0]), "conv_w": np.concatenate([columns(hy_conv_w[0, j]) for j in range(3)], 1),
        "conv_b": columns(hy_conv_b[0]), "hy_b1": padded(hy_b1[0][:, None]), "hy_b2": padded(hy_b2[0][:, None]),
        "freq": padded(hy_freq[0][:, None]), "skip": np.concatenate([columns(hy_skip[0, o]) for o in range(2)], 1),
        "final_g": columns(final_g), "g2": np.concatenate([columns(norm_g_2[l].reshape(-1)) for l in range(LAYERS)], 1),
        "time": tab["time"], "inv_freq": tab["inv_freq"], "row_valid": tab["row_valid"]}
    A["cols"] = np.concatenate([cols[n] for n in COLS], 1).astype(f, copy=False)
    for n in ("eye", "dft", "emb", "delta", "dft_ch", "dft_cos", "dft_sin", "tab_layers", "gla_mask"):
        A[n] = tab[n]
    poolw = np.zeros((P, 2 * P), f)
    for g in range(4):
        poolw[64 * (g % 2):64 * (g % 2) + 64, P * (g // 2) + 64 * (g % 2):P * (g // 2) + 64 * (g % 2) + 64] = pool_w[0, g]
    A["tab_attn"] = np.concatenate(tab["tab_attn"] + [poolw], 1)
    A["hy_w1"], A["hy_w2"], A["fn_w"] = hy_w1[0], hy_w2[0], fn_w[0]
    A["hy_w3"] = np.ascontiguousarray(hy_w3[0].reshape(64, 2, 2, 2, 384).transpose(0, 1, 3, 2, 4).reshape(64, -1))
    A["wmod0"] = units(w_mod[0][:, :2 * D])
    A["wmod"] = np.concatenate([units(w_mod[0][:, 2 * D:]), units(w_mod[1])] + [units(w_mod_2[l]) for l in range(LAYERS)])
    w = ev_w_in[0]
    ev = np.concatenate([w[:, 1280:1536], w[:, 1536:1792], w[:, 512:1280], w[:, 0:256], w[:, 256:512], w[:, 1792:2560]], 1)
    w = od_w_in[0]
    od = np.concatenate([w[:, :2304], w[:, 3072:3328], w[:, 2304:3072], w[:, 3328:]], 1)
    stream = [pairs(tiles(m)) for m in (ev, ev_w_out[0], od, od_w_out[0])]
    blobs = []
    for l in range(LAYERS):
        w = w_in_2[l]
        misc = np.zeros((D, P), f)
        misc[:, 0:16], misc[:, 32:44] = w[:, 2188:2204], w[:, 1408:1420]
        parts = [w[:, 0:768], w[:, 768:1024], w[:, 1024:1408], w[:, 1420:1548], w[:, 1548:1676], w[:, 1676:1932],
                 w[:, 1932:2188], w[:, 2204:2460], w[:, 2460:2716], misc]
        stream.append(pairs(tiles(np.concatenate(parts, 1))))
        cols2 = {
            "ws": gmlp_ws_2[l].transpose(2, 0, 1).reshape(P, 4 * P),
            "w2k": np.concatenate([cmp_w2_2[l, 0]] * 2, 1), "w2v": np.concatenate([cmp_w2_2[l, 1]] * 2, 1),
            "gate_w": padded(gla_gate_w2_2[l]),
            "gm_b": np.concatenate([np.repeat(gmlp_b_2[l, 2 * m:2 * m + 2], 64, 0) for m in range(2)], 1),
            "conv": np.concatenate([columns(conv_w_2[l, j]) for j in range(3)], 1),
            "pos": cmp_pos_2[l].reshape(2, 2, 16, 64).transpose(1, 3, 0, 2).reshape(P, 32), "gate_b": columns(gla_gate_b_2[l]),
            "gain": columns(grp_gain_2[l])}
        blob = np.zeros((1, P, 2 * D), f)
        blob[0, :, :N_BLOB] = np.concatenate([cols2[n] for n in BLOB], 1)
        stream += [blob, pairs(tiles(w_o_2[l]))]
        up = tiles(w_up_2[l])
        down = w_down_2[l].reshape(2, 16, P, KT, P).transpose(0, 3, 2, 1, 4).reshape(2, KT, P, 2 * D)
        for a in range(2):
            stream += [pairs(up[16 * a:16 * a + 16]), down[a]]
    stream.append(np.zeros((1, P, 2 * D), f))
    A["wt"] = np.concatenate(stream).reshape(-1, 2 * D)
    A["cmp_w1"] = np.concatenate([cmp_w1_2[l].reshape(2, 2, 16, 64, P).transpose(1, 3, 0, 2, 4).reshape(P, 32 * P) for l in range(LAYERS)])
    return A


def kernel(**inputs):
    import concourse.bacc as bacc
    from concourse.bass_utils import run_bass_kernel_spmd

    arrays = {k: np.ascontiguousarray(a) for k, a in layout(**{k: np.asarray(a) for k, a in inputs.items()}).items()}

    def build(known=None):
        nc = bacc.Bacc("TRN2", target_bir_lowering=False, num_devices=1)
        A = {k: nc.dram_tensor(f"in_{k}", a.shape, mybir.dt.from_np(a.dtype), kind="ExternalInput").ap() for k, a in arrays.items()}
        A["out"] = nc.dram_tensor("out_x", (D, S), mybir.dt.float32, kind="ExternalOutput").ap()
        return nc, program(nc, A, known)

    nc, _ = build(build()[1])
    r = run_bass_kernel_spmd(nc, [{f"in_{k}": a for k, a in arrays.items()}], core_ids=[0])
    return np.ascontiguousarray(r.results[0]["out_x"].T)[None]
```
